# Optimizing a Trainium2 kernel written in Bass

```python
import math
import jax, jax.numpy as jnp
from jax import lax
import numpy as np

D_MODEL = 1024
BATCH = 1
SEQ = 512
DEPTH = 2

N_A_LAYERS = DEPTH // 2
N_B_LAYERS = DEPTH - N_A_LAYERS
EPS = 1e-6

A_HEADS = 8
A_DK = 128
A_DV = 256
A_QK_W = A_HEADS * A_DK
A_V_W = A_HEADS * A_DV
A_CONV_CH = 2 * A_QK_W + A_V_W
A_IN_W = A_CONV_CH + A_V_W + 2 * A_HEADS
CONV_W = 4
CHUNK = 64

B_Q_HEADS = 32
B_KV_HEADS = 4
B_GROUP = B_Q_HEADS // B_KV_HEADS
B_HD = 64
B_W = B_Q_HEADS * B_HD
B_KV_W = B_KV_HEADS * B_HD
WINDOW = 128
BLOCK = 128

N_BUCKETS = 32
MAX_DIST = 128


def rms_norm(x, g):
    xf = x.astype(jnp.float32)
    y = xf * lax.rsqrt(jnp.mean(xf * xf, axis=-1, keepdims=True) + EPS)
    return (y * g.astype(jnp.float32)).astype(x.dtype)

def l2_norm(x):
    xf = x.astype(jnp.float32)
    return xf * lax.rsqrt(jnp.sum(xf * xf, axis=-1, keepdims=True) + EPS)

def causal_depthwise_conv(x, w):
    c = x.shape[-1]
    return lax.conv_general_dilated(
        x, w[:, None, :].astype(x.dtype), window_strides=(1,),
        padding=[(CONV_W - 1, 0)], dimension_numbers=("NWC", "WIO", "NWC"),
        feature_group_count=c)

def chunk_gated_delta_rule(q, k, v, g, beta):
    B, T, H, _ = q.shape
    N = T // CHUNK

    def chunks(t):
        return t.reshape(B, N, CHUNK, H, -1).transpose(0, 1, 3, 2, 4)

    q, k, v = chunks(q), chunks(k), chunks(v)
    g = jnp.cumsum(g.reshape(B, N, CHUNK, H).transpose(0, 1, 3, 2), axis=-1)
    beta = beta.reshape(B, N, CHUNK, H).transpose(0, 1, 3, 2)

    tri = jnp.tril(jnp.ones((CHUNK, CHUNK), dtype=bool))
    strict = jnp.tril(jnp.ones((CHUNK, CHUNK), dtype=bool), -1)
    decay = jnp.exp(jnp.where(tri, g[..., :, None] - g[..., None, :], -jnp.inf))

    kk = jnp.einsum("bnhcd,bnhsd->bnhcs", k, k)
    lower = jnp.where(strict, beta[..., :, None] * kk * decay, 0.0)
    rhs = jnp.concatenate([v * beta[..., None], k * (beta * jnp.exp(g))[..., None]], axis=-1)
    sol = lax.linalg.triangular_solve(lower, rhs, left_side=True, lower=True, unit_diagonal=True)
    u, w = sol[..., :A_DV], sol[..., A_DV:]

    qk = jnp.einsum("bnhcd,bnhsd->bnhcs", q, k) * decay
    q_dec = q * jnp.exp(g)[..., None]
    k_dec = k * jnp.exp(g[..., -1:] - g)[..., None]
    g_last = jnp.exp(g[..., -1])

    def step(S, inp):
        qk_i, qd_i, kd_i, u_i, w_i, gl_i = inp
        v_new = u_i - jnp.einsum("bhck,bhkv->bhcv", w_i, S)
        o = jnp.einsum("bhck,bhkv->bhcv", qd_i, S) + jnp.einsum("bhcs,bhsv->bhcv", qk_i, v_new)
        S = S * gl_i[..., None, None] + jnp.einsum("bhck,bhcv->bhkv", kd_i, v_new)
        return S, o

    xs = tuple(t.swapaxes(0, 1) for t in (qk, q_dec, k_dec, u, w, g_last))
    S0 = jnp.zeros((B, H, A_DK, A_DV), jnp.float32)
    _, o = lax.scan(step, S0, xs)
    return o.transpose(1, 0, 3, 2, 4).reshape(B, T, H, A_DV)

def gated_deltanet_mixer(h, w_in, conv_w, a_log, dt_bias, o_gain, w_out):
    B, T, _ = h.shape
    proj = h @ w_in
    qkv, z, ab = jnp.split(proj, [A_CONV_CH, A_CONV_CH + A_V_W], axis=-1)
    qkv = jax.nn.silu(causal_depthwise_conv(qkv, conv_w))
    q, k, v = jnp.split(qkv, [A_QK_W, 2 * A_QK_W], axis=-1)
    q = l2_norm(q.reshape(B, T, A_HEADS, A_DK)) * (A_DK ** -0.5)
    k = l2_norm(k.reshape(B, T, A_HEADS, A_DK))
    v = v.reshape(B, T, A_HEADS, A_DV).astype(jnp.float32)
    b_logit, a_logit = jnp.split(ab.astype(jnp.float32), 2, axis=-1)
    beta = jax.nn.sigmoid(b_logit)
    g = -jnp.exp(a_log.astype(jnp.float32)) * jax.nn.softplus(a_logit + dt_bias.astype(jnp.float32))
    o = chunk_gated_delta_rule(q, k, v, g, beta)
    o = rms_norm(o, o_gain) * jax.nn.silu(z.reshape(B, T, A_HEADS, A_DV).astype(jnp.float32))
    return o.reshape(B, T, A_V_W).astype(h.dtype) @ w_out

def shared_kv(x, kv_norm, w_kv, k_gain):
    B, T, _ = x.shape
    nb = T // BLOCK
    kv = rms_norm(x, kv_norm) @ w_kv
    k, v = jnp.split(kv, 2, axis=-1)
    k = rms_norm(k.reshape(B, T, B_KV_HEADS, B_HD), k_gain)
    v = v.reshape(B, T, B_KV_HEADS, B_HD)

    def band(t):
        tb = t.reshape(B, nb, BLOCK, B_KV_HEADS, B_HD)
        prev = jnp.concatenate([jnp.zeros_like(tb[:, :1]), tb[:, :-1]], axis=1)
        return jnp.concatenate([prev, tb], axis=2)

    return band(k), band(v)

def t5_causal_bucket(dist):
    n = np.maximum(dist, 0)
    max_exact = N_BUCKETS // 2
    large = max_exact + (np.log(np.maximum(n, 1) / max_exact) / np.log(MAX_DIST / max_exact)
                         * (N_BUCKETS - max_exact)).astype(np.int64)
    large = np.minimum(large, N_BUCKETS - 1)
    return np.where(n < max_exact, n, large).astype(np.int32)

def band_bias_and_mask(rel_bias, seq):
    nb = seq // BLOCK
    qi = np.arange(BLOCK)[:, None]
    s = np.arange(2 * BLOCK)[None, :]
    dist = qi + BLOCK - s
    in_window = (dist >= 0) & (dist < WINDOW)
    bias = rel_bias.astype(jnp.float32)[jnp.asarray(t5_causal_bucket(dist))]
    bias = bias.transpose(2, 0, 1).reshape(B_KV_HEADS, B_GROUP, BLOCK, 2 * BLOCK)
    key_pos = np.arange(nb)[:, None] * BLOCK - BLOCK + s
    mask = in_window[None] & (key_pos >= 0)[:, None, :]
    return bias, jnp.asarray(mask)

def swa_sink_mixer(h, w_in, q_gain, sinks, w_out, k_band, v_band, bias, mask):
    B, T, _ = h.shape
    nb = T // BLOCK
    q, z = jnp.split(h @ w_in, 2, axis=-1)
    q = rms_norm(q.reshape(B, T, B_Q_HEADS, B_HD), q_gain) * (B_HD ** -0.5)
    q = q.reshape(B, nb, BLOCK, B_KV_HEADS, B_GROUP, B_HD)
    logits = jnp.einsum("bnqkgd,bnskd->bnkgqs", q, k_band).astype(jnp.float32) + bias
    logits = jnp.where(mask[None, :, None, None], logits, -jnp.inf)
    sink = sinks.astype(jnp.float32).reshape(B_KV_HEADS, B_GROUP)[..., None, None]
    m = jnp.maximum(jnp.max(logits, axis=-1, keepdims=True), sink)
    p = jnp.exp(logits - m)
    probs = p / (jnp.sum(p, axis=-1, keepdims=True) + jnp.exp(sink - m))
    o = jnp.einsum("bnkgqs,bnskd->bnqkgd", probs.astype(v_band.dtype), v_band)
    o = o.reshape(B, T, B_W) * jax.nn.silu(z)
    return o @ w_out

def first_inputs(seed: int = 0) -> dict:
    key = jax.random.key(seed)
    ks = jax.random.split(key, 20)
    f = jnp.float32
    D = D_MODEL
    nA, nB = N_A_LAYERS, N_B_LAYERS

    def nrm(k, shape, scale):
        return jax.random.normal(k, shape, f) * scale

    dt = jnp.exp(jax.random.uniform(ks[5], (nA, A_HEADS), f, math.log(1e-3), math.log(1e-1)))
    return {
        "x": nrm(ks[0], (BATCH, SEQ, D), 1.0),
        "a_norm": 1.0 + nrm(ks[1], (nA, D), 0.02),
        "a_w_in": nrm(ks[2], (nA, D, A_IN_W), D ** -0.5),
        "a_conv": nrm(ks[3], (nA, CONV_W, A_CONV_CH), CONV_W ** -0.5),
        "a_A_log": jnp.log(jax.random.uniform(ks[4], (nA, A_HEADS), f, 1.0, 16.0)),
        "a_dt_bias": dt + jnp.log(-jnp.expm1(-dt)),
        "a_o_gain": 1.0 + nrm(ks[6], (nA, A_DV), 0.02),
        "a_w_out": nrm(ks[7], (nA, A_V_W, D), A_V_W ** -0.5),
        "kv_norm": 1.0 + nrm(ks[8], (D,), 0.02),
        "w_kv": nrm(ks[9], (D, 2 * B_KV_W), D ** -0.5),
        "k_gain": 1.0 + nrm(ks[10], (B_HD,), 0.02),
        "rel_bias": nrm(ks[11], (N_BUCKETS, B_Q_HEADS), 0.5),
        "b_norm": 1.0 + nrm(ks[12], (nB, D), 0.02),
        "b_w_in": nrm(ks[13], (nB, D, 2 * B_W), D ** -0.5),
        "b_q_gain": 1.0 + nrm(ks[14], (nB, B_HD), 0.02),
        "b_sinks": nrm(ks[15], (nB, B_Q_HEADS), 0.5),
        "b_w_out": nrm(ks[16], (nB, B_W, D), B_W ** -0.5),
    }

def first_block(x, a_norm, a_w_in, a_conv, a_A_log, a_dt_bias, a_o_gain, a_w_out,
              kv_norm, w_kv, k_gain, rel_bias,
              b_norm, b_w_in, b_q_gain, b_sinks, b_w_out):
    bias, mask = band_bias_and_mask(rel_bias, x.shape[1])
    k_band = v_band = None
    for layer in range(DEPTH):
        if layer < N_A_LAYERS:
            i = layer
            x = x + gated_deltanet_mixer(rms_norm(x, a_norm[i]), a_w_in[i], a_conv[i], a_A_log[i],
                                         a_dt_bias[i], a_o_gain[i], a_w_out[i])
            if layer == N_A_LAYERS - 1:
                k_band, v_band = shared_kv(x, kv_norm, w_kv, k_gain)
        else:
            j = layer - N_A_LAYERS
            x = x + swa_sink_mixer(rms_norm(x, b_norm[j]), b_w_in[j], b_q_gain[j], b_sinks[j],
                                   b_w_out[j], k_band, v_band, bias, mask)
    return x


N_MIXERS = 2
POOL_WINDOWS = (2, 4, 8, 16)
N_POOL_GROUPS = len(POOL_WINDOWS)
POOL_GROUP_DIM = D_MODEL // N_POOL_GROUPS
CONV_KERNEL = 31
D_FF = ((8 * D_MODEL // 3 + 255) // 256) * 256
RMS_EPS = 1e-6
LN_EPS = 1e-5
FFN_RESIDUAL_WEIGHT = 0.5
N_POOL_LAYERS = len(range(0, DEPTH, N_MIXERS))
N_CONV_LAYERS = len(range(1, DEPTH, N_MIXERS))


def rmsnorm(x, g):
    xf = x.astype(jnp.float32)
    y = xf * lax.rsqrt(jnp.mean(xf * xf, axis=-1, keepdims=True) + RMS_EPS)
    return (y * g.astype(jnp.float32)).astype(x.dtype)

def layernorm(x, g, b):
    xf = x.astype(jnp.float32)
    mu = jnp.mean(xf, axis=-1, keepdims=True)
    xc = xf - mu
    var = jnp.mean(xc * xc, axis=-1, keepdims=True)
    y = xc * lax.rsqrt(var + LN_EPS) * g.astype(jnp.float32) + b.astype(jnp.float32)
    return y.astype(x.dtype)

def swiglu_ffn(x, w_in, w_out):
    gate, up = jnp.split(x @ w_in, 2, axis=-1)
    return (jax.nn.silu(gate) * up) @ w_out

def pool_mixer(x, w_pool, b_pool, scale):
    B, S, D = x.shape
    xf = x.astype(jnp.float32)
    c = jnp.concatenate([jnp.zeros((B, 1, D), jnp.float32), jnp.cumsum(xf, axis=1)], axis=1)
    t = jnp.arange(S)
    parts = []
    for g, w in enumerate(POOL_WINDOWS):
        cg = c[..., g * POOL_GROUP_DIM:(g + 1) * POOL_GROUP_DIM]
        lo = jnp.clip(t - w // 2, 0, S)
        hi = jnp.clip(t - w // 2 + w, 0, S)
        cnt = (hi - lo).astype(jnp.float32)
        win_sum = jnp.take(cg, hi, axis=1) - jnp.take(cg, lo, axis=1)
        parts.append(win_sum / cnt[None, :, None])
    pooled = jnp.concatenate(parts, axis=-1) - xf
    pooled = pooled.astype(x.dtype).reshape(B, S, N_POOL_GROUPS, POOL_GROUP_DIM)
    y = jnp.einsum('bsgc,gcd->bsgd', pooled, w_pool).reshape(B, S, D) + b_pool
    return y * scale

def conformer_conv(x, w_pw1, b_pw1, w_dw, b_dw, ln_g, ln_b, w_pw2, b_pw2):
    D = x.shape[-1]
    a, gate = jnp.split(x @ w_pw1 + b_pw1, 2, axis=-1)
    h = a * jax.nn.sigmoid(gate)
    h = lax.conv_general_dilated(
        h, w_dw[:, None, :], window_strides=(1,),
        padding=[(CONV_KERNEL // 2, CONV_KERNEL // 2)],
        dimension_numbers=('NWC', 'WIO', 'NWC'),
        feature_group_count=D) + b_dw
    h = jax.nn.silu(layernorm(h, ln_g, ln_b))
    return h @ w_pw2 + b_pw2

def second_inputs(seed: int = 0) -> dict:
    key = jax.random.key(seed)
    ks = jax.random.split(key, 16)
    D, F, K = D_MODEL, D_FF, CONV_KERNEL
    nrm = lambda k, shape, s: jax.random.normal(k, shape, jnp.float32) * s
    return {
        "x": nrm(ks[0], (BATCH, SEQ, D), 1.0),
        "norm_g": 1.0 + nrm(ks[1], (DEPTH, 3, D), 0.05),
        "ffn_w_in": nrm(ks[2], (DEPTH, 2, D, 2 * F), D ** -0.5),
        "ffn_w_out": nrm(ks[3], (DEPTH, 2, F, D), F ** -0.5),
        "pool_w": nrm(ks[4], (N_POOL_LAYERS, N_POOL_GROUPS, POOL_GROUP_DIM, POOL_GROUP_DIM), POOL_GROUP_DIM ** -0.5),
        "pool_b": nrm(ks[5], (N_POOL_LAYERS, D), 0.02),
        "pool_scale": 1.0 + nrm(ks[6], (N_POOL_LAYERS, D), 0.1),
        "conv_w_pw1": nrm(ks[7], (N_CONV_LAYERS, D, 2 * D), D ** -0.5),
        "conv_b_pw1": nrm(ks[8], (N_CONV_LAYERS, 2 * D), 0.02),
        "conv_w_dw": nrm(ks[9], (N_CONV_LAYERS, K, D), K ** -0.5),
        "conv_b_dw": nrm(ks[10], (N_CONV_LAYERS, D), 0.02),
        "conv_ln_g": 1.0 + nrm(ks[11], (N_CONV_LAYERS, D), 0.05),
        "conv_ln_b": nrm(ks[12], (N_CONV_LAYERS, D), 0.02),
        "conv_w_pw2": nrm(ks[13], (N_CONV_LAYERS, D, D), D ** -0.5),
        "conv_b_pw2": nrm(ks[14], (N_CONV_LAYERS, D), 0.02),
        "final_g": 1.0 + nrm(ks[15], (D,), 0.05),
    }

def second_block(x, norm_g, ffn_w_in, ffn_w_out, pool_w, pool_b, pool_scale,
              conv_w_pw1, conv_b_pw1, conv_w_dw, conv_b_dw, conv_ln_g, conv_ln_b,
              conv_w_pw2, conv_b_pw2, final_g):
    for i in range(DEPTH):
        x = x + FFN_RESIDUAL_WEIGHT * swiglu_ffn(rmsnorm(x, norm_g[i, 0]), ffn_w_in[i, 0], ffn_w_out[i, 0])
        h = rmsnorm(x, norm_g[i, 1])
        j = i // N_MIXERS
        if i % N_MIXERS == 0:
            x = x + pool_mixer(h, pool_w[j], pool_b[j], pool_scale[j])
        else:
            x = x + conformer_conv(h, conv_w_pw1[j], conv_b_pw1[j], conv_w_dw[j], conv_b_dw[j],
                                   conv_ln_g[j], conv_ln_b[j], conv_w_pw2[j], conv_b_pw2[j])
        x = x + FFN_RESIDUAL_WEIGHT * swiglu_ffn(rmsnorm(x, norm_g[i, 2]), ffn_w_in[i, 1], ffn_w_out[i, 1])
    return rmsnorm(x, final_g)


def setup_inputs(seed=0):
    out = dict(first_inputs(seed))
    for name, value in second_inputs(seed + 1).items():
        if name != "x":
            out[name + "_2"] = value
    return out


def reference(
    x, a_norm, a_w_in, a_conv, a_A_log, a_dt_bias, a_o_gain, a_w_out, kv_norm, w_kv, k_gain,
    rel_bias, b_norm, b_w_in, b_q_gain, b_sinks, b_w_out, norm_g_2, ffn_w_in_2, ffn_w_out_2,
    pool_w_2, pool_b_2, pool_scale_2, conv_w_pw1_2, conv_b_pw1_2, conv_w_dw_2, conv_b_dw_2,
    conv_ln_g_2, conv_ln_b_2, conv_w_pw2_2, conv_b_pw2_2, final_g_2,
):
    x = first_block(
        x, a_norm, a_w_in, a_conv, a_A_log, a_dt_bias, a_o_gain, a_w_out, kv_norm, w_kv, k_gain,
        rel_bias, b_norm, b_w_in, b_q_gain, b_sinks, b_w_out,
    )
    return second_block(
        x, norm_g_2, ffn_w_in_2, ffn_w_out_2, pool_w_2, pool_b_2, pool_scale_2, conv_w_pw1_2,
        conv_b_pw1_2, conv_w_dw_2, conv_b_dw_2, conv_ln_g_2, conv_ln_b_2, conv_w_pw2_2,
        conv_b_pw2_2, final_g_2,
    )


_drawn_inputs = setup_inputs


def setup_inputs(seed=0):
    import zlib

    import numpy as np

    out = dict(_drawn_inputs(seed))
    spreads = {}
    factors = {'a_norm': 2.756,
     'a_o_gain': 4.891,
     'kv_norm': 8.0,
     'k_gain': 8.0,
     'b_norm': 8.0,
     'b_q_gain': 8.0,
     'b_sinks': 64.0,
     'pool_b_2': 200.0,
     'conv_b_pw1_2': 200.0,
     'conv_b_dw_2': 200.0,
     'conv_ln_b_2': 200.0,
     'conv_b_pw2_2': 200.0,
     'norm_g_2': 8.0,
     'ffn_w_in_2': 4.272,
     'ffn_w_out_2': 4.262,
     'pool_w_2': 2.956,
     'pool_scale_2': 32.184,
     'conv_w_pw1_2': 35.339,
     'conv_w_dw_2': 35.662,
     'conv_ln_g_2': 64.0,
     'conv_w_pw2_2': 26.998}
    for name, (base, spread) in spreads.items():
        noise = np.random.default_rng([zlib.crc32(name.encode()), seed]).standard_normal(out[name].shape)
        drawn = base * np.exp(spread * noise) if base else spread * noise
        out[name] = __import__('jax').numpy.asarray(drawn.astype(out[name].dtype))
    for name, factor in factors.items():
        out[name] = (out[name] * factor).astype(out[name].dtype)
    return out
```

```python
import math
from contextlib import ExitStack

import numpy as np

import concourse.bass as bass
from concourse import mybir

F32 = mybir.dt.float32
F32R = mybir.dt.float32r
ACT = mybir.ActivationFunctionType
ALU = mybir.AluOpType

P = 128
D = 1024
T = 512
KC = D // P
TC = T // P
A_HEADS, A_DK, A_DV, TAPS = 8, 128, 256, 4
A_QK_W, A_V_W = A_HEADS * A_DK, A_HEADS * A_DV
A_Z0 = 2 * A_QK_W + A_V_W
A_AB0 = A_Z0 + A_V_W
A_PAIRS = A_HEADS // 2
B_HEADS, B_KV, B_HD = 32, 4, 64
B_W, B_KV_W = B_HEADS * B_HD, B_KV * B_HD
WINDOW = 128
BUCKETS, MAX_DIST = 32, 128
FF = 2816
FF_STEPS = FF // 256
DW = 31
DW_PAD = DW // 2
POOL_PAD = 8
LEVELS = 7
TILE = 2048
MASKED = -1e30
EPS, LN_EPS = 1e-6, 1e-5

A_BODY = "IIIIIIOO"
B_BODY = "IIO"
FF_TILES = "II" + "IIO" * (FF_STEPS - 1) + "O"
TILES = A_BODY * A_PAIRS + "II" + B_BODY * 8
T_KV = len(A_BODY) * A_PAIRS
T_B = T_KV + 2
T_FF = [len(TILES)]
TILES += FF_TILES
T_POOL = len(TILES)
TILES += "P"
T_FF.append(len(TILES))
TILES += FF_TILES
T_FF.append(len(TILES))
TILES += FF_TILES
T_PW1 = len(TILES)
TILES += "I" * 8
T_PW2 = len(TILES)
TILES += "O" * 4
T_FF.append(len(TILES))
TILES += FF_TILES
CHUNKS = {"I": 2, "O": 8, "P": 8}

CHUNK_CREDIT, SPLIT_CREDIT, IN_CREDIT, OUT_CREDIT = 1, 2, 4, 8


def chunks_before(t):
    return sum(CHUNKS[k] for k in TILES[:t])


def in_before(t):
    return 2 * TILES[:t].count("I")


def out_before(t):
    return 8 * (TILES[:t].count("O") + TILES[:t].count("P"))


def pairs_before(t):
    return TILES[:t].count("O")


def at(f, t, i, period):
    return f(t) if i is None else i * (f(t + period) - f(t)) + f(t)


class Marks:

    def __init__(self, sem, names):
        self.sem, self.names = sem, names
        self.n, self.pos, self.next = len(names), {x: k for k, x in enumerate(names)}, 0
        assert len(self.pos) == self.n

    def begin(self, eng):
        eng.sem_inc(self.sem, self.n)

    def done(self, name, ins):
        assert self.names[self.next % self.n] == name, (name, self.names[self.next % self.n])
        self.next += 1
        ins.then_inc(self.sem, 1)

    def wait(self, eng, name, i=0):
        eng.wait_ge(self.sem, i * self.n + (self.n + self.pos[name] + 1))

    def before(self, eng, name, i=0):
        eng.wait_ge(self.sem, i * self.n + (self.pos[name] + 1))


def bucket_runs():
    n = np.arange(WINDOW)
    exact = BUCKETS // 2
    large = exact + (np.log(np.maximum(n, 1) / exact) / np.log(MAX_DIST / exact)
                     * (BUCKETS - exact)).astype(np.int64)
    b = np.where(n < exact, n, np.minimum(large, BUCKETS - 1))
    return [(int(v), int(np.argmax(b == v)), int((b == v).sum())) for v in np.unique(b)]


DW_ROWS = DW * KC
PARAMS = {}


def _place():
    PARAMS["a_conv"] = 0
    PARAMS["dw"] = 128
    row = 3 * 128
    for name, n in (("a_norm", 8), ("kv_norm", 8), ("b_norm", 8), ("norm_g", 48), ("pool_b", 8),
                    ("pool_scale", 8), ("pw1_b", 16), ("dw_b", 8), ("ln_g", 8)):
        PARAMS[name] = row
        row += n
    row = 4 * 128
    for name, n in (("ln_b", 8), ("pw2_b", 8), ("final_g", 8), ("o_gain", 2), ("k_gain", 1),
                    ("q_gain", 1)):
        PARAMS[name] = row
        row += n


_place()


def build(nc, x, a_norm, a_w_in, a_conv, a_A_log, a_dt_bias, a_o_gain, a_w_out, kv_norm, w_kv,
          k_gain, rel_bias, b_norm, b_w_in, b_q_gain, b_sinks, b_w_out, norm_g, ffn_w_in,
          ffn_w_out, pool_w, pool_b, pool_scale, pw1_w, pw1_b, dw_w, dw_b, ln_g, ln_b, pw2_w,
          pw2_b, final_g, out):
    ctx = ExitStack()
    with ctx:
        def sb(name, shape, dt=F32, into=ctx):
            return into.enter_context(nc.sbuf_tensor(name, shape, dt))

        def sem(name):
            return ctx.enter_context(nc.semaphore(name))

        xT = sb("xT", [P, KC, T])
        h_hi = sb("h_hi", [P, KC, T], F32R)
        h_lo = sb("h_lo", [P, KC, T], F32R)
        w_raw = sb("w_raw", [P, 2, TILE])
        w_hi = sb("w_hi", [P, 2, TILE], F32R)
        w_lo = sb("w_lo", [P, 2, TILE], F32R)
        a_hi = sb("a_hi", [P, 2, 2, T], F32R)
        a_lo = sb("a_lo", [P, 2, 2, T], F32R)
        cols = sb("cols", [P, 5 * P])
        ident = sb("ident", [P, P])
        ones = sb("ones", [P, P])
        tri = sb("tri", [P, P])
        flip = sb("flip", [P, P])
        causal = sb("causal", [P, P])
        half_ones = sb("half_ones", [P, 2])
        level_mask = sb("level_mask", [P, LEVELS, P])
        eps = sb("eps", [P, 4])
        tok = sb("tok", [P, 16])
        sinks = sb("sinks", [P, B_HEADS])
        a_neg = sb("a_neg", [P, A_HEADS])
        a_log = sb("a_log", [P, A_HEADS])
        a_dt = sb("a_dt", [P, A_HEADS])
        wab_raw = sb("wab_raw", [P, KC, 16])
        wab_hi = sb("wab_hi", [P, KC, 16], F32R)
        wab_lo = sb("wab_lo", [P, KC, 16], F32R)

        NORM_COLS = 7 * T
        with ExitStack() as s:
            n_sq = sb("n_sq", [P, 2, T], into=s)
            n_sum = sb("n_sum", [P, T], into=s)
            n_rb = sb("n_rb", [P, T], into=s)
            n_rstd = sb("n_rstd", [P, T], into=s)
            n_h = sb("n_h", [P, 2, T], into=s)
        with ExitStack() as s:
            sb("below_setup", [P, NORM_COLS], into=s)
            param_rows = sb("param_rows", [P, 5, P], into=s)
            x_tok = sb("x_tok", [P, TC, D], into=s)
            rel_in = sb("rel_in", [BUCKETS, B_HEADS], into=s)
            rel_T = sb("rel_T", [B_HEADS, BUCKETS], into=s)
            rel_line = sb("rel_line", [B_HEADS, 3 * P], into=s)
        with ExitStack() as s:
            gate = {k: sb("gate_" + k, [P, TC, A_HEADS], into=s)
                    for k in ("g", "beta", "neg_cum", "beta_exp", "k_decay", "last", "t0", "t1", "t2", "t3", "u")}
            conv_in = sb("conv_in", [P, 2, T + TAPS - 1], into=s)
            conv_out = sb("conv_out", [P, 2, T], into=s)
            qkv = sb("qkv", [P, 8, T], into=s)
            square = sb("square", [P, 4, T], into=s)
            g_wide = sb("g_wide", [P, 2, T], into=s)
            b_wide = sb("b_wide", [P, 2, T], into=s)
            masked = sb("masked", [P, 2, T], into=s)
            decay = sb("decay", [P, 2, T], into=s)
            expg = sb("expg", [P, 2, T], into=s)
            lower_T = sb("lower_T", [P, 2, T], into=s)
            qk_T = sb("qk_T", [P, 2, T], into=s)
            k_dec = sb("k_dec", [P, 2, T], into=s)
            v_beta = sb("v_beta", [P, 2, TC, A_DV], into=s)
            v_new = sb("v_new", [P, 2, A_DV], into=s)
            state = sb("state", [P, 2, A_DV], into=s)
            z_gate = sb("z_gate", [P, 2, T], into=s)
        inv_T, inv, prod, neg_wT, k_bg = g_wide, b_wide, masked, decay, expg
        o_out = v_beta[:].rearrange("p a c v -> p (a c v)").rearrange("p (n t) -> p n t", t=T)
        with ExitStack() as s:
            sb("below_b", [P, NORM_COLS], into=s)
            k_rev = sb("k_rev", [P, B_KV, T], into=s)
            v_rev = sb("v_rev", [P, TC, B_KV, B_HD], into=s)
            k_cur = sb("k_cur", [P, T], into=s)
            v_cur = sb("v_cur", [P, TC, 3 * B_HD], into=s)
            bias_cur = sb("bias_cur", [P, 2, 4, 2 * P], into=s)
            small = {k: sb("row_" + k, [P, 2, 4], into=s) for k in ("sink", "max", "top", "neg", "sinkd", "sinke", "sum", "den", "inv")}
            with ExitStack() as s2:
                kvf = sb("kvf", [P, 4, T], into=s2)
                kv_sq = sb("kv_sq", [P, 2, T], into=s2)
                k_tok = sb("k_tok", [P, TC, B_KV, 2, B_HD], into=s2)
                v_tok = sb("v_tok", [P, TC, B_KV_W], into=s2)
            q_cur = sb("q_cur", [P, 2, T], into=s)
            q_sq = sb("q_sq", [P, 2, T], into=s)
            zb_gate = sb("zb_gate", [P, 2, T], into=s)
            probs = sb("probs", [P, 2, 4, 2 * P], into=s)
            probs_T = sb("probs_T", [P, 2, 2, 4, P], into=s)
        with ExitStack() as s:
            sb("below_c", [P, NORM_COLS], into=s)
            f_gate = sb("f_gate", [P, 2, T], into=s)
            f_hid = sb("f_hid", [P, 2, T], into=s)
            pool_h = sb("pool_h", [P, KC, T + 2 * POOL_PAD], into=s)
            pool_s = sb("pool_s", [P, 2, T + 2 * POOL_PAD], into=s)
            inv_cnt = sb("inv_cnt", [P, 4, T], into=s)
            pool_y = sb("pool_y", [P, 2, T], into=s)
        with ExitStack() as s:
            sb("below_d", [P, NORM_COLS], into=s)
            glu = sb("glu", [P, KC, T + 2 * DW_PAD], into=s)
            glu_s = sb("glu_s", [P, 2, T], into=s)
            dw_y = sb("dw_y", [P, KC, T], into=s)
            ln_mean = sb("ln_mean", [P, T], into=s)
            y_tok = sb("y_tok", [P, TC, D], into=s)
        rel_scratch = nc.dram_tensor("rel_scratch", [B_HEADS, 3 * P], F32, kind="Internal").ap()
        rel_band = bass.AP(tensor=rel_scratch.tensor, offset=0, ap=[[3 * P, B_HEADS], [1, P], [1, 2 * P]])

        ps = ctx.enter_context(nc.psum_tensor("ps", [P, 8, T], F32))

        raw_loaded = [sem("raw_loaded0"), sem("raw_loaded1")]
        hi_done = sem("hi_done")
        lo_done = sem("lo_done")
        chunk_done = sem("chunk_done")
        in_free = sem("in_free")
        out_free = sem("out_free")
        pair_ready = sem("pair_ready")
        a_hi_ready = sem("a_hi_ready")
        conv_pad = sem("conv_pad")
        norm_out = sem("norm_out")
        sq_ready, sum_ready, stat_ready = sem("sq_ready"), sem("sum_ready"), sem("stat_ready")
        root_ready, inv_ready, wide_ready, bcast_ready, rstd_ready = (
            sem("root_ready"), sem("inv_ready"), sem("wide_ready"), sem("bcast_ready"), sem("rstd_ready"))
        hf_ready, h_hi_ready, h_ready = sem("hf_ready"), sem("h_hi_ready"), sem("h_ready")
        x_loaded, rows_clear, rows_loaded, small_loaded = (
            sem("x_loaded"), sem("rows_clear"), sem("rows_loaded"), sem("small_loaded"))
        consts, cols_ready, x_ready = sem("consts"), sem("cols_ready"), sem("x_ready")
        setup_pe, rel_ready, rel_stored = sem("setup_pe"), sem("rel_ready"), sem("rel_stored")
        rel_chain = sem("rel_chain")
        SMALL = 16 * 5
        bias_loaded = [sem("bias_loaded0"), sem("bias_loaded1")]
        out_stored, y_ready, y_pe = sem("out_stored"), sem("y_ready"), sem("y_pe")

        def col(name, k):
            c = PARAMS[name] + k
            return cols[:, c:c + 1]

        def cols256(w, c):
            return w[:, c].rearrange("(k p) n -> p k n", p=P)

        def rows256(w, r):
            return w[r, :].rearrange("(k p) n -> p k n", p=P)

        def load(sp, t, src, i=None, period=0):
            sp.wait_ge(lo_done, at(lambda u: u - 2 + SPLIT_CREDIT + 1, t, i, period))
            n = 1024 if len(src.shape) == 3 and src.shape[1] == 2 else 256
            dst = w_raw[:, t % 2].rearrange("p (k n) -> p k n", n=n)
            sp.dma_start(dst, src).then_inc(raw_loaded[t % 2], 16)

        def round_tile(act, t, i=None, period=0):
            act.wait_ge(raw_loaded[t % 2], at(lambda u: 16 * (u // 2 + 1), t, i, period))
            if t >= 2 or i is not None:
                act.wait_ge(chunk_done, at(lambda u: chunks_before(u - 1) + CHUNK_CREDIT, t, i, period))
            nc.scalar.activation(w_hi[:, t % 2], w_raw[:, t % 2], ACT.Copy).then_inc(hi_done, 1)

        def split_tile(dve, t, i=None, period=0):
            dve.wait_ge(hi_done, at(lambda u: u + 1, t, i, period))
            nc.vector.tensor_tensor(w_lo[:, t % 2], w_raw[:, t % 2], w_hi[:, t % 2].bitcast(F32),
                                    ALU.subtract).then_inc(lo_done, 1)

        def products(dst, terms, arrives=None):
            for k, (wh, wl, xh, xl) in enumerate(terms):
                last = k == len(terms) - 1
                if arrives is not None:
                    arrives[0].wait_ge(h_ready, arrives[1] + k + 1)
                nc.tensor.matmul(dst, wh, xh, start=(k == 0), stop=False)
                nc.tensor.matmul(dst, wh, xl, start=False, stop=False)
                m = nc.tensor.matmul(dst, wl, xh, start=False, stop=last)
            return m

        def pe_tile(pe, t, i=None, period=0, h_from=None, all_free=False):
            kind, slot = TILES[t], t % 2
            pe.wait_ge(lo_done, at(lambda u: u + 1 + SPLIT_CREDIT, t, i, period))
            wh, wl = w_hi[:, slot], w_lo[:, slot]
            if kind == "I":
                bank = 2 * ((in_before(t) // 2) % 2)
                pe.wait_ge(in_free, at(in_before, t, i, period) + (IN_CREDIT if all_free else IN_CREDIT - 2))
                for c in range(2):
                    terms = []
                    for k in range(KC):
                        w = slice(k * 256 + c * P, k * 256 + c * P + P)
                        terms.append((wh[:, w], wl[:, w], h_hi[:, k], h_lo[:, k]))
                    arrives = (pe, h_from) if c == 0 and h_from is not None else None
                    products(ps[:, bank + c], terms, arrives).then_inc(chunk_done, 1)
            else:
                if kind == "O":
                    pe.wait_ge(pair_ready, at(lambda u: pairs_before(u) + 1, t, i, period))
                else:
                    pe.wait_ge(h_ready, h_from + KC)
                buf = pairs_before(t) % 2
                for n in range(8):
                    pe.wait_ge(out_free, at(out_before, t, i, period) + (n - 4 + OUT_CREDIT + 1))
                    terms = []
                    for k in range(2):
                        if kind == "O":
                            w = slice(k * D + n * P, k * D + n * P + P)
                            terms.append((wh[:, w], wl[:, w], a_hi[:, buf, k], a_lo[:, buf, k]))
                        else:
                            g = n // 2
                            w = slice((2 * g + k) * 256 + (n % 2) * P, (2 * g + k) * 256 + (n % 2) * P + P)
                            terms.append((wh[:, w], wl[:, w], h_hi[:, 2 * g + k], h_lo[:, 2 * g + k]))
                    products(ps[:, 4 + n % 4], terms).then_inc(chunk_done, 1)

        def add_chunks(dve, t, ns, i=None, period=0, scale=1.0, bias=None):
            for n in ns:
                dve.wait_ge(chunk_done, at(chunks_before, t, i, period) + (n + 1 + CHUNK_CREDIT))
                src = ps[:, 4 + n % 4]
                if bias is not None:
                    ins = nc.vector.scalar_tensor_tensor(xT[:, n], src, col(bias, n), xT[:, n], ALU.add, ALU.add)
                else:
                    ins = nc.vector.scalar_tensor_tensor(xT[:, n], src, scale, xT[:, n], ALU.mult, ALU.add)
                ins.then_inc(out_free, 1)

        def wait_chunk(eng, t, c, i=None, period=0):
            eng.wait_ge(chunk_done, at(chunks_before, t, i, period) + (c + 1 + CHUNK_CREDIT))

        def out_added(eng, t, n):
            eng.wait_ge(out_free, out_before(t) + n + 1 + OUT_CREDIT)

        def in_all_free(eng, t, i=None, period=0):
            eng.wait_ge(in_free, at(in_before, t, i, period) + IN_CREDIT)

        def out_all_free(eng, t, i=None, period=0):
            eng.wait_ge(out_free, at(out_before, t, i, period) + OUT_CREDIT)

        def act_squares(act, m, ready, src=None):
            for n in range(KC):
                ready(act, n)
                if m or n >= 2:
                    act.wait_ge(sum_ready, 8 * m + n - 1)
                nc.scalar.activation(n_sq[:, n % 2], (xT if src is None else src)[:, n], ACT.Square).then_inc(sq_ready, 1)

        def pool_sums(pool, m):
            for n in range(KC):
                pool.wait_ge(sq_ready, 8 * m + n + 1)
                if n:
                    pool.wait_ge(sum_ready, 8 * m + n)
                elif m:
                    pool.wait_ge(stat_ready, m)
                if n == 0:
                    ins = nc.gpsimd.tensor_copy(n_sum[:], n_sq[:, 0])
                else:
                    ins = nc.gpsimd.tensor_tensor(n_sum[:], n_sum[:], n_sq[:, n % 2], ALU.add)
                ins.then_inc(sum_ready, 1)

        def pe_stat(pe, m, t):
            pe.wait_ge(sum_ready, 8 * m + 8)
            in_all_free(pe, t)
            for c in range(TC):
                ins = nc.tensor.matmul(ps[:, 0, c:c + 1], n_sum[:, c * P:c * P + P], ones[:, 0:1],
                                       start=True, stop=True)
            ins.then_inc(stat_ready, 1)
            pe.wait_ge(wide_ready, m + 1)
            for c in range(TC):
                ins = nc.tensor.matmul(ps[:, 1, c * P:c * P + P], n_rb[:, c * P:c * P + P], ident[:],
                                       start=True, stop=True)
            ins.then_inc(bcast_ready, 1)

        def act_root(act, m, e=0):
            act.wait_ge(stat_ready, m + 1)
            if m:
                act.wait_ge(inv_ready, m)
            nc.scalar.activation(tok[:, 0:4], ps[:, 0, 0:4], ACT.Sqrt, bias=eps[:, e:e + 1],
                                 scale=1.0 / D).then_inc(root_ready, 1)

        def dve_rstd(dve, m):
            dve.wait_ge(root_ready, m + 1)
            if m:
                dve.wait_ge(wide_ready, m)
            nc.vector.reciprocal(tok[:, 4:8], tok[:, 0:4]).then_inc(inv_ready, 1)
            dve.wait_ge(inv_ready, m + 1)
            nc.vector.tensor_copy(n_rb[:].rearrange("p (c q) -> p c q", q=P),
                                  tok[:, 4:8].rearrange("p (c o) -> p c o", o=1).to_broadcast([P, TC, P])
                                  ).then_inc(wide_ready, 1)
            dve.wait_ge(bcast_ready, m + 1)
            nc.vector.tensor_copy(n_rstd[:], ps[:, 1]).then_inc(rstd_ready, 1)

        def dve_h(dve, m, q, gain, prev_tile=None):
            dve.wait_ge(rstd_ready, m + 1)
            if prev_tile is not None:
                wait_chunk(dve, prev_tile, 1)
            for n in range(KC + 1):
                if n < KC:
                    if n >= 2:
                        dve.wait_ge(h_ready, 8 * q + n - 1)
                    nc.vector.scalar_tensor_tensor(n_h[:, n % 2], xT[:, n], col(*gain(n)), n_rstd[:],
                                                   ALU.mult, ALU.mult).then_inc(hf_ready, 1)
                if n >= 1:
                    dve.wait_ge(h_hi_ready, 8 * q + n)
                    nc.vector.tensor_tensor(h_lo[:, n - 1], n_h[:, (n - 1) % 2],
                                            h_hi[:, n - 1].bitcast(F32), ALU.subtract).then_inc(h_ready, 1)

        def act_h(act, q):
            for n in range(KC):
                act.wait_ge(hf_ready, 8 * q + n + 1)
                nc.scalar.activation(h_hi[:, n], n_h[:, n % 2], ACT.Copy).then_inc(h_hi_ready, 1)

        NA = len(A_BODY)
        heads = (0, 1)
        lv = range(1, LEVELS)
        gates_dve = Marks(sem("gates_dve"), ["z", "pos", "u", "um1", "lost", "rinv", "corr", "l2",
                                             "sp", "g", "ncum", "neg", "be"])
        gates_act = Marks(sem("gates_act"), ["beta", "abs", "exp", "ln", "alog", "cum", "kdec", "last"])
        gates_pe = Marks(sem("gates_pe"), ["ab", "cum", "total"])
        a_pe = Marks(sem("a_pe"), [f"gb{a}" for a in heads] + [f"bb{a}" for a in heads]
                     + [f"ss{c}" for c in range(4)] + [f"rb{c}" for c in range(4)]
                     + [f"kk{a}" for a in heads] + [f"qk{a}" for a in heads]
                     + [f"kt{a}" for a in heads] + [f"vt{a}0" for a in heads]
                     + [f"T0{a}" for a in heads]
                     + [x for l in lv for x in
                        ([f"A{l}{a}" for a in heads] + ([f"vt{a}1" for a in heads] if l == 1 else [])
                         + [f"X{l}{a}" for a in heads]
                         + ([f"T{l}{a}" for a in heads] if l < LEVELS - 1 else []))]
                     + [f"nw{a}" for a in heads]
                     + [f"{x}{c}{a}" for c in range(TC) for x in (("vn", "o", "sn") if c < TC - 1 else ("vn", "o"))
                        for a in heads]
                     + [f"os{a}" for a in heads] + [f"or{a}" for a in heads])
        a_act = Marks(sem("a_act"), [f"silu{c}" for c in range(8)] + [f"sq{c}" for c in range(4)] + ["rq", "rk"]
                      + [f"{x}{a}" for x in ("eg", "d") for a in heads]
                      + [f"Tc{l}{a}" for l in range(LEVELS - 1) for a in heads]
                      + [f"nw{a}" for a in heads] + [f"vn{c}{a}" for c in range(TC) for a in heads]
                      + [f"os{a}{d}" for a in heads for d in range(2)] + [f"or{a}" for a in heads])
        a_dve = Marks(sem("a_dve"), [f"gw{a}" for a in heads] + [f"bw{a}" for a in heads]
                      + [f"cv{c}{j}" for c in range(8) for j in range(TAPS)]
                      + ["rinv"] + [f"rw{c}" for c in range(4)] + [f"nrm{c}" for c in range(4)]
                      + [f"msk{a}" for a in heads]
                      + [f"{x}{a}" for a in heads for x in ("db", "lt", "qk", "qd", "u0", "u1")]
                      + [f"{x}{a}" for a in heads for x in ("kb", "kd", "vb0")]
                      + [x for l in lv for x in ([f"P{l}{a}" for a in heads]
                         + ([f"vb1{a}" for a in heads] if l == 1 else []) + [f"U{l}{a}" for a in heads])]
                      + [f"S{c}{a}" for c in range(TC - 1) for a in heads]
                      + ["orinv0", "orw0", "orinv1", "orw1"]
                      + [f"og{a}{d}" for a in heads for d in range(2)]
                      + [f"gt{a}{d}" for a in heads for d in range(2)])

        def pe_gates(pe):
            pe.wait_ge(h_ready, 8)
            pe.wait_ge(small_loaded, SMALL)
            for c in range(TC):
                q = slice(c * P, c * P + P)
                ins = products(ps[:, 7, 16 * c:16 * c + 16],
                               [(h_hi[:, k, q], h_lo[:, k, q], wab_hi[:, k], wab_lo[:, k]) for k in range(KC)])
            gates_pe.done("ab", ins)
            gates_dve.wait(pe, "g")
            g = gate["g"][:].rearrange("p c h -> p (c h)")
            gates_pe.done("cum", nc.tensor.matmul(ps[:, 6, 0:32], tri[:], g, start=True, stop=True))
            gates_pe.done("total", nc.tensor.matmul(ps[:, 6, 32:64], ones[:], g, start=True, stop=True))

        def act_gates(act):
            g = gate
            gates_pe.wait(act, "ab")
            abp = ps[:, 7, 0:64].rearrange("p (c j) -> p c j", j=16)
            gates_act.done("beta", nc.scalar.activation(g["beta"][:], abp[:, :, 0:8], ACT.Sigmoid))
            gates_dve.wait(act, "z")
            gates_act.done("abs", nc.scalar.activation(g["t1"][:], g["t0"][:], ACT.Abs))
            gates_act.wait(act, "abs")
            gates_act.done("exp", nc.scalar.activation(g["t1"][:], g["t1"][:], ACT.Exp, scale=-1.0))
            gates_dve.wait(act, "u")
            gates_act.done("ln", nc.scalar.activation(g["t2"][:], g["u"][:], ACT.Ln))
            act.wait_ge(small_loaded, SMALL)
            gates_act.done("alog", nc.scalar.activation(a_neg[:], a_log[:], ACT.Exp))
            gates_dve.wait(act, "neg")
            cum = ps[:, 6, 0:32].rearrange("p (c h) -> p c h", h=8)
            tot = ps[:, 6, 32:64].rearrange("p (c h) -> p c h", h=8)
            gates_act.done("cum", nc.scalar.activation(g["beta_exp"][:], cum, ACT.Exp))
            gates_act.done("kdec", nc.scalar.activation(g["k_decay"][:], g["t3"][:], ACT.Exp))
            gates_act.done("last", nc.scalar.activation(g["last"][:], tot, ACT.Exp))

        def dve_gates(dve):
            g, v = gate, nc.vector
            gates_act.wait(dve, "beta")
            dve.wait_ge(small_loaded, SMALL)
            abp = ps[:, 7, 0:64].rearrange("p (c j) -> p c j", j=16)

            def wide(t):
                return t[:].rearrange("p (o h) -> p o h", o=1).to_broadcast([P, TC, A_HEADS])

            gates_dve.done("z", v.tensor_tensor(g["t0"][:], abp[:, :, 8:16], wide(a_dt), ALU.add))
            gates_dve.wait(dve, "z")
            gates_dve.done("pos", v.tensor_scalar(g["t3"][:], g["t0"][:], 0.0, None, ALU.max))
            gates_act.wait(dve, "exp")
            gates_dve.done("u", v.tensor_scalar(g["u"][:], g["t1"][:], 1.0, None, ALU.add))
            gates_dve.wait(dve, "u")
            gates_dve.done("um1", v.tensor_scalar(g["t0"][:], g["u"][:], -1.0, None, ALU.add))
            gates_dve.wait(dve, "um1")
            gates_dve.done("lost", v.tensor_tensor(g["t1"][:], g["t1"][:], g["t0"][:], ALU.subtract))
            gates_dve.done("rinv", v.reciprocal(g["k_decay"][:], g["u"][:]))
            gates_dve.wait(dve, "rinv")
            gates_dve.done("corr", v.tensor_tensor(g["t1"][:], g["t1"][:], g["k_decay"][:], ALU.mult))
            gates_dve.wait(dve, "corr")
            gates_act.wait(dve, "ln")
            gates_dve.done("l2", v.tensor_tensor(g["t1"][:], g["t1"][:], g["t2"][:], ALU.add))
            gates_dve.wait(dve, "l2")
            gates_dve.done("sp", v.tensor_tensor(g["t1"][:], g["t1"][:], g["t3"][:], ALU.add))
            gates_dve.wait(dve, "sp")
            gates_act.wait(dve, "alog")
            gates_dve.done("g", v.scalar_tensor_tensor(g["g"][:], g["t1"][:], -1.0, wide(a_neg), ALU.mult, ALU.mult))
            gates_pe.wait(dve, "total")
            cum = ps[:, 6, 0:32].rearrange("p (c h) -> p c h", h=8)
            tot = ps[:, 6, 32:64].rearrange("p (c h) -> p c h", h=8)
            gates_dve.done("ncum", v.tensor_scalar(g["neg_cum"][:], cum, -1.0, None, ALU.mult))
            gates_dve.wait(dve, "ncum")
            gates_dve.done("neg", v.tensor_tensor(g["t3"][:], tot, g["neg_cum"][:], ALU.add))
            gates_act.wait(dve, "cum")
            gates_dve.done("be", v.tensor_tensor(g["beta_exp"][:], g["beta_exp"][:], g["beta"][:], ALU.mult))

        def by_chunk(ap):
            return ap.rearrange("p (c q) -> p c q", q=P)

        def gate_col(name, i, a):
            return gate[name][:, :, bass.ds(i * 2 + a, 1)]

        def pe_a(pe, i):
            for k in range(4):
                pe_tile(pe, k, i, NA)
            mm, tr = nc.tensor.matmul, nc.tensor.transpose
            v = lambda t, a, c: t[:, a, c * P:c * P + P]
            pb = lambda b, c: ps[:, b, c * P:c * P + P]
            in_all_free(pe, 4, i, NA)
            out_all_free(pe, 0, i, NA)
            for a in heads:
                a_dve.wait(pe, f"gw{a}", i)
                for c in range(TC):
                    ins = mm(pb(a, c), v(g_wide, a, c), tri[:], start=True, stop=True)
                a_pe.done(f"gb{a}", ins)
            for a in heads:
                a_dve.wait(pe, f"bw{a}", i)
                for c in range(TC):
                    ins = mm(pb(2 + a, c), v(b_wide, a, c), ident[:], start=True, stop=True)
                a_pe.done(f"bb{a}", ins)
            for c in range(4):
                a_act.wait(pe, f"sq{c}", i)
                for q in range(TC):
                    ins = mm(ps[:, 4, 4 * c + q:4 * c + q + 1], square[:, c, q * P:q * P + P], ones[:, 0:1],
                             start=True, stop=True)
                a_pe.done(f"ss{c}", ins)
            for c in range(4):
                a_dve.wait(pe, f"rw{c}", i)
                for q in range(TC):
                    ins = mm(pb(4 + c, q), square[:, c, q * P:q * P + P], ident[:], start=True, stop=True)
                a_pe.done(f"rb{c}", ins)
            for a in heads:
                a_dve.wait(pe, f"nrm{2 + a}", i)
                a_dve.wait(pe, f"nrm{a}", i)
                for c in range(TC):
                    ins = mm(pb(4 + a, c), v(qkv, 2 + a, c), v(qkv, 2 + a, c), start=True, stop=True)
                a_pe.done(f"kk{a}", ins)
            for a in heads:
                for c in range(TC):
                    ins = mm(pb(6 + a, c), v(qkv, 2 + a, c), v(qkv, a, c), start=True, stop=True)
                a_pe.done(f"qk{a}", ins)
            for a in heads:
                a_act.wait(pe, f"eg{a}", i)
                a_dve.wait(pe, f"msk{a}", i)
                for c in range(TC):
                    ins = tr(pb(a, c), v(qkv, 2 + a, c), ident[:])
                a_pe.done(f"kt{a}", ins)
            for a in heads:
                a_dve.wait(pe, f"db{a}", i)
                a_act.wait(pe, "silu7", i)
                for c in range(TC):
                    ins = tr(pb(2 + a, c), v(qkv, 4 + 2 * a, c), ident[:])
                a_pe.done(f"vt{a}0", ins)
            for l in range(LEVELS):
                if l:
                    for a in heads:
                        a_act.wait(pe, f"Tc{l - 1}{a}", i)
                        a_dve.wait(pe, f"qk{a}" if l == 1 else f"P{l - 1}{a}", i)
                        for c in range(TC):
                            ins = mm(pb(4 + a, c), v(lower_T, a, c), v(inv, a, c), start=True, stop=True)
                        a_pe.done(f"A{l}{a}", ins)
                    if l == 1:
                        for a in heads:
                            a_dve.wait(pe, f"vb0{a}", i)
                            for c in range(TC):
                                ins = tr(pb(2 + a, c), v(qkv, 5 + 2 * a, c), ident[:])
                            a_pe.done(f"vt{a}1", ins)
                    for a in heads:
                        a_dve.wait(pe, f"P{l}{a}", i)
                        for c in range(TC):
                            ins = mm(pb(6 + a, c), v(prod, a, c), v(inv_T, a, c), start=True, stop=True)
                        a_pe.done(f"X{l}{a}", ins)
                if l < LEVELS - 1:
                    for a in heads:
                        a_dve.wait(pe, f"U{l}{a}" if l else f"u1{a}", i)
                        if l == 0:
                            a_dve.wait(pe, f"kd{a}", i)
                        else:
                            a_act.wait(pe, f"Tc{l - 1}{a}", i)
                        for c in range(TC):
                            ins = tr(pb(a, c), v(inv_T, a, c), ident[:])
                        a_pe.done(f"T{l}{a}", ins)
            for a in heads:
                a_dve.wait(pe, f"U{LEVELS - 1}{a}", i)
                a_dve.wait(pe, f"vb1{a}", i)
                for c in range(TC):
                    ins = mm(pb(2 + a, c), v(k_bg, a, c), v(inv_T, a, c), start=True, stop=True)
                a_pe.done(f"nw{a}", ins)
            for c in range(TC):
                for a in heads:
                    b = ps[:, 4 + a, 0:A_DV]
                    if c:
                        a_act.wait(pe, f"vn{c - 1}{a}", i)
                        a_dve.wait(pe, f"S{c - 1}{a}", i)
                        a_act.wait(pe, f"nw{a}", i)
                    ins = mm(b, v(inv_T, a, c), v_beta[:, a, c], start=True, stop=c == 0)
                    if c:
                        ins = mm(b, v(neg_wT, a, c), state[:, a], start=False, stop=True)
                    a_pe.done(f"vn{c}{a}", ins)
                for a in heads:
                    a_act.wait(pe, f"vn{c}{a}", i)
                    if c == 0:
                        a_act.wait(pe, "nw1", i)
                        a_dve.wait(pe, f"qd{a}", i)
                    for d in range(2):
                        b = pb(2 * a + d, c)
                        if c:
                            mm(b, state[:, a, d * P:d * P + P], v(qkv, a, c), start=True, stop=False)
                        ins = mm(b, v_new[:, a, d * P:d * P + P], v(qk_T, a, c), start=c == 0, stop=True)
                    a_pe.done(f"o{c}{a}", ins)
                if c < TC - 1:
                    for a in heads:
                        ins = mm(ps[:, 4 + a, A_DV:2 * A_DV], v(k_dec, a, c), v_new[:, a], start=True, stop=True)
                        a_pe.done(f"sn{c}{a}", ins)
            for a in heads:
                for q in range(TC):
                    for d in range(2):
                        a_act.wait(pe, f"os{a}{d}", i)
                        ins = mm(ps[:, 6, 4 * a + q:4 * a + q + 1], square[:, 2 * a + d, q * P:q * P + P],
                                 ones[:, 0:1], start=d == 0, stop=d == 1)
                a_pe.done(f"os{a}", ins)
            for a in heads:
                a_dve.wait(pe, f"orw{a}", i)
                a_act.wait(pe, "or1", i)
                for q in range(TC):
                    ins = mm(pb(6 + a, q), square[:, 2 * a, q * P:q * P + P], ident[:], start=True, stop=True)
                a_pe.done(f"or{a}", ins)
            a_dve.wait(pe, "og11", i)
            for a in heads:
                pe_tile(pe, 4 + a, i, NA)
            for a in heads:
                pe_tile(pe, 6 + a, i, NA)

        def act_a(act, i):
            fn = nc.scalar.activation
            for k in range(4):
                round_tile(act, k + 1, i, NA)
                for c in (2 * k, 2 * k + 1):
                    wait_chunk(act, k, c % 2, i, NA)
                    if c >= 2:
                        a_dve.wait(act, f"cv{c - 2}{TAPS - 1}", i)
                    else:
                        a_dve.before(act, f"cv{c + 6}{TAPS - 1}", i)
                    fn(conv_in[:, c % 2, TAPS - 1:], ps[:, c % 4], ACT.Copy).then_inc(in_free, 1)
                    if c:
                        a_dve.wait(act, f"cv{c - 1}{TAPS - 1}", i)
                        a_act.done(f"silu{c - 1}", fn(qkv[:, c - 1], conv_out[:, (c - 1) % 2], ACT.Silu))
            a_dve.wait(act, f"cv7{TAPS - 1}", i)
            a_act.done("silu7", fn(qkv[:, 7], conv_out[:, 1], ACT.Silu))
            for c in range(4):
                a_act.wait(act, f"silu{c}", i)
                a_act.done(f"sq{c}", fn(square[:, c], qkv[:, c], ACT.Square))
            a_pe.wait(act, "ss3", i)
            a_act.done("rq", fn(tok[:, 0:8], ps[:, 4, 0:8], ACT.Sqrt, bias=eps[:, 1:2], scale=float(A_DK)))
            a_act.done("rk", fn(tok[:, 8:16], ps[:, 4, 8:16], ACT.Sqrt, bias=eps[:, 0:1]))
            for a in heads:
                a_pe.wait(act, f"gb{a}", i)
                a_act.done(f"eg{a}", fn(expg[:, a], ps[:, a], ACT.Exp))
            for a in heads:
                a_dve.wait(act, f"msk{a}", i)
                for c in range(TC):
                    ins = fn(decay[:, a, c * P:c * P + P], masked[:, a, c * P:c * P + P], ACT.Exp,
                             bias=gate["neg_cum"][:, c, bass.ds(i * 2 + a, 1)])
                a_act.done(f"d{a}", ins)
            for l in range(LEVELS - 1):
                for a in heads:
                    a_pe.wait(act, f"T{l}{a}", i)
                    a_act.done(f"Tc{l}{a}", fn(inv[:, a], ps[:, a], ACT.Copy))
            for a in heads:
                a_pe.wait(act, f"nw{a}", i)
                a_dve.wait(act, f"qk{a}", i)
                a_act.done(f"nw{a}", fn(neg_wT[:, a], ps[:, 2 + a], ACT.Copy, scale=-1.0))
            for c in range(TC):
                for a in heads:
                    a_pe.wait(act, f"vn{c}{a}", i)
                    if c:
                        a_pe.wait(act, f"sn{c - 1}{a}", i)
                    a_act.done(f"vn{c}{a}", fn(v_new[:, a], ps[:, 4 + a, 0:A_DV], ACT.Copy))
            for a in heads:
                a_pe.wait(act, f"o{TC - 1}{a}", i)
                for d in range(2):
                    a_act.done(f"os{a}{d}", fn(square[:, 2 * a + d], ps[:, 2 * a + d], ACT.Square))
            a_pe.wait(act, "os1", i)
            for a in heads:
                a_act.done(f"or{a}", fn(tok[:, 4 * a:4 * a + 4], ps[:, 6, 4 * a:4 * a + 4], ACT.Sqrt,
                                        bias=eps[:, 0:1], scale=1.0 / A_DV))
            for a in heads:
                round_tile(act, 5 + a, i, NA)
                for d in range(2):
                    wait_chunk(act, 4 + a, d, i, NA)
                    if a:
                        pair_wait(act, 6, i, NA)
                    fn(z_gate[:, d], ps[:, 2 * a + d], ACT.Silu).then_inc(in_free, 1)
                for d in range(2):
                    a_dve.wait(act, f"gt{a}{d}", i)
                    fn(a_hi[:, a, d], z_gate[:, d], ACT.Copy).then_inc(a_hi_ready, 1)
            round_tile(act, 7, i, NA)
            round_tile(act, 8, i, NA)

        def pair_wait(eng, t, i=None, period=0):
            eng.wait_ge(pair_ready, at(lambda u: pairs_before(u) + 1, t, i, period))

        def dve_pair(dve, t, src, i=None, period=0):
            buf = pairs_before(t) % 2
            for d in range(2):
                dve.wait_ge(a_hi_ready, at(lambda u: 2 * pairs_before(u), t, i, period) + (d + 1))
                ins = nc.vector.tensor_tensor(a_lo[:, buf, d], src[:, d], a_hi[:, buf, d].bitcast(F32), ALU.subtract)
            ins.then_inc(pair_ready, 1)

        def dve_a(dve, i):
            v = nc.vector
            a_pe.before(dve, "o31", i)
            for name, wide in (("g", g_wide), ("beta", b_wide)):
                for a in heads:
                    a_dve.done(f"{name[0]}w{a}", v.tensor_copy(
                        by_chunk(wide[:, a]), gate_col(name, i, a).to_broadcast([P, TC, P])))
            for k in range(4):
                split_tile(dve, k + 1, i, NA)
                for c in (2 * k, 2 * k + 1):
                    dve.wait_ge(in_free, at(in_before, k, i, NA) + (c % 2 + 1 + IN_CREDIT))
                    if c >= 2:
                        a_act.wait(dve, f"silu{c - 2}", i)
                    else:
                        a_act.before(dve, f"silu{c + 6}", i)
                    w = (0, 8)[c in (2, 3)] + c % 2 if c < 4 else 16 + c - 4
                    step = 2 if c < 4 else 4
                    for j in range(TAPS):
                        src = conv_in[:, c % 2, j:j + T]
                        tap = cols[:, bass.ds(i * step + (PARAMS["a_conv"] + j * 32 + w), 1)]
                        dst = conv_out[:, c % 2]
                        if j == 0:
                            ins = v.tensor_scalar(dst, src, tap, None, ALU.mult)
                        else:
                            a_dve.wait(dve, f"cv{c}{j - 1}", i)
                            ins = v.scalar_tensor_tensor(dst, src, tap, dst, ALU.mult, ALU.add)
                        a_dve.done(f"cv{c}{j}", ins)
            a_act.wait(dve, "rk", i)
            a_act.wait(dve, "rq", i)
            a_dve.done("rinv", v.reciprocal(tok[:, 0:16], tok[:, 0:16]))
            a_dve.wait(dve, "rinv", i)
            for c in range(4):
                a_dve.done(f"rw{c}", v.tensor_copy(by_chunk(square[:, c]),
                           tok[:, 4 * c:4 * c + 4].rearrange("p (c o) -> p c o", o=1).to_broadcast([P, TC, P])))
            for c in range(4):
                a_pe.wait(dve, f"rb{c}", i)
                a_dve.done(f"nrm{c}", v.tensor_tensor(qkv[:, c], qkv[:, c], ps[:, 4 + c], ALU.mult))
            mask4 = causal[:].rearrange("p (o q) -> p o q", o=1).to_broadcast([P, TC, P])
            lvl4 = lambda l: level_mask[:, l:l + 1, :].to_broadcast([P, TC, P])
            ident4 = ident[:].rearrange("p (o q) -> p o q", o=1).to_broadcast([P, TC, P])
            for a in heads:
                a_act.wait(dve, f"eg{a}", i)
                a_dve.done(f"msk{a}", v.tensor_tensor(by_chunk(masked[:, a]), by_chunk(ps[:, a]), mask4, ALU.add))
            for a in heads:
                a_act.wait(dve, f"d{a}", i)
                a_dve.done(f"db{a}", v.tensor_tensor(lower_T[:, a], decay[:, a], ps[:, 2 + a], ALU.mult))
                a_dve.wait(dve, f"db{a}", i)
                a_pe.wait(dve, f"kk{a}", i)
                a_dve.done(f"lt{a}", v.tensor_tensor(lower_T[:, a], lower_T[:, a], ps[:, 4 + a], ALU.mult))
                a_pe.wait(dve, f"qk{a}", i)
                a_dve.done(f"qk{a}", v.tensor_tensor(qk_T[:, a], decay[:, a], ps[:, 6 + a], ALU.mult))
                a_dve.done(f"qd{a}", v.tensor_tensor(qkv[:, a], qkv[:, a], expg[:, a], ALU.mult))
                a_dve.wait(dve, f"lt{a}", i)
                a_dve.done(f"u0{a}", v.tensor_tensor(by_chunk(inv_T[:, a]), by_chunk(lower_T[:, a]), lvl4(0), ALU.mult))
                a_dve.wait(dve, f"u0{a}", i)
                a_dve.done(f"u1{a}", v.tensor_tensor(by_chunk(inv_T[:, a]), ident4, by_chunk(inv_T[:, a]), ALU.subtract))
            for a in heads:
                wide = lambda name, n: gate_col(name, i, a).to_broadcast([P, TC, n])
                a_pe.wait(dve, f"kt{a}", i)
                a_dve.wait(dve, f"qd{a}", i)
                a_dve.done(f"kb{a}", v.tensor_tensor(by_chunk(k_bg[:, a]), by_chunk(ps[:, a]), wide("beta_exp", P), ALU.mult))
                a_dve.done(f"kd{a}", v.tensor_tensor(by_chunk(k_dec[:, a]), by_chunk(ps[:, a]), wide("k_decay", P), ALU.mult))
                a_pe.wait(dve, f"vt{a}0", i)
                a_dve.done(f"vb0{a}", v.tensor_tensor(v_beta[:, a, :, 0:P], by_chunk(ps[:, 2 + a]), wide("beta", P), ALU.mult))
            for l in lv:
                for a in heads:
                    a_pe.wait(dve, f"A{l}{a}", i)
                    a_dve.done(f"P{l}{a}", v.tensor_tensor(by_chunk(prod[:, a]), by_chunk(ps[:, 4 + a]), lvl4(l), ALU.mult))
                if l == 1:
                    for a in heads:
                        a_pe.wait(dve, f"vt{a}1", i)
                        a_dve.done(f"vb1{a}", v.tensor_tensor(v_beta[:, a, :, P:], by_chunk(ps[:, 2 + a]),
                                   gate_col("beta", i, a).to_broadcast([P, TC, P]), ALU.mult))
                for a in heads:
                    a_pe.wait(dve, f"X{l}{a}", i)
                    a_dve.done(f"U{l}{a}", v.tensor_tensor(inv_T[:, a], inv_T[:, a], ps[:, 6 + a], ALU.subtract))
            for c in range(TC - 1):
                for a in heads:
                    a_pe.wait(dve, f"sn{c}{a}", i)
                    if c == 0:
                        ins = v.tensor_copy(state[:, a], ps[:, 4 + a, A_DV:])
                    else:
                        last = gate["last"][:, c, bass.ds(i * 2 + a, 1)]
                        ins = v.scalar_tensor_tensor(state[:, a], state[:, a], last, ps[:, 4 + a, A_DV:], ALU.mult, ALU.add)
                    a_dve.done(f"S{c}{a}", ins)
            for a in heads:
                a_act.wait(dve, f"or{a}", i)
                s = slice(4 * a, 4 * a + 4)
                a_dve.done(f"orinv{a}", v.reciprocal(tok[:, s], tok[:, s]))
                a_dve.wait(dve, f"orinv{a}", i)
                a_dve.done(f"orw{a}", v.tensor_copy(by_chunk(square[:, 2 * a]),
                           tok[:, s].rearrange("p (c o) -> p c o", o=1).to_broadcast([P, TC, P])))
            for a in heads:
                a_pe.wait(dve, f"or{a}", i)
                cp = v.tensor_copy(square[:, 2 * a + 1], ps[:, 6 + a])
                cp.then_inc(norm_out, 1)
                dve.wait_ge(norm_out, i * 2 + (a + 1))
                for d in range(2):
                    a_dve.done(f"og{a}{d}", v.scalar_tensor_tensor(
                        o_out[:, 2 * a + d], ps[:, 2 * a + d], col("o_gain", d), square[:, 2 * a + 1], ALU.mult, ALU.mult))
            for a in heads:
                split_tile(dve, 5 + a, i, NA)
                for d in range(2):
                    dve.wait_ge(in_free, at(in_before, 4 + a, i, NA) + (d + 1 + IN_CREDIT))
                    a_dve.wait(dve, f"og{a}{d}", i)
                    ins = v.tensor_tensor(z_gate[:, d], z_gate[:, d], o_out[:, 2 * a + d], ALU.mult)
                    a_dve.done(f"gt{a}{d}", ins)
                dve_pair(dve, 6 + a, z_gate, i, NA)
            add_chunks(dve, 6, range(0, 4), i, NA)
            split_tile(dve, 7, i, NA)
            add_chunks(dve, 6, range(4, 8), i, NA)
            add_chunks(dve, 7, range(0, 4), i, NA)
            split_tile(dve, 8, i, NA)
            add_chunks(dve, 7, range(4, 8), i, NA)


        NB = 2 * len(B_BODY)
        kv_pe = Marks(sem("kv_pe"), ["ss", "rb0", "rb1", "kt", "vt", "kr0", "kr1", "kr2", "kr3", "vr"])
        kv_act = Marks(sem("kv_act"), ["sq0", "sq1", "root", "vt", "kr0", "kr1", "kr2", "kr3"])
        kv_dve = Marks(sem("kv_dve"), ["pad0", "pad1", "rinv", "rw0", "rw1", "n0", "n1", "kt0", "kt1", "vr"])
        blocks = range(TC)
        b_pe = Marks(sem("b_pe"), [f"{x}{pp}" for pp in range(2) for x in
                     ("ss", "rb0", "rb1", "S0", "S1", "pt0", "S2", "pv0", "pt1", "S3", "pv1", "pt2", "pv2",
                      "pt3", "pv3")])
        b_act = Marks(sem("b_act"), [f"{x}{pp}" for pp in range(2) for x in
                      (["sq0", "c0", "sq1", "c1"] + (["kc", "vc"] if pp == 0 else []) + ["root"]
                       + ["ex0", "se0", "ex1", "se1", "pc0", "ex2", "se2", "pc1", "ex3", "se3", "pc2", "pc3"])
                      if not x.startswith("c")])
        b_dve = Marks(sem("b_dve"), [f"{x}{pp}" for pp in range(2) for x in
                      ["rinv", "rw0", "rw1", "nq0", "nq1"]
                      + [y for step in ("T0", "T1", "N0", "T2", "N1", "D1", "T3", "N2", "D2", "N3", "D3")
                         for y in {"T": [f"sk{step[1]}", f"add{step[1]}", f"top{step[1]}", f"neg{step[1]}", f"sd{step[1]}"],
                                   "N": [f"dn{step[1]}", f"ri{step[1]}", f"pn{step[1]}"],
                                   "D": [f"pd{step[1]}"]}[step[0]]]
                      + ["gt0", "gt1"]])

        def pe_kv(pe):
            mm, tr = nc.tensor.matmul, nc.tensor.transpose
            pe_tile(pe, T_KV, h_from=8)
            pe_tile(pe, T_KV + 1)
            out_all_free(pe, T_KV)
            for c in range(2):
                kv_act.wait(pe, f"sq{c}")
                for q in blocks:
                    o = 2 * (4 * c + q)
                    ins = mm(ps[:, 4, o:o + 2], kv_sq[:, c, q * P:q * P + P], half_ones[:], start=True, stop=True)
            kv_pe.done("ss", ins)
            for c in range(2):
                kv_dve.wait(pe, f"rw{c}")
                for q in blocks:
                    ins = mm(ps[:, 4 + c, q * P:q * P + P], kv_sq[:, c, q * P:q * P + P], ident[:], start=True, stop=True)
                kv_pe.done(f"rb{c}", ins)
            in_all_free(pe, T_B)
            for name, first, bank in (("kt", 0, 6), ("vt", 2, 0)):
                if first == 0:
                    kv_dve.wait(pe, "n1")
                for q in blocks:
                    for c in range(2):
                        o = ((q % 2) * 2 + c) * P
                        ins = tr(ps[:, bank + q // 2, o:o + P], kvf[:, first + c, q * P:q * P + P], ident[:])
                kv_pe.done(name, ins)
            kv_dve.wait(pe, "kt1")
            for j in range(B_KV):
                for q in blocks:
                    ins = mm(ps[:, 2 + j, (3 - q) * P:(4 - q) * P],
                             k_tok[:, q, j].rearrange("p u d -> p (u d)"), flip[:], start=True, stop=True)
                kv_pe.done(f"kr{j}", ins)
            kv_act.wait(pe, "vt")
            for q in blocks:
                o = (q % 2) * 256
                ins = mm(ps[:, 6 + q // 2, o:o + 256], flip[:], v_tok[:, q], start=True, stop=True)
            kv_pe.done("vr", ins)

        def act_kv(act):
            fn = nc.scalar.activation
            round_tile(act, T_KV + 1)
            for c in range(4):
                wait_chunk(act, T_KV + c // 2, c % 2)
                fn(kvf[:, c], ps[:, c], ACT.Copy).then_inc(in_free, 1)
                if c < 2:
                    act.wait_ge(in_free, in_before(T_KV) + c + 1 + IN_CREDIT)
                    kv_act.done(f"sq{c}", fn(kv_sq[:, c], kvf[:, c], ACT.Square))
            kv_pe.wait(act, "ss")
            kv_act.done("root", fn(tok[:, 0:16], ps[:, 4, 0:16], ACT.Sqrt, bias=eps[:, 0:1], scale=1.0 / B_HD))
            kv_pe.wait(act, "vt")
            kv_act.done("vt", fn(v_tok[:].rearrange("p q c -> p (q c)"),
                                 ps[:, 0:2].rearrange("p k t -> p (k t)"), ACT.Copy))
            for j in range(B_KV):
                kv_pe.wait(act, f"kr{j}")
                kv_act.done(f"kr{j}", fn(k_rev[:, j], ps[:, 2 + j], ACT.Copy))
            round_tile(act, T_B)

        def dve_kv(dve):
            v = nc.vector
            kv_dve.done("pad0", v.memset(v_cur[:, :, 0:B_HD], 0.0))
            kv_dve.done("pad1", v.memset(v_cur[:, :, 2 * B_HD:], 0.0))
            split_tile(dve, T_KV + 1)
            kv_act.wait(dve, "root")
            kv_dve.done("rinv", v.reciprocal(tok[:, 0:16], tok[:, 0:16]))
            kv_dve.wait(dve, "rinv")
            for c in range(2):
                kv_dve.done(f"rw{c}", v.tensor_copy(
                    kv_sq[:, c].rearrange("p (n d) -> p n d", d=B_HD),
                    tok[:, 8 * c:8 * c + 8].rearrange("p (n o) -> p n o", o=1).to_broadcast([P, 8, B_HD])))
            for c in range(2):
                kv_pe.wait(dve, f"rb{c}")
                kv_dve.done(f"n{c}", v.scalar_tensor_tensor(kvf[:, c], kvf[:, c], col("k_gain", 0), ps[:, 4 + c],
                                                            ALU.mult, ALU.mult))
            kv_pe.wait(dve, "kt")
            for u in range(2):
                kv_dve.done(f"kt{u}", v.tensor_copy(
                    k_tok[:, :, :, u, :].rearrange("p q j d -> p (q j) d"),
                    ps[:, 6:8].rearrange("p k t -> p (k t)").rearrange("p (n d) -> p n d", d=B_HD)))
            kv_pe.wait(dve, "vr")
            kv_dve.done("vr", v.tensor_copy(v_rev[:].rearrange("p q j d -> p (q j d)"),
                                            ps[:, 6:8].rearrange("p k t -> p (k t)")))
            split_tile(dve, T_B)

        def width(b):
            return P if b == 0 else 2 * P

        def pe_b(pe, j, pp):
            mm, tr = nc.tensor.matmul, nc.tensor.transpose
            t = T_B + 3 * pp
            pe_tile(pe, t, j, NB)
            pe_tile(pe, t + 1, j, NB)
            m = lambda name, ins: b_pe.done(f"{name}{pp}", ins)
            out_all_free(pe, t, j, NB)
            for c in range(2):
                b_act.wait(pe, f"sq{c}{pp}", j)
                for q in blocks:
                    o = 2 * (4 * c + q)
                    ins = mm(ps[:, 4, o:o + 2], q_sq[:, c, q * P:q * P + P], half_ones[:], start=True, stop=True)
            m("ss", ins)
            for c in range(2):
                b_dve.wait(pe, f"rw{c}{pp}", j)
                for q in blocks:
                    ins = mm(ps[:, 4 + c, q * P:q * P + P], q_sq[:, c, q * P:q * P + P], ident[:], start=True, stop=True)
                m(f"rb{c}", ins)

            def scores(b):
                if b == 0:
                    b_dve.wait(pe, f"nq1{pp}", j)
                    b_act.wait(pe, "vc0", j)
                    in_all_free(pe, t + 2, j, NB)
                elif b >= 2:
                    b_dve.wait(pe, f"add{b - 2}{pp}", j)
                for hh in range(4):
                    c, lo = hh // 2, B_HD * (hh % 2)
                    ins = mm(ps[:, 2 * (b % 2) + hh % 2, c * 256:c * 256 + width(b)],
                             q_cur[lo:lo + B_HD, c, b * P:b * P + P],
                             k_cur[lo:lo + B_HD, (3 - b) * P:(3 - b) * P + width(b)], start=True, stop=True)
                m(f"S{b}", ins)

            def turn(b):
                b_dve.wait(pe, f"pn{b}{pp}", j)
                if b:
                    b_act.wait(pe, f"pc{b - 1}{pp}", j)
                    if b > 1:
                        b_dve.wait(pe, f"pd{b - 1}{pp}", j)
                for half in range(width(b) // P):
                    for hh in range(4):
                        ins = tr(ps[:, 4 + half, hh * P:hh * P + P], probs[:, b % 2, hh, half * P:half * P + P], ident[:])
                m(f"pt{b}", ins)

            def values(b):
                b_act.wait(pe, f"pc{b}{pp}", j)
                if b:
                    b_dve.wait(pe, f"pd{b}{pp}", j)
                n, k = 2 * (width(b) // P), 0
                for half in range(width(b) // P):
                    for odd in range(2):
                        lo = B_HD * (1 - odd)
                        ins = mm(ps[:, 6 + b // 2, (b % 2) * 256:(b % 2) * 256 + 256],
                                 v_cur[:, b - half, lo:lo + 2 * B_HD],
                                 probs_T[:, b % 2, half, odd::2, :], start=k == 0, stop=k == n - 1)
                        k += 1
                m(f"pv{b}", ins)

            scores(0)
            scores(1)
            turn(0)
            scores(2)
            values(0)
            turn(1)
            scores(3)
            values(1)
            turn(2)
            values(2)
            turn(3)
            values(3)
            pe_tile(pe, t + 2, j, NB)

        def act_b(act, j, pp):
            fn = nc.scalar.activation
            t = T_B + 3 * pp
            m = lambda name, ins: b_act.done(f"{name}{pp}", ins)
            round_tile(act, t + 1, j, NB)
            for c in range(2):
                wait_chunk(act, t, c, j, NB)
                m(f"sq{c}", fn(q_sq[:, c], ps[:, c], ACT.Square))
                fn(q_cur[:, c], ps[:, c], ACT.Copy).then_inc(in_free, 1)
            if pp == 0:
                m("kc", fn(k_cur[:], k_rev[:, bass.ds(j, 1), :].rearrange("p o t -> p (o t)"), ACT.Copy))
                m("vc", fn(v_cur[:, :, B_HD:2 * B_HD],
                           v_rev[:, :, bass.ds(j, 1), :].rearrange("p q o d -> p q (o d)"), ACT.Copy))
            round_tile(act, t + 2, j, NB)
            for c in range(2):
                wait_chunk(act, t + 1, c, j, NB)
                fn(zb_gate[:, c], ps[:, 2 + c], ACT.Silu).then_inc(in_free, 1)
            b_pe.wait(act, f"ss{pp}", j)
            m("root", fn(tok[:, 0:16], ps[:, 4, 0:16], ACT.Sqrt, bias=eps[:, 2:3]))

            def exps(b):
                b_dve.wait(act, f"neg{b}{pp}", j)
                for hh in range(4):
                    p = probs[:, b % 2, hh, 0:width(b)]
                    ins = fn(p, p, ACT.Exp, bias=small["neg"][:, b % 2, hh:hh + 1], accum_out=small["sum"][:, b % 2, hh:hh + 1])
                m(f"ex{b}", ins)
                b_dve.wait(act, f"sd{b}{pp}", j)
                m(f"se{b}", fn(small["sinke"][:, b % 2], small["sinkd"][:, b % 2], ACT.Exp))

            def copy(b):
                b_pe.wait(act, f"pt{b}{pp}", j)
                m(f"pc{b}", fn(probs_T[:, b % 2, 0].rearrange("p h q -> p (h q)"), ps[:, 4], ACT.Copy))

            exps(0)
            exps(1)
            copy(0)
            exps(2)
            copy(1)
            exps(3)
            copy(2)
            copy(3)
            for c in range(2):
                b_dve.wait(act, f"gt{c}{pp}", j)
                fn(a_hi[:, pp, c], zb_gate[:, c], ACT.Copy).then_inc(a_hi_ready, 1)
            round_tile(act, t + 3, j, NB)

        def dve_b(dve, j, pp):
            v = nc.vector
            t = T_B + 3 * pp
            m = lambda name, ins: b_dve.done(f"{name}{pp}", ins)
            own = lambda name: b_dve.wait(dve, f"{name}{pp}", j)
            split_tile(dve, t + 1, j, NB)
            split_tile(dve, t + 2, j, NB)
            b_act.wait(dve, f"root{pp}", j)
            m("rinv", v.reciprocal(tok[:, 0:16], tok[:, 0:16]))
            own("rinv")
            for c in range(2):
                m(f"rw{c}", v.tensor_copy(
                    q_sq[:, c].rearrange("p (n d) -> p n d", d=B_HD),
                    tok[:, 8 * c:8 * c + 8].rearrange("p (n o) -> p n o", o=1).to_broadcast([P, 8, B_HD])))
            for c in range(2):
                b_pe.wait(dve, f"rb{c}{pp}", j)
                m(f"nq{c}", v.scalar_tensor_tensor(q_cur[:, c], q_cur[:, c], col("q_gain", 0), ps[:, 4 + c],
                                                   ALU.mult, ALU.mult))
            sink = sinks[:, bass.ds(j * 8 + 4 * pp, 4)]

            def tops(b):
                b_pe.wait(dve, f"S{b}{pp}", j)
                if b == 0:
                    dve.wait_ge(bias_loaded[pp], j * 16 + 16)
                w, r = width(b), {k: x[:, b % 2] for k, x in small.items()}
                m(f"sk{b}", v.tensor_scalar(r["sink"], sink, 1.0, None, ALU.mult))
                for hh in range(4):
                    o = (hh // 2) * 256
                    ins = v.tensor_tensor_reduce(
                        out=probs[:, b % 2, hh, 0:w], in0=ps[:, 2 * (b % 2) + hh % 2, o:o + w],
                        in1=bias_cur[:, pp, hh, 0:w], scale=1.0, scalar=-3.0e38, op0=ALU.add, op1=ALU.max,
                        accum_out=r["max"][:, hh:hh + 1])
                m(f"add{b}", ins)
                own(f"add{b}")
                m(f"top{b}", v.tensor_tensor(r["top"], r["max"], r["sink"], ALU.max))
                own(f"top{b}")
                m(f"neg{b}", v.tensor_scalar(r["neg"], r["top"], -1.0, None, ALU.mult))
                m(f"sd{b}", v.tensor_tensor(r["sinkd"], r["sink"], r["top"], ALU.subtract))

            def norms(b):
                w, r = width(b), {k: x[:, b % 2] for k, x in small.items()}
                b_act.wait(dve, f"se{b}{pp}", j)
                m(f"dn{b}", v.tensor_tensor(r["den"], r["sum"], r["sinke"], ALU.add))
                own(f"dn{b}")
                m(f"ri{b}", v.reciprocal(r["inv"], r["den"]))
                own(f"ri{b}")
                p = probs[:, b % 2, :, 0:w]
                m(f"pn{b}", v.tensor_tensor(p, p, r["inv"].rearrange("p (h o) -> p h o", o=1).to_broadcast([P, 4, w]),
                                            ALU.mult))

            def copy(b):
                b_pe.wait(dve, f"pt{b}{pp}", j)
                m(f"pd{b}", v.tensor_copy(probs_T[:, b % 2, 1].rearrange("p h q -> p (h q)"), ps[:, 5]))

            tops(0)
            tops(1)
            norms(0)
            tops(2)
            norms(1)
            copy(1)
            tops(3)
            norms(2)
            copy(2)
            norms(3)
            copy(3)
            b_pe.wait(dve, f"pv3{pp}", j)
            for c in range(2):
                o = ps[:, 6:8].rearrange("p k (b c q) -> p c k b q", b=2, c=2)[:, c]
                z = zb_gate[:, c].rearrange("p (k b q) -> p k b q", k=2, b=2)
                m(f"gt{c}", v.tensor_tensor(z, z, o, ALU.mult))
            dve_pair(dve, t + 2, zb_gate, j, NB)
            add_chunks(dve, t + 2, range(0, 2), j, NB)
            split_tile(dve, t + 3, j, NB)
            add_chunks(dve, t + 2, range(2, 8), j, NB)

        f_silu = sem("f_silu")

        def ff_first(f):
            return T_FF[f]

        def pe_ff(pe, f, q):
            t = T_FF[f]
            pe_tile(pe, t, h_from=8 * q, all_free=True)
            pe_tile(pe, t + 1)
            with pe.Fori(0, FF_STEPS // 2) as i:
                for r in range(2):
                    for k in range(3):
                        pe_tile(pe, t + 2 + 3 * r + k, i, 6, all_free=k == 0)
            pe_tile(pe, t + 2 + 3 * (FF_STEPS - 1))

        def ff_silu(act, f, t, s, i=None):
            for c in range(2):
                wait_chunk(act, t, c, i, 6)
                act.wait_ge(in_free, at(in_before, t, i, 6) + (2 * c - 2 + IN_CREDIT))
                nc.scalar.activation(f_gate[:, c], ps[:, c], ACT.Silu).then_inc(f_silu, 1)

        def ff_round(act, f, t, i=None):
            for c in range(2):
                act.wait_ge(in_free, at(in_before, t, i, 6) + (2 * c + 2 + IN_CREDIT))
                buf = a_buf(f, t)
                nc.scalar.activation(a_hi[:, buf, c], f_hid[:, c], ACT.Copy).then_inc(a_hi_ready, 1)

        def a_tile(f, t):
            s = (t - T_FF[f] + 1) // 3
            return T_FF[f] + 4 + 3 * s if s < FF_STEPS - 1 else T_FF[f] + 2 + 3 * (FF_STEPS - 1)

        def a_buf(f, t):
            return pairs_before(a_tile(f, t)) % 2

        def act_ff(act, f):
            t = T_FF[f]
            round_tile(act, t + 1)
            round_tile(act, t + 2)
            ff_silu(act, f, t, 0)
            ff_round(act, f, t)
            with act.Fori(0, FF_STEPS // 2) as i:
                for r in range(2):
                    u = t + 2 + 3 * r
                    round_tile(act, u + 1, i, 6)
                    round_tile(act, u + 2, i, 6)
                    ff_silu(act, f, u, 1 + r, i)
                    round_tile(act, u + 3, i, 6)
                    ff_round(act, f, u, i)
            end = t + 2 + 3 * (FF_STEPS - 1)
            if end + 1 < len(TILES):
                round_tile(act, end + 1)

        def ff_product(dve, f, t, s, i=None):
            n = pairs_before(a_tile(f, t))
            dve.wait_ge(pair_ready, n if i is None else i * 2 + n)
            for c in range(2):
                wait_chunk(dve, t + 1, c, i, 6)
                dve.wait_ge(f_silu, (2 * (FF_STEPS * f + s) + c + 1) if i is None
                            else i * 4 + (2 * (FF_STEPS * f + s) + c + 1))
                nc.vector.tensor_tensor(f_hid[:, c], f_gate[:, c], ps[:, 2 + c], ALU.mult).then_inc(in_free, 2)

        def ff_pair(dve, f, t, i=None):
            u = a_tile(f, t)
            base, buf = pairs_before(u), pairs_before(u) % 2
            for d in range(2):
                n = 2 * base + d + 1
                dve.wait_ge(a_hi_ready, n if i is None else i * 4 + n)
                ins = nc.vector.tensor_tensor(a_lo[:, buf, d], f_hid[:, d], a_hi[:, buf, d].bitcast(F32), ALU.subtract)
            ins.then_inc(pair_ready, 1)

        def dve_ff(dve, f):
            t = T_FF[f]
            split_tile(dve, t + 1)
            split_tile(dve, t + 2)
            ff_product(dve, f, t, 0)
            ff_pair(dve, f, t)
            with dve.Fori(0, FF_STEPS // 2) as i:
                for r in range(2):
                    u = t + 2 + 3 * r
                    split_tile(dve, u + 1, i, 6)
                    split_tile(dve, u + 2, i, 6)
                    ff_product(dve, f, u, 1 + r, i)
                    add_chunks(dve, u + 2, range(0, 2), i, 6, scale=0.5)
                    split_tile(dve, u + 3, i, 6)
                    add_chunks(dve, u + 2, range(2, 4), i, 6, scale=0.5)
                    ff_pair(dve, f, u, i)
                    add_chunks(dve, u + 2, range(4, 8), i, 6, scale=0.5)
            end = t + 2 + 3 * (FF_STEPS - 1)
            add_chunks(dve, end, range(0, 2), scale=0.5)
            if end + 1 < len(TILES):
                split_tile(dve, end + 1)
            add_chunks(dve, end, range(2, 8), scale=0.5)

        pool_step = sem("pool_step")
        pool_consts = sem("pool_consts")

        def gp_pool_consts(pool):
            pool.memset(pool_h[:, :, 0:POOL_PAD], 0.0).then_inc(pool_consts, 1)
            pool.memset(pool_h[:, :, POOL_PAD + T:], 0.0).then_inc(pool_consts, 1)
            n = 2
            for g in range(4):
                w = 2 << g
                pool.memset(inv_cnt[:, g], 1.0 / w).then_inc(pool_consts, 1)
                n += 1
            pool.wait_ge(pool_consts, n)
            for g in range(4):
                w = 2 << g
                for x in range(w // 2):
                    pool.memset(inv_cnt[:, g, x:x + 1], 1.0 / (x + w // 2)).then_inc(pool_consts, 1)
                    n += 1
                for x in range(T - w // 2 + 1, T):
                    pool.memset(inv_cnt[:, g, x:x + 1], 1.0 / (T - x + w // 2)).then_inc(pool_consts, 1)
                    n += 1
            return n

        POOL_CONSTS = 2 + 4 + sum((2 << g) - 1 for g in range(4))

        def dve_pool(dve, m, q, gain):
            v, L = nc.vector, T + 2 * POOL_PAD
            dve.wait_ge(rstd_ready, m + 1)
            dve.wait_ge(pool_consts, POOL_CONSTS)
            k = 0

            def step(ins):
                nonlocal k
                k += 1
                ins.then_inc(pool_step, 1)
                dve.wait_ge(pool_step, k)

            for n in range(KC + 1):
                if n < KC:
                    g, h = n // 2, pool_h[:, n]
                    step(v.scalar_tensor_tensor(h[:, POOL_PAD:POOL_PAD + T], xT[:, n], col(*gain(n)), n_rstd[:],
                                                ALU.mult, ALU.mult))
                    src, lo = h, 0
                    for lvl in range(g + 1):
                        back = 1 if lvl == 0 else 1 << (lvl - 1)
                        ahead = 0 if lvl == 0 else back
                        lo += back
                        a, b = (POOL_PAD, POOL_PAD + T) if lvl == g else (lo, L - lo)
                        dst = pool_s[:, lvl % 2]
                        step(v.tensor_tensor(dst[:, a:b], src[:, a - back:b - back], src[:, a + ahead:b + ahead], ALU.add))
                        src = dst
                    step(v.tensor_tensor(pool_y[:, n % 2], src[:, POOL_PAD:POOL_PAD + T], inv_cnt[:, g], ALU.mult))
                    if n >= 2:
                        dve.wait_ge(h_ready, 8 * q + n - 1)
                    v.tensor_tensor(n_h[:, n % 2], pool_y[:, n % 2], h[:, POOL_PAD:POOL_PAD + T],
                                    ALU.subtract).then_inc(hf_ready, 1)
                if n >= 1:
                    dve.wait_ge(h_hi_ready, 8 * q + n)
                    v.tensor_tensor(h_lo[:, n - 1], n_h[:, (n - 1) % 2], h_hi[:, n - 1].bitcast(F32),
                                    ALU.subtract).then_inc(h_ready, 1)
            for n in range(8):
                wait_chunk(dve, T_POOL, n)
                step(v.tensor_scalar(pool_y[:, n % 2], ps[:, 4 + n % 4], col("pool_b", n), col("pool_scale", n),
                                     ALU.add, ALU.mult))
                v.tensor_tensor(xT[:, n], xT[:, n], pool_y[:, n % 2], ALU.add).then_inc(out_free, 1)
                if n == 1:
                    split_tile(dve, T_POOL + 1)

        NC = 2
        glu_act = sem("glu_act")
        glu_pad = sem("glu_pad")
        dw_step = sem("dw_step")
        ln_pe = Marks(sem("ln_pe"), ["sum", "mean"])
        ln_dve = Marks(sem("ln_dve"), ["mean", "wide", "copy"] + [f"c{n}" for n in range(KC)] + [f"n{n}" for n in range(KC)])
        ln_act = Marks(sem("ln_act"), [f"s{n}" for n in range(KC)])

        def pe_conv(pe, m, q):
            for k in range(NC):
                pe_tile(pe, T_PW1 + k, h_from=8 * q if k == 0 else None)
            with pe.Fori(0, KC // 2 - 1) as i:
                for k in range(NC):
                    pe_tile(pe, T_PW1 + NC + k, i, NC, all_free=k == 0)
            in_all_free(pe, T_PW2)
            pe.wait_ge(dw_step, DW * KC)
            for c in range(TC):
                for n in range(KC):
                    ins = nc.tensor.matmul(ps[:, 0, c:c + 1], dw_y[:, n, c * P:c * P + P], ones[:, 0:1],
                                           start=n == 0, stop=n == KC - 1)
            ln_pe.done("sum", ins)
            ln_dve.wait(pe, "wide")
            for c in range(TC):
                ins = nc.tensor.matmul(ps[:, 1, c * P:c * P + P], n_rb[:, c * P:c * P + P], ident[:], start=True, stop=True)
            ln_pe.done("mean", ins)
            ln_dve.wait(pe, "copy")
            pe_stat(pe, m, T_PW2)
            for s in range(4):
                pe_tile(pe, T_PW2 + s)

        def act_glu(act, base, i=None):
            t = T_PW1 + base
            round_tile(act, t + 1, i, NC)
            round_tile(act, t + 2, i, NC)
            for c in range(2):
                wait_chunk(act, t + 1, c, i, NC)
                act.wait_ge(in_free, at(in_before, t, i, NC) + (2 * c - 2 + IN_CREDIT))
                bias = (col("pw1_b", KC + base + c) if i is None
                        else cols[:, bass.ds(i * 2 + (PARAMS["pw1_b"] + KC + base + c), 1)])
                nc.scalar.activation(glu_s[:, c], ps[:, 2 + c], ACT.Sigmoid, bias=bias).then_inc(glu_act, 1)

        def act_conv(act, m):
            act_glu(act, 0)
            with act.Fori(0, KC // 2 - 1) as i:
                act_glu(act, NC, i)
            act_squares(act, m, lambda e, n: ln_dve.wait(e, f"c{n}"), dw_y)
            act_root(act, m, 3)
            for n in range(KC):
                ln_dve.wait(act, f"n{n}")
                ln_act.done(f"s{n}", nc.scalar.activation(dw_y[:, n], dw_y[:, n], ACT.Silu, bias=col("ln_b", n),
                                                          scale=col("ln_g", n)))
                ln_act.wait(act, f"s{n}")
                buf = pairs_before(T_PW2 + n // 2) % 2
                if n >= 4:
                    wait_chunk(act, T_PW2 + n // 2 - 2, 7)
                nc.scalar.activation(a_hi[:, buf, n % 2], dw_y[:, n], ACT.Copy).then_inc(a_hi_ready, 1)
                if n in (1, 3, 5, 7):
                    round_tile(act, T_PW2 + n // 2 + 1)

        def dve_glu(dve, base, i=None):
            v, t = nc.vector, T_PW1 + base
            split_tile(dve, t + 1, i, NC)
            split_tile(dve, t + 2, i, NC)
            for c in range(2):
                n = base + c
                wait_chunk(dve, t, c, i, NC)
                dve.wait_ge(glu_act, n + 1 if i is None else i * 2 + (n + 1))
                g = glu[:, n:n + 1] if i is None else glu[:, bass.ds(i * 2 + n, 1)]
                bias = col("pw1_b", n) if i is None else cols[:, bass.ds(i * 2 + (PARAMS["pw1_b"] + n), 1)]
                src = ps[:, c:c + 1, :]
                v.scalar_tensor_tensor(g[:, :, DW_PAD:DW_PAD + T], src, bias, glu_s[:, c:c + 1], ALU.add,
                                       ALU.mult).then_inc(in_free, 2)
            for c in range(2):
                n = base + c
                g = glu[:, n:n + 1] if i is None else glu[:, bass.ds(i * 2 + n, 1)]
                y = dw_y[:, n:n + 1] if i is None else dw_y[:, bass.ds(i * 2 + n, 1)]
                dve.wait_ge(in_free, at(in_before, t, i, NC) + (2 * c + 2 + IN_CREDIT))
                for j in range(DW):
                    def pc(r):
                        return cols[:, r:r + 1] if i is None else cols[:, bass.ds(i * 2 + r, 1)]
                    tap = pc(PARAMS["dw"] + j * KC + n)
                    src = g[:, :, j:j + T]
                    if j == 0:
                        ins = v.tensor_scalar(y, src, tap, pc(PARAMS["dw_b"] + n), ALU.mult, ALU.add)
                    else:
                        done = DW * n + j
                        dve.wait_ge(dw_step, done if i is None else i * (2 * DW) + done)
                        ins = v.scalar_tensor_tensor(y, src, tap, y, ALU.mult, ALU.add)
                    ins.then_inc(dw_step, 1)

        def dve_conv(dve, m):
            v = nc.vector
            v.memset(glu[:, :, 0:DW_PAD], 0.0).then_inc(glu_pad, 1)
            v.memset(glu[:, :, DW_PAD + T:], 0.0).then_inc(glu_pad, 1)
            dve.wait_ge(glu_pad, 2)
            dve_glu(dve, 0)
            with dve.Fori(0, KC // 2 - 1) as i:
                dve_glu(dve, NC, i)
            ln_pe.wait(dve, "sum")
            ln_dve.done("mean", v.tensor_scalar(tok[:, 0:4], ps[:, 0, 0:4], 1.0 / D, None, ALU.mult))
            ln_dve.wait(dve, "mean")
            ln_dve.done("wide", v.tensor_copy(by_chunk(n_rb[:]), tok[:, 0:4].rearrange("p (c o) -> p c o", o=1)
                                              .to_broadcast([P, TC, P])))
            ln_pe.wait(dve, "mean")
            ln_dve.done("copy", v.tensor_copy(ln_mean[:], ps[:, 1]))
            ln_dve.wait(dve, "copy")
            for n in range(KC):
                ln_dve.done(f"c{n}", v.tensor_tensor(dw_y[:, n], dw_y[:, n], ln_mean[:], ALU.subtract))
            dve_rstd(dve, m)
            dve.wait_ge(rstd_ready, m + 1)
            for n in range(KC):
                ln_dve.done(f"n{n}", v.tensor_tensor(dw_y[:, n], dw_y[:, n], n_rstd[:], ALU.mult))
            for s in range(2):
                dve_pair(dve, T_PW2 + s, dw_y[:, 2 * s:2 * s + 2])
                if s == 0:
                    split_tile(dve, T_PW2 + 1)
            for s in range(4):
                add_chunks(dve, T_PW2 + s, range(8), bias="pw2_b" if s == 3 else None)
                if s < 3:
                    split_tile(dve, T_PW2 + s + 2)
                if s < 2:
                    dve_pair(dve, T_PW2 + s + 2, dw_y[:, 2 * s + 4:2 * s + 6])

        def sp_setup(sp):
            for q in range(TC):
                sp.dma_start(x_tok[:, q], x[0, q * P:q * P + P, :]).then_inc(x_loaded, 16)

        def over_partitions(v, n):
            return bass.AP(tensor=v.tensor, offset=v.offset, ap=[[0, P], [1, n]])

        def act_loads(act):
            ld = lambda dst, src: act.dma_start(dst, src).then_inc(small_loaded, 16)
            ld(wab_raw[:], a_w_in[0][:, A_AB0:A_AB0 + 16].rearrange("(k p) n -> p k n", p=P))
            ld(a_log[:], over_partitions(a_A_log, A_HEADS))
            ld(a_dt[:], over_partitions(a_dt_bias, A_HEADS))
            ld(sinks[:], over_partitions(b_sinks, B_HEADS))
            ld(rel_in[:], rel_bias)
            act.wait_ge(rows_clear, 1)
            n = 0
            for name, v, rows in (
                    ("a_conv", a_conv[0].rearrange("k (c p) -> (k c) p", p=P), TAPS * 32),
                    ("a_norm", a_norm[0].rearrange("(c p) -> c p", p=P), KC),
                    ("kv_norm", kv_norm.rearrange("(c p) -> c p", p=P), KC),
                    ("b_norm", b_norm[0].rearrange("(c p) -> c p", p=P), KC),
                    ("norm_g", norm_g.rearrange("l n (c p) -> (l n c) p", p=P), 6 * KC),
                    ("pool_b", pool_b[0].rearrange("(c p) -> c p", p=P), KC),
                    ("pool_scale", pool_scale[0].rearrange("(c p) -> c p", p=P), KC),
                    ("pw1_b", pw1_b[0].rearrange("(c p) -> c p", p=P), 2 * KC),
                    ("dw_b", dw_b[0].rearrange("(c p) -> c p", p=P), KC),
                    ("ln_g", ln_g[0].rearrange("(c p) -> c p", p=P), KC),
                    ("ln_b", ln_b[0].rearrange("(c p) -> c p", p=P), KC),
                    ("pw2_b", pw2_b[0].rearrange("(c p) -> c p", p=P), KC),
                    ("final_g", final_g.rearrange("(c p) -> c p", p=P), KC),
                    ("o_gain", a_o_gain[0].rearrange("(c p) -> c p", p=P), 2)):
                r, b = PARAMS[name] % P, PARAMS[name] // P
                act.dma_start(param_rows[r:r + rows, b], v).then_inc(rows_loaded, 16)
                n += 1
            dw = dw_w[0].rearrange("k (c p) -> (k c) p", p=P)
            act.dma_start(param_rows[:, 1], dw[0:P]).then_inc(rows_loaded, 16)
            act.dma_start(param_rows[0:DW_ROWS - P, 2], dw[P:DW_ROWS]).then_inc(rows_loaded, 16)
            for name, v in (("k_gain", k_gain.rearrange("(o d) -> o d", o=1)), ("q_gain", b_q_gain)):
                r = PARAMS[name] % P
                for u in range(2):
                    act.dma_start(param_rows[r:r + 1, 4, u * B_HD:(u + 1) * B_HD], v).then_inc(rows_loaded, 16)
            return n + 6

        ROW_LOADS = 20
        setup_const = sem("setup_const")

        def gp_setup(pool):
            n = 0

            def step(ins):
                nonlocal n
                n += 1
                ins.then_inc(setup_const, 1)
                pool.wait_ge(setup_const, n)

            pool.memset(param_rows[:], 0.0).then_inc(rows_clear, 1)
            step(pool.memset(ident[:], 0.0))
            step(pool.affine_select(out=ident[:], in_=ident[:], compare_op=ALU.not_equal, fill=1.0, base=0,
                                    pattern=[[-1, P]], channel_multiplier=1))
            step(pool.memset(ones[:], 1.0))
            step(pool.affine_select(out=tri[:], in_=ones[:], compare_op=ALU.is_ge, fill=0.0, base=0,
                                    pattern=[[1, P]], channel_multiplier=-1))
            step(pool.memset(flip[:], 0.0))
            step(pool.affine_select(out=flip[:], in_=flip[:], compare_op=ALU.not_equal, fill=1.0, base=-(P - 1),
                                    pattern=[[1, P]], channel_multiplier=1))
            step(pool.memset(causal[:], 0.0))
            step(pool.affine_select(out=causal[:], in_=causal[:], compare_op=ALU.is_ge, fill=MASKED, base=0,
                                    pattern=[[1, P]], channel_multiplier=-1))
            step(pool.memset(half_ones[:], 0.0))
            step(pool.memset(half_ones[0:B_HD, 0:1], 1.0))
            step(pool.memset(half_ones[B_HD:P, 1:2], 1.0))
            for k, e in enumerate((EPS, A_DK * EPS, B_HD * EPS, LN_EPS)):
                step(pool.memset(eps[:, k:k + 1], e))
            step(pool.memset(level_mask[:], 0.0))
            m = level_mask[:, 0].rearrange("p (n u) -> p n u", u=2)[:, :, 1:2]
            step(pool.affine_select(out=m, in_=m, compare_op=ALU.not_equal, fill=1.0, base=0,
                                    pattern=[[-2, P // 2], [0, 1]], channel_multiplier=1))
            for l in range(1, LEVELS):
                b = 1 << l
                m = level_mask[:, l].rearrange("p (n r) -> p n r", r=2 * b)[:, :, 0:b]
                step(pool.memset(m, 1.0))
                step(pool.affine_select(out=m, in_=m, compare_op=ALU.is_ge, fill=0.0, base=-b,
                                        pattern=[[-2 * b, P // (2 * b)], [0, b]], channel_multiplier=1))
                step(pool.affine_select(out=m, in_=m, compare_op=ALU.is_ge, fill=0.0, base=2 * b - 1,
                                        pattern=[[2 * b, P // (2 * b)], [0, b]], channel_multiplier=-1))
            return n

        SETUP_CONSTS = 11 + 4 + 2 + 3 * (LEVELS - 1)

        def gp_relative(pool):
            pool.wait_ge(rel_ready, 1)
            pool.dma_start(rel_scratch, rel_line[:]).then_inc(rel_stored, 16)
            pool.wait_ge(rel_stored, 16)

        def pe_setup(pe):
            pe.sem_inc(chunk_done, CHUNK_CREDIT)
            pe.wait_ge(setup_const, SETUP_CONSTS)
            pe.wait_ge(x_loaded, 16 * TC)
            for k in range(KC):
                if k >= 6:
                    pe.wait_ge(x_ready, k - 5)
                for q in range(TC):
                    ins = nc.tensor.transpose(ps[:, 2 + k % 6, q * P:q * P + P], x_tok[:, q, k * P:k * P + P], ident[:])
                ins.then_inc(setup_pe, 1)
            pe.wait_ge(rows_loaded, 16 * ROW_LOADS)
            for r in range(5):
                ins = nc.tensor.transpose(ps[:, r // 4, (r % 4) * P:(r % 4) * P + P], param_rows[:, r], ident[:])
            ins.then_inc(setup_pe, 1)

        def act_setup(act):
            act.sem_inc(in_free, IN_CREDIT)
            act.wait_ge(small_loaded, SMALL)
            nc.scalar.activation(wab_hi[:], wab_raw[:], ACT.Copy).then_inc(wab_round, 1)
            round_tile(act, 0)

        wab_round, wab_ready = sem("wab_round"), sem("wab_ready")

        def dve_setup(dve):
            v = nc.vector
            dve.sem_inc(lo_done, SPLIT_CREDIT)
            dve.sem_inc(out_free, OUT_CREDIT)
            for k in range(KC):
                dve.wait_ge(setup_pe, k + 1)
                v.tensor_copy(xT[:, k], ps[:, 2 + k % 6]).then_inc(x_ready, 1)
            dve.wait_ge(setup_pe, KC + 1)
            v.tensor_copy(cols[:], ps[:, 0:2].rearrange("p k t -> p (k t)")[:, 0:5 * P]).then_inc(cols_ready, 1)
            dve.wait_ge(wab_round, 1)
            v.tensor_tensor(wab_lo[:], wab_raw[:], wab_hi[:].bitcast(F32), ALU.subtract).then_inc(wab_ready, 1)
            split_tile(dve, 0)
            dve.wait_ge(small_loaded, SMALL)
            v.transpose(rel_T[:], rel_in[:]).then_inc(rel_chain, 1)
            v.memset(rel_line[:], MASKED).then_inc(rel_chain, 1)
            dve.wait_ge(rel_chain, 2)
            for bucket, first, n in bucket_runs():
                o = P - 1 + first
                ins = v.tensor_copy(rel_line[:, o:o + n], rel_T[:, bucket:bucket + 1].to_broadcast([B_HEADS, n]))
                ins.then_inc(rel_chain, 1)
            dve.wait_ge(rel_chain, 2 + len(bucket_runs()))
            dve.sem_inc(rel_ready, 1)

        out_dve = sem("out_dve")

        def dve_output(dve, m):
            v = nc.vector
            dve.wait_ge(rstd_ready, m + 1)
            for n in range(KC):
                v.scalar_tensor_tensor(dw_y[:, n], xT[:, n], col("final_g", n), n_rstd[:], ALU.mult,
                                       ALU.mult).then_inc(out_dve, 1)
            for q in range(1, TC, 2):
                dve.wait_ge(y_pe, q + 1)
                v.tensor_copy(y_tok[:, q], ps[:, 2 * q:2 * q + 2].rearrange("p k t -> p (k t)")).then_inc(y_ready, 1)

        y_act = sem("y_act")

        def act_output(act):
            for q in range(0, TC, 2):
                act.wait_ge(y_pe, q + 1)
                nc.scalar.activation(y_tok[:, q], ps[:, 2 * q:2 * q + 2].rearrange("p k t -> p (k t)"),
                                     ACT.Copy).then_inc(y_act, 1)

        def pe_output(pe):
            pe.wait_ge(out_dve, KC)
            for q in range(TC):
                for n in range(KC):
                    ins = nc.tensor.transpose(ps[:, 2 * q + n // 4, (n % 4) * P:(n % 4) * P + P],
                                              dw_y[:, n, q * P:q * P + P], ident[:])
                ins.then_inc(y_pe, 1)

        def sp_output(sp):
            for q in range(TC):
                sp.wait_ge((y_act, y_ready)[q % 2], q // 2 + 1)
                sp.dma_start(out[0, q * P:q * P + P, :], y_tok[:, q]).then_inc(out_stored, 16)
            sp.wait_ge(out_stored, 16 * TC)

        FF_W = [(0, 0), (0, 1), (1, 0), (1, 1)]
        T_A_END, T_B_END = T_KV, T_FF[0]

        def added(t):
            return lambda e, n: out_added(e, t, n)

        def end_of(f):
            return T_FF[f] + 2 + 3 * (FF_STEPS - 1)

        def gain_of(name, first=0):
            return lambda n: (name, first + n)

        block = ctx.enter_context(nc.Block())

        @block.sync
        def _(sp):
            sp_setup(sp)
            wi = a_w_in[0]
            with sp.Fori(0, A_PAIRS) as i:
                for k, c in enumerate((0, A_QK_W)):
                    load(sp, k, cols256(wi, bass.ds(i * 256 + c, 256)), i, NA)
                for k in range(2):
                    load(sp, 2 + k, cols256(wi, bass.ds(i * 512 + (2 * A_QK_W + 256 * k), 256)), i, NA)
                for k in range(2):
                    load(sp, 4 + k, cols256(wi, bass.ds(i * 512 + (A_Z0 + 256 * k), 256)), i, NA)
                for k in range(2):
                    load(sp, 6 + k, rows256(a_w_out[0], bass.ds(i * 512 + 256 * k, 256)), i, NA)
            for k in range(2):
                load(sp, T_KV + k, cols256(w_kv, slice(256 * k, 256 * k + 256)))
            with sp.Fori(0, B_KV) as j:
                for pp in range(2):
                    t = T_B + 3 * pp
                    for k, c in enumerate((0, B_W)):
                        load(sp, t + k, cols256(b_w_in[0], bass.ds(j * 512 + (256 * pp + c), 256)), j, NB)
                    load(sp, t + 2, rows256(b_w_out[0], bass.ds(j * 512 + 256 * pp, 256)), j, NB)

            def ff(f):
                t, (l, k) = T_FF[f], FF_W[f]
                w_in, w_out = ffn_w_in[l, k], ffn_w_out[l, k]
                load(sp, t, cols256(w_in, slice(0, 256)))
                load(sp, t + 1, cols256(w_in, slice(FF, FF + 256)))
                with sp.Fori(0, FF_STEPS // 2) as i:
                    for r in range(2):
                        u = t + 2 + 3 * r
                        load(sp, u, cols256(w_in, bass.ds(i * 512 + 256 * (r + 1), 256)), i, 6)
                        load(sp, u + 1, cols256(w_in, bass.ds(i * 512 + (FF + 256 * (r + 1)), 256)), i, 6)
                        load(sp, u + 2, rows256(w_out, bass.ds(i * 512 + 256 * r, 256)), i, 6)
                load(sp, end_of(f), rows256(w_out, slice(FF - 256, FF)))

            ff(0)
            load(sp, T_POOL, pool_w[0].rearrange("g (k p) n -> p (g k) n", p=P))
            ff(1)
            ff(2)
            for c in range(2):
                load(sp, T_PW1 + c, cols256(pw1_w[0], slice(D * c, D * c + 256)))
            with sp.Fori(0, KC // 2 - 1) as i:
                for c in range(2):
                    load(sp, T_PW1 + NC + c, cols256(pw1_w[0], bass.ds(i * 256 + (256 + D * c), 256)), i, NC)
            for s in range(4):
                load(sp, T_PW2 + s, rows256(pw2_w[0], slice(256 * s, 256 * s + 256)))
            ff(3)
            sp_output(sp)

        @block.gpsimd
        def _(pool):
            assert gp_setup(pool) == SETUP_CONSTS
            pool_sums(pool, 0)
            gp_relative(pool)
            pool_sums(pool, 1)
            with pool.Fori(0, B_KV) as j:
                for pp in range(2):
                    b_dve.before(pool, f"add3{pp}", j)
                    pool.dma_start(bias_cur[:, pp], rel_band[bass.ds(j * 8 + 4 * pp, 4)].rearrange("h q s -> q h s")
                                   ).then_inc(bias_loaded[pp], 16)
            pool_sums(pool, 2)
            assert gp_pool_consts(pool) == POOL_CONSTS
            for m in range(3, 10):
                pool_sums(pool, m)

        @block.scalar
        def _(act):
            assert act_loads(act) == ROW_LOADS
            act_setup(act)
            act_squares(act, 0, lambda e, n: e.wait_ge(x_ready, n + 1))
            act_root(act, 0)
            act_h(act, 0)
            gates_act.begin(act)
            act_gates(act)
            a_act.begin(act)
            gates_dve.wait(act, "be")
            with act.Fori(0, A_PAIRS) as i:
                act_a(act, i)
            act_squares(act, 1, added(T_A_END - 1))
            act_root(act, 1)
            act_h(act, 1)
            kv_act.begin(act)
            act_kv(act)
            act_h(act, 2)
            b_act.begin(act)
            with act.Fori(0, B_KV) as j:
                for pp in range(2):
                    act_b(act, j, pp)

            def norm(m, q, t):
                act_squares(act, m, added(t))
                act_root(act, m)
                if q is not None:
                    act_h(act, q)

            norm(2, 3, T_B_END - 1)
            act_ff(act, 0)
            norm(3, 4, end_of(0))
            round_tile(act, T_POOL + 1)
            norm(4, 5, T_POOL)
            act_ff(act, 1)
            norm(5, 6, end_of(1))
            act_ff(act, 2)
            norm(6, 7, end_of(2))
            ln_act.begin(act)
            act_conv(act, 7)
            norm(8, 8, T_PW2 + 3)
            act_ff(act, 3)
            norm(9, None, end_of(3))
            act_output(act)

        @block.vector
        def _(dve):
            dve_setup(dve)
            dve.wait_ge(cols_ready, 1)
            dve_rstd(dve, 0)
            dve_h(dve, 0, 0, gain_of("a_norm"))
            gates_dve.begin(dve)
            dve_gates(dve)
            a_dve.begin(dve)
            dve.wait_ge(h_ready, KC)
            dve.wait_ge(rel_stored, 16)
            nc.vector.memset(conv_in[:, :, 0:TAPS - 1], 0.0).then_inc(conv_pad, 1)
            dve.wait_ge(conv_pad, 1)
            gates_dve.wait(dve, "be")
            gates_act.wait(dve, "last")
            with dve.Fori(0, A_PAIRS) as i:
                dve_a(dve, i)
            dve_rstd(dve, 1)
            dve_h(dve, 1, 1, gain_of("kv_norm"))
            kv_dve.begin(dve)
            dve_kv(dve)
            dve_h(dve, 1, 2, gain_of("b_norm"), prev_tile=T_KV + 1)
            b_dve.begin(dve)
            with dve.Fori(0, B_KV) as j:
                for pp in range(2):
                    dve_b(dve, j, pp)
            dve_rstd(dve, 2)
            dve_h(dve, 2, 3, gain_of("norm_g", 0))
            dve_ff(dve, 0)
            dve_rstd(dve, 3)
            dve_pool(dve, 3, 4, gain_of("norm_g", KC))
            dve_rstd(dve, 4)
            dve_h(dve, 4, 5, gain_of("norm_g", 2 * KC))
            dve_ff(dve, 1)
            dve_rstd(dve, 5)
            dve_h(dve, 5, 6, gain_of("norm_g", 3 * KC))
            dve_ff(dve, 2)
            dve_rstd(dve, 6)
            dve_h(dve, 6, 7, gain_of("norm_g", 4 * KC))
            ln_dve.begin(dve)
            dve_conv(dve, 7)
            dve_rstd(dve, 8)
            dve_h(dve, 8, 8, gain_of("norm_g", 5 * KC))
            dve_ff(dve, 3)
            dve_rstd(dve, 9)
            dve_output(dve, 9)

        @block.tensor
        def _(pe):
            pe_setup(pe)
            pe.wait_ge(cols_ready, 1)
            pe_stat(pe, 0, 0)
            pe.wait_ge(wab_ready, 1)
            gates_pe.begin(pe)
            pe_gates(pe)
            a_pe.begin(pe)
            with pe.Fori(0, A_PAIRS) as i:
                pe_a(pe, i)
            pe_stat(pe, 1, T_KV)
            kv_pe.begin(pe)
            pe_kv(pe)
            b_pe.begin(pe)
            pe.wait_ge(h_ready, 8 * 3)
            kv_act.wait(pe, "kr3")
            kv_dve.wait(pe, "vr")
            with pe.Fori(0, B_KV) as j:
                for pp in range(2):
                    pe_b(pe, j, pp)
            pe_stat(pe, 2, T_FF[0])
            pe_ff(pe, 0, 3)
            pe_stat(pe, 3, T_POOL)
            pe_tile(pe, T_POOL, h_from=8 * 4)
            pe_stat(pe, 4, T_POOL + 1)
            pe_ff(pe, 1, 5)
            pe_stat(pe, 5, T_FF[2])
            pe_ff(pe, 2, 6)
            pe_stat(pe, 6, T_PW1)
            ln_pe.begin(pe)
            pe_conv(pe, 7, 7)
            pe_stat(pe, 8, T_FF[3])
            pe_ff(pe, 3, 8)
            pe_stat(pe, 9, len(TILES))
            pe_output(pe)


_INS = ["x", "a_norm", "a_w_in", "a_conv", "a_A_log", "a_dt_bias", "a_o_gain", "a_w_out", "kv_norm", "w_kv",
        "k_gain", "rel_bias", "b_norm", "b_w_in", "b_q_gain", "b_sinks", "b_w_out", "norm_g_2", "ffn_w_in_2",
        "ffn_w_out_2", "pool_w_2", "pool_b_2", "pool_scale_2", "conv_w_pw1_2", "conv_b_pw1_2", "conv_w_dw_2",
        "conv_b_dw_2", "conv_ln_g_2", "conv_ln_b_2", "conv_w_pw2_2", "conv_b_pw2_2", "final_g_2"]


def kernel(**inputs):
    import numpy as _np
    import concourse.bacc as _bacc
    from concourse import mybir as _mybir
    from concourse.bass_utils import run_bass_kernel_spmd as _run

    nc = _bacc.Bacc("TRN2", target_bir_lowering=False, num_devices=1)
    arrays, args = {}, []
    for name in _INS:
        a = _np.ascontiguousarray(inputs[name])
        arrays[f"in_{name}_dram"] = a
        args.append(nc.dram_tensor(f"in_{name}_dram", a.shape, _mybir.dt.from_np(a.dtype), kind="ExternalInput").ap())
    out = nc.dram_tensor("out_dram", (1, T, D), F32, kind="ExternalOutput").ap()
    build(nc, *args, out)
    r = _run(nc, [arrays], core_ids=[0])
    return r.results[0]["out_dram"]
```

```python
import math
from contextlib import ExitStack

import numpy as np

import concourse.bass as bass
from concourse import mybir

F32 = mybir.dt.float32
F32R = mybir.dt.float32r
ACT = mybir.ActivationFunctionType
ALU = mybir.AluOpType

P = 128
D = 1024
T = 512
KC = D // P
TC = T // P
A_HEADS, A_DK, A_DV, TAPS = 8, 128, 256, 4
A_QK_W, A_V_W = A_HEADS * A_DK, A_HEADS * A_DV
A_Z0 = 2 * A_QK_W + A_V_W
A_AB0 = A_Z0 + A_V_W
A_PAIRS = A_HEADS // 2
B_HEADS, B_KV, B_HD = 32, 4, 64
B_W, B_KV_W = B_HEADS * B_HD, B_KV * B_HD
WINDOW = 128
BUCKETS, MAX_DIST = 32, 128
FF = 2816
FF_STEPS = FF // 256
DW = 31
DW_PAD = DW // 2
PE_TAPS = 11
POOL_PAD = 8
LEVELS = 7
TILE = 2048
MASKED = -1e30
EPS, LN_EPS = 1e-6, 1e-5

A_BODY = "IIIIIIOO"
A_TILES = "IIII" + A_BODY * (A_PAIRS - 1) + "IIOO"
B_STEPS = B_HEADS // 4
B_TILES = "II" + "IIO" * (B_STEPS - 1) + "O"
FF_TILES = "II" + "IIO" * (FF_STEPS - 1) + "O"
TILES = A_TILES + "II" + B_TILES
T_KV = len(A_TILES)
T_B = T_KV + 2
T_FF = [len(TILES)]
TILES += FF_TILES
T_POOL = len(TILES)
TILES += "P"
T_FF.append(len(TILES))
TILES += FF_TILES
T_FF.append(len(TILES))
TILES += FF_TILES
T_PW1 = len(TILES)
TILES += "I" * 8
T_PW2 = len(TILES)
TILES += "O" * 4
T_FF.append(len(TILES))
TILES += FF_TILES
CHUNKS = {"I": 2, "O": 8, "P": 8}

CHUNK_CREDIT, SPLIT_CREDIT, IN_CREDIT, OUT_CREDIT = 1, 2, 4, 8


def chunks_before(t):
    return sum(CHUNKS[k] for k in TILES[:t])


def in_before(t):
    return 2 * TILES[:t].count("I")


def out_before(t):
    return 8 * (TILES[:t].count("O") + TILES[:t].count("P"))


def pairs_before(t):
    return TILES[:t].count("O")


def at(f, t, i, period):
    return f(t) if i is None else i * (f(t + period) - f(t)) + f(t)


class Marks:

    def __init__(self, sem, names):
        self.sem, self.names = sem, names
        self.n, self.pos, self.next = len(names), {x: k for k, x in enumerate(names)}, 0
        assert len(self.pos) == self.n

    def begin(self, eng, done=0):
        if done < self.n:
            eng.sem_inc(self.sem, self.n - done)
        self.next = -done

    def done(self, name, ins):
        assert self.names[self.next % self.n] == name, (name, self.names[self.next % self.n])
        self.next += 1
        ins.then_inc(self.sem, 1)

    def wait(self, eng, name, i=0):
        eng.wait_ge(self.sem, i * self.n + (self.n + self.pos[name] + 1))

    def before(self, eng, name, i=0):
        eng.wait_ge(self.sem, i * self.n + (self.pos[name] + 1))


def bucket_runs():
    n = np.arange(WINDOW)
    exact = BUCKETS // 2
    large = exact + (np.log(np.maximum(n, 1) / exact) / np.log(MAX_DIST / exact)
                     * (BUCKETS - exact)).astype(np.int64)
    b = np.where(n < exact, n, np.minimum(large, BUCKETS - 1))
    return [(int(v), int(np.argmax(b == v)), int((b == v).sum())) for v in np.unique(b)]


DW_ROWS = DW * KC
PARAMS = {}


def _place():
    PARAMS["a_conv"] = 0
    PARAMS["dw"] = 128
    row = 3 * 128
    for name, n in (("a_norm", 8), ("kv_norm", 8), ("b_norm", 8), ("norm_g", 48), ("pool_b", 8),
                    ("pool_scale", 8), ("pw1_b", 16), ("dw_b", 8), ("ln_g", 8)):
        PARAMS[name] = row
        row += n
    row = 4 * 128
    for name, n in (("ln_b", 8), ("pw2_b", 8), ("final_g", 8), ("o_gain", 2), ("k_gain", 1),
                    ("q_gain", 1)):
        PARAMS[name] = row
        row += n


_place()


def build(nc, x, a_norm, a_w_in, a_conv, a_A_log, a_dt_bias, a_o_gain, a_w_out, kv_norm, w_kv,
          k_gain, rel_bias, b_norm, b_w_in, b_q_gain, b_sinks, b_w_out, norm_g, ffn_w_in,
          ffn_w_out, pool_w, pool_b, pool_scale, pw1_w, pw1_b, dw_w, dw_b, ln_g, ln_b, pw2_w,
          pw2_b, final_g, out):
    ctx = ExitStack()
    with ctx:
        def sb(name, shape, dt=F32, into=ctx):
            return into.enter_context(nc.sbuf_tensor(name, shape, dt))

        def sem(name):
            return ctx.enter_context(nc.semaphore(name))

        xT = sb("xT", [P, KC, T])
        h_hi = sb("h_hi", [P, KC, T], F32R)
        h_lo = sb("h_lo", [P, KC, T], F32R)
        w_raw = sb("w_raw", [P, 2, TILE])
        w_hi = sb("w_hi", [P, 2, TILE], F32R)
        w_lo = sb("w_lo", [P, 2, TILE], F32R)
        a_hi = sb("a_hi", [P, 2, 2, T], F32R)
        a_lo = sb("a_lo", [P, 2, 2, T], F32R)
        cols = sb("cols", [P, 5 * P])
        ident = sb("ident", [P, P])
        ones = sb("ones", [P, P])
        tri = sb("tri", [P, P])
        flip = sb("flip", [P, P])
        causal = sb("causal", [P, P])
        half_ones = sb("half_ones", [P, 2])
        level_mask = sb("level_mask", [P, LEVELS, P])
        eps = sb("eps", [P, 4])
        tok = sb("tok", [P, 16])
        sinks = sb("sinks", [P, B_HEADS])
        table_junk = sb("table_junk", [P, 1])
        a_neg = sb("a_neg", [P, A_HEADS])
        a_log = sb("a_log", [P, A_HEADS])
        a_dt = sb("a_dt", [P, A_HEADS])
        wab_raw = sb("wab_raw", [P, KC, 16])
        wab_hi = sb("wab_hi", [P, KC, 16], F32R)
        wab_lo = sb("wab_lo", [P, KC, 16], F32R)

        NORM_COLS = 7 * T
        with ExitStack() as s:
            n_sq = sb("n_sq", [P, 2, T], into=s)
            n_sum = sb("n_sum", [P, T], into=s)
            n_rb = sb("n_rb", [P, T], into=s)
            n_rstd = sb("n_rstd", [P, T], into=s)
            n_h = sb("n_h", [P, 2, T], into=s)
        with ExitStack() as s:
            sb("below_setup", [P, NORM_COLS], into=s)
            param_rows = sb("param_rows", [P, 5, P], into=s)
            x_tok = sb("x_tok", [P, TC, D], into=s)
        with ExitStack() as s:
            gate = {k: sb("gate_" + k, [P, TC, A_HEADS], into=s)
                    for k in ("g", "beta", "neg_cum", "beta_exp", "k_decay", "last", "t0", "t1", "t2", "t3", "u")}
            conv_in = sb("conv_in", [P, 2, T + TAPS - 1], into=s)
            qkv = sb("qkv", [P, 8, T], into=s)
            qn = sb("qn", [P, 2, T], into=s)
            square = sb("square", [P, 4, T], into=s)
            g_wide = sb("g_wide", [P, 2, T], into=s)
            b_wide = sb("b_wide", [P, 2, T], into=s)
            masked = sb("masked", [P, 2, T], into=s)
            decay = sb("decay", [P, 2, T], into=s)
            expg = sb("expg", [P, 2, T], into=s)
            lower_T = sb("lower_T", [P, 2, T], into=s)
            qk_T = sb("qk_T", [P, 2, T], into=s)
            k_dec = sb("k_dec", [P, 2, T], into=s)
            v_beta = sb("v_beta", [P, 2, TC, A_DV], into=s)
            v_new = sb("v_new", [P, 2, A_DV], into=s)
            state = sb("state", [P, 2, A_DV], into=s)
            z_gate = sb("z_gate", [P, 4, T], into=s)
        rel_in, rel_T = z_gate[0:BUCKETS, 2, 0:B_HEADS], z_gate[0:B_HEADS, 2, P:P + BUCKETS]
        rel_line = z_gate[0:B_HEADS, 3, 0:3 * P]
        inv_T, inv, prod, neg_wT, k_bg = g_wide, b_wide, masked, decay, expg
        o_out = v_beta[:].rearrange("p a c v -> p (a c v)").rearrange("p (n t) -> p n t", t=T)
        with ExitStack() as s:
            sb("below_b", [P, NORM_COLS], into=s)
            k_rev = sb("k_rev", [P, B_KV, T], into=s)
            v_rev = sb("v_rev", [P, TC, B_KV, B_HD], into=s)
            k_cur = sb("k_cur", [P, T], into=s)
            v_cur = sb("v_cur", [P, TC, 3 * B_HD], into=s)
            bias_cur = sb("bias_cur", [P, 2, 4, 2 * P], into=s)
            small = {k: sb("row_" + k, [P, 2, 4], into=s) for k in ("sink", "max", "top", "neg", "sinkd", "sinke", "sum", "den", "inv")}
            q_cur = sb("q_cur", [P, 2, 2, T], into=s)
            q_sq = sb("q_sq", [P, 2, T], into=s)
            with ExitStack() as s2:
                kvf = sb("kvf", [P, 4, T], into=s2)
                kv_sq = sb("kv_sq", [P, 2, T], into=s2)
                k_tok = sb("k_tok", [P, TC, B_KV, 2, B_HD], into=s2)
                v_tok = sb("v_tok", [P, TC, B_KV_W], into=s2)
            zb_gate = sb("zb_gate", [P, 2, 2, T], into=s)
            probs = sb("probs", [P, 2, 4, 2 * P], into=s)
            probs_T = sb("probs_T", [P, 2, 2, 4, P], into=s)
        with ExitStack() as s:
            sb("below_c", [P, NORM_COLS], into=s)
            f_gate = sb("f_gate", [P, 2, T], into=s)
            f_hid = sb("f_hid", [P, 2, T], into=s)
            inv_cnt = sb("inv_cnt", [P, 4, T + 2 * POOL_PAD], into=s)
            band = sb("band", [P, 4, TC, P + 2 * POOL_PAD], into=s)
            pool_g = sb("pool_g", [P, 4, TC, 256], into=s)
            pool_y = sb("pool_y", [P, 2, T], into=s)
        with ExitStack() as s:
            sb("below_d", [P, NORM_COLS], into=s)
            glu = sb("glu", [P, KC, T + 2 * DW_PAD], into=s)
            glu_s = sb("glu_s", [P, 2, T], into=s)
            dw_y = sb("dw_y", [P, KC, T], into=s)
            glu_hi = sb("glu_hi", [P, 2, T + 2 * DW_PAD], F32R, into=s)
            glu_lo = sb("glu_lo", [P, 2, T + 2 * DW_PAD], F32R, into=s)
            taps_hi = sb("taps_hi", [P, PE_TAPS, KC], F32R, into=s)
            taps_lo = sb("taps_lo", [P, PE_TAPS, KC], F32R, into=s)
            diag_hi = sb("diag_hi", [P, 2, PE_TAPS, P], F32R, into=s)
            diag_lo = sb("diag_lo", [P, 2, PE_TAPS, P], F32R, into=s)
        with ExitStack() as s:
            sb("below_out", [P, NORM_COLS], into=s)
            y_tok = sb("y_tok", [P, TC, D], into=s)
        rel_scratch = nc.dram_tensor("rel_scratch", [B_HEADS, 3 * P], F32, kind="Internal").ap()
        rel_band = bass.AP(tensor=rel_scratch.tensor, offset=0, ap=[[3 * P, B_HEADS], [1, P], [1, 2 * P]])

        ps = ctx.enter_context(nc.psum_tensor("ps", [P, 8, T], F32))

        raw_loaded = [sem("raw_loaded0"), sem("raw_loaded1")]
        hi_done = sem("hi_done")
        lo_done = sem("lo_done")
        chunk_done = sem("chunk_done")
        in_free = sem("in_free")
        out_free = sem("out_free")
        pair_ready = sem("pair_ready")
        a_hi_ready = sem("a_hi_ready")
        conv_pad = sem("conv_pad")
        sq_ready, sum_ready, stat_ready = sem("sq_ready"), sem("sum_ready"), sem("stat_ready")
        root_ready, inv_ready, wide_ready, bcast_ready, rstd_ready = (
            sem("root_ready"), sem("inv_ready"), sem("wide_ready"), sem("bcast_ready"), sem("rstd_ready"))
        hf_ready, h_hi_ready, h_ready = sem("hf_ready"), sem("h_hi_ready"), sem("h_ready")
        x_loaded, rows_clear, rows_loaded, small_loaded = (
            sem("x_loaded"), sem("rows_clear"), sem("rows_loaded"), sem("small_loaded"))
        cols_ready, x_ready = sem("cols_ready"), sem("x_ready")
        setup_pe, rel_ready, rel_stored = sem("setup_pe"), sem("rel_ready"), sem("rel_stored")
        rel_chain = sem("rel_chain")
        SMALL = 16 * 5
        FIRST_TILE = {1: T_KV, 3: T_POOL, 4: T_POOL + 1, 5: T_FF[2], 6: T_PW1, 8: T_FF[3]}
        LN_STAT = 7
        COPIED = (1, 3, 7, 9)
        junk_ready = sem("junk_ready")
        total_ready = sem("total_ready")
        bias_loaded = [sem("bias_loaded0"), sem("bias_loaded1")]
        out_stored, y_ready, y_pe = sem("out_stored"), sem("y_ready"), sem("y_pe")

        def col(name, k):
            c = PARAMS[name] + k
            return cols[:, c:c + 1]

        def cols256(w, c):
            return w[:, c].rearrange("(k p) n -> p k n", p=P)

        def rows256(w, r):
            return w[r, :].rearrange("(k p) n -> p k n", p=P)

        def load(sp, t, src, i=None, period=0):
            sp.wait_ge(lo_done, at(lambda u: u - 2 + SPLIT_CREDIT + 1, t, i, period))
            n = 1024 if len(src.shape) == 3 and src.shape[1] == 2 else 256
            dst = w_raw[:, t % 2].rearrange("p (k n) -> p k n", n=n)
            sp.dma_start(dst, src).then_inc(raw_loaded[t % 2], 16)

        def round_tile(act, t, i=None, period=0):
            act.wait_ge(raw_loaded[t % 2], at(lambda u: 16 * (u // 2 + 1), t, i, period))
            if t >= 2 or i is not None:
                act.wait_ge(chunk_done, at(lambda u: chunks_before(u - 1) + CHUNK_CREDIT, t, i, period))
            nc.scalar.activation(w_hi[:, t % 2], w_raw[:, t % 2], ACT.Copy).then_inc(hi_done, 1)

        def split_tile(dve, t, i=None, period=0):
            dve.wait_ge(hi_done, at(lambda u: u + 1, t, i, period))
            nc.vector.tensor_tensor(w_lo[:, t % 2], w_raw[:, t % 2], w_hi[:, t % 2].bitcast(F32),
                                    ALU.subtract).then_inc(lo_done, 1)

        def arriving(pe, h_from, wh, wl, banks):
            for k in range(KC):
                pe.wait_ge(h_ready, h_from + k + 1)
                for c in range(2):
                    w, dst = slice(k * 256 + c * P, k * 256 + c * P + P), ps[:, banks[c]]
                    nc.tensor.matmul(dst, wh[:, w], h_hi[:, k], start=k == 0, stop=False)
                    nc.tensor.matmul(dst, wh[:, w], h_lo[:, k], start=False, stop=False)
                    ins = nc.tensor.matmul(dst, wl[:, w], h_hi[:, k], start=False, stop=k == KC - 1)
                    if k == KC - 1:
                        ins.then_inc(chunk_done, 1)

        def products(dst, terms):
            for k, (wh, wl, xh, xl) in enumerate(terms):
                last = k == len(terms) - 1
                nc.tensor.matmul(dst, wh, xh, start=(k == 0), stop=False)
                nc.tensor.matmul(dst, wh, xl, start=False, stop=False)
                m = nc.tensor.matmul(dst, wl, xh, start=False, stop=last)
            return m

        def pe_tile(pe, t, i=None, period=0, h_from=None, all_free=False):
            kind, slot = TILES[t], t % 2
            pe.wait_ge(lo_done, at(lambda u: u + 1 + SPLIT_CREDIT, t, i, period))
            wh, wl = w_hi[:, slot], w_lo[:, slot]
            if kind == "I":
                bank = 2 * ((in_before(t) // 2) % 2)
                pe.wait_ge(in_free, at(in_before, t, i, period) + (IN_CREDIT if all_free else IN_CREDIT - 2))
                if h_from is not None:
                    arriving(pe, h_from, wh, wl, (bank, bank + 1))
                    return
                for c in range(2):
                    terms = []
                    for k in range(KC):
                        w = slice(k * 256 + c * P, k * 256 + c * P + P)
                        terms.append((wh[:, w], wl[:, w], h_hi[:, k], h_lo[:, k]))
                    products(ps[:, bank + c], terms).then_inc(chunk_done, 1)
            else:
                pe.wait_ge(pair_ready, at(lambda u: pairs_before(u) + 1, t, i, period))
                buf = pairs_before(t) % 2
                for n in range(8):
                    pe.wait_ge(out_free, at(out_before, t, i, period) + (n - 4 + OUT_CREDIT + 1))
                    terms = []
                    for k in range(2):
                        w = slice(k * D + n * P, k * D + n * P + P)
                        terms.append((wh[:, w], wl[:, w], a_hi[:, buf, k], a_lo[:, buf, k]))
                    products(ps[:, 4 + n % 4], terms).then_inc(chunk_done, 1)

        def add_chunks(dve, t, ns, i=None, period=0, scale=1.0, bias=None, stat=None):
            for n in ns:
                dve.wait_ge(chunk_done, at(chunks_before, t, i, period) + (n + 1 + CHUNK_CREDIT))
                src = ps[:, 4 + n % 4]
                if bias is not None:
                    ins = nc.vector.scalar_tensor_tensor(xT[:, n], src, col(bias, n), xT[:, n], ALU.add, ALU.add)
                else:
                    ins = nc.vector.scalar_tensor_tensor(xT[:, n], src, scale, xT[:, n], ALU.mult, ALU.add)
                ins.then_inc(out_free, 1)
                if stat is not None and n >= 2:
                    dve_sum(dve, stat, n - 1)

        def wait_chunk(eng, t, c, i=None, period=0):
            eng.wait_ge(chunk_done, at(chunks_before, t, i, period) + (c + 1 + CHUNK_CREDIT))

        def out_added(eng, t, n):
            eng.wait_ge(out_free, out_before(t) + n + 1 + OUT_CREDIT)

        def in_all_free(eng, t, i=None, period=0):
            eng.wait_ge(in_free, at(in_before, t, i, period) + IN_CREDIT)

        def out_all_free(eng, t, i=None, period=0):
            eng.wait_ge(out_free, at(out_before, t, i, period) + OUT_CREDIT)

        def act_squares(act, m, ready, src=None):
            for n in range(KC):
                ready(act, n)
                if n >= 2:
                    act.wait_ge(sum_ready, 7 * m + n - 1)
                elif m and n == 1:
                    act.wait_ge(stat_ready, m)
                elif m:
                    act.wait_ge(sum_ready, 7 * m)
                nc.scalar.activation(n_sq[:, n % 2], (xT if src is None else src)[:, n], ACT.Square).then_inc(sq_ready, 1)

        def pe_stat(pe, m, t):
            out_all_free(pe, t)
            pe.wait_ge(total_ready, m + 1 if m < LN_STAT else m)
            for c in range(TC):
                ins = nc.tensor.matmul(ps[:, 6, c:c + 1], n_sum[:, c * P:c * P + P], ones[:, 0:1], start=True, stop=True)
            ins.then_inc(stat_ready, 1)
            pe_spread(pe, m)

        def pe_spread(pe, m):
            pe.wait_ge(wide_ready, m + 1)
            for c in range(TC):
                ins = nc.tensor.matmul(ps[:, 7, c * P:c * P + P], n_rb[:, c * P:c * P + P], ident[:],
                                       start=True, stop=True)
            ins.then_inc(bcast_ready, 1)

        def act_root(act, m, e=0):
            nc.scalar.activation(table_junk[:], eps[:, 0:1], ACT.Sqrt).then_inc(junk_ready, 1)
            act.wait_ge(stat_ready, m + 1)
            if m:
                act.wait_ge(inv_ready, m)
            nc.scalar.activation(tok[:, 0:4], ps[:, 6, 0:4], ACT.Sqrt, bias=eps[:, e:e + 1],
                                 scale=1.0 / D).then_inc(root_ready, 1)

        def dve_sum(dve, m, n):
            dve.wait_ge(sq_ready, 8 * m + n + 1)
            if n > 1:
                dve.wait_ge(sum_ready, 7 * m + n)
            nc.vector.tensor_tensor(n_sum[:], n_sq[:, 0] if n == 1 else n_sum[:], n_sq[:, n % 2],
                                    ALU.add).then_inc(sum_ready, 2 if n == 1 else 1)

        def dve_rstd(dve, m, copied=False, meanwhile=None):
            if m != LN_STAT:
                dve.wait_ge(sq_ready, 8 * m + 8)
                dve.wait_ge(sum_ready, 7 * m + 7)
                nc.vector.tensor_tensor(n_sum[:], n_sum[:], n_sq[:, (KC - 1) % 2], ALU.add).then_inc(total_ready, 1)
            if m in FIRST_TILE:
                split_tile(dve, FIRST_TILE[m])
            dve.wait_ge(root_ready, m + 1)
            if m:
                dve.wait_ge(wide_ready, m)
            nc.vector.reciprocal(tok[:, 4:8], tok[:, 0:4]).then_inc(inv_ready, 1)
            dve.wait_ge(inv_ready, m + 1)
            nc.vector.tensor_copy(n_rb[:].rearrange("p (c q) -> p c q", q=P),
                                  tok[:, 4:8].rearrange("p (c o) -> p c o", o=1).to_broadcast([P, TC, P])
                                  ).then_inc(wide_ready, 1)
            if meanwhile is not None:
                meanwhile(dve)
            dve.wait_ge(bcast_ready, m + 1)
            if copied:
                nc.vector.tensor_copy(n_rstd[:], ps[:, 7]).then_inc(rstd_ready, 1)
                dve.wait_ge(rstd_ready, COPIED.index(m) + 1)

        def dve_h(dve, m, q, gain, prev_tile=None):
            rstd = n_rstd[:] if m in COPIED else ps[:, 7]
            if prev_tile is not None:
                wait_chunk(dve, prev_tile, 1)
            for n in range(KC + 1):
                if n < KC:
                    if n >= 2:
                        dve.wait_ge(h_ready, 8 * q + n - 1)
                    nc.vector.scalar_tensor_tensor(n_h[:, n % 2], xT[:, n], col(*gain(n)), rstd,
                                                   ALU.mult, ALU.mult).then_inc(hf_ready, 1)
                if n >= 1:
                    dve.wait_ge(h_hi_ready, 8 * q + n)
                    nc.vector.tensor_tensor(h_lo[:, n - 1], n_h[:, (n - 1) % 2],
                                            h_hi[:, n - 1].bitcast(F32), ALU.subtract).then_inc(h_ready, 1)

        def act_h(act, q, after={}):
            for n in range(KC):
                act.wait_ge(hf_ready, 8 * q + n + 1)
                nc.scalar.activation(h_hi[:, n], n_h[:, n % 2], ACT.Copy).then_inc(h_hi_ready, 1)
                if n in after:
                    after[n]()

        NA = len(A_BODY)
        heads = (0, 1)
        lv = range(1, LEVELS)
        gates_dve = Marks(sem("gates_dve"), ["z", "pos", "u", "um1", "lost", "rinv", "corr", "l2",
                                             "sp", "g", "ncum", "neg", "be"])
        gates_act = Marks(sem("gates_act"), ["abc", "beta", "abs", "exp", "ln", "alog", "cum", "kdec", "last"])
        gates_pe = Marks(sem("gates_pe"), ["abT", "ab", "cum", "total"])
        a_pe = Marks(sem("a_pe"), [f"ss{c}" for c in range(4)] + [f"gb{a}" for a in heads] + [f"bb{a}" for a in heads]
                     + [f"rb{c}" for c in range(4)]
                     + [f"kk{a}" for a in heads] + [f"qk{a}" for a in heads]
                     + [f"kt{a}" for a in heads]
                     + [f"T0{a}" for a in heads]
                     + [x for l in lv for x in
                        ([f"A{l}{a}" for a in heads] + ([f"vt{a}{l - 1}" for a in heads] if l < 3 else [])
                         + [f"X{l}{a}" for a in heads]
                         + ([f"T{l}{a}" for a in heads] if l < LEVELS - 1 else []))]
                     + [f"nw{a}" for a in heads]
                     + [f"{x}{c}{a}" for c in range(TC) for x in (("vn", "o", "sn") if c < TC - 1 else ("vn", "o"))
                        for a in heads]
                     + [f"os{a}" for a in heads] + [f"or{a}" for a in heads])
        a_act = Marks(sem("a_act"), [f"sq{c}" for c in range(4)] + ["rq", "rk"]
                      + [f"eg{a}" for a in heads] + [f"d{a}" for a in heads]
                      + [f"Tc{l}{a}" for l in range(LEVELS - 1) for a in heads]
                      + [f"nw{a}" for a in heads] + [f"vn{c}{a}" for c in range(TC) for a in heads]
                      + [f"os{a}{d}" for a in heads for d in range(2)] + [f"or{a}" for a in heads]
                      + [f"z{c}" for c in range(4)])
        a_dve = Marks(sem("a_dve"), [f"gw{a}" for a in heads] + [f"bw{a}" for a in heads]
                      + ["rinv"] + [f"rw{c}" for c in range(4)]
                      + [f"msk{a}" for a in heads] + [f"nrm{c}" for c in range(4)]
                      + [f"{x}{a}" for a in heads for x in ("db", "lt", "qk", "qd", "u0", "u1")]
                      + [f"{x}{a}" for a in heads for x in ("kb", "kd")]
                      + [x for l in lv for x in ([f"P{l}{a}" for a in heads]
                         + ([f"vb{l - 1}{a}" for a in heads] if l < 3 else []) + [f"U{l}{a}" for a in heads])]
                      + [f"S{c}{a}" for c in range(TC - 1) for a in heads]
                      + ["orinv0", "orw0", "orinv1", "orw1"]
                      + [x for a in heads for x in (f"oc{a}", f"og{a}0", f"og{a}1")]
                      + [f"gt{a}{d}" for a in heads for d in range(2)])
        QKV = range(8)
        n_act = Marks(sem("n_act"), [f"silu{c}" for c in QKV])
        n_dve = Marks(sem("n_dve"), [f"cv{c + u}{j}" for c in QKV[::2] for j in range(TAPS) for u in range(2)])

        def a_tile_at(k, i):
            if isinstance(i, int) and i == A_PAIRS - 1 and k >= 6:
                return T_KV - 8 + k, None, 0
            return 4 + k, i, NA

        def last_pair(i):
            return isinstance(i, int) and i == A_PAIRS - 1

        def pe_gates(pe, fill):
            pe.wait_ge(h_ready, 8)
            pe.wait_ge(small_loaded, SMALL)
            gates_pe.done("abT", products(ps[0:16, 6], [(wab_hi[:, k], wab_lo[:, k], h_hi[:, k], h_lo[:, k])
                                                        for k in range(KC)]))
            fill(4)
            gates_act.wait(pe, "abc")
            for c in range(TC):
                ins = nc.tensor.transpose(ps[:, 7, 16 * c:16 * c + 16], masked[0:16, 0, c * P:c * P + P],
                                          ident[0:16, 0:16])
            gates_pe.done("ab", ins)

        def pe_cumulate(pe):
            gates_dve.wait(pe, "g")
            g = gate["g"][:].rearrange("p c h -> p (c h)")
            gates_pe.done("cum", nc.tensor.matmul(ps[:, 6, 0:32], tri[:], g, start=True, stop=True))
            gates_pe.done("total", nc.tensor.matmul(ps[:, 6, 32:64], ones[:], g, start=True, stop=True))

        def act_gates(act):
            g = gate
            gates_pe.wait(act, "abT")
            gates_act.done("abc", nc.scalar.activation(masked[0:16, 0], ps[0:16, 6], ACT.Copy))
            gates_pe.wait(act, "ab")
            abp = ps[:, 7, 0:64].rearrange("p (c j) -> p c j", j=16)
            gates_act.done("beta", nc.scalar.activation(g["beta"][:], abp[:, :, 0:8], ACT.Sigmoid))
            gates_dve.wait(act, "z")
            gates_act.done("abs", nc.scalar.activation(g["t1"][:], g["t0"][:], ACT.Abs))
            gates_act.wait(act, "abs")
            gates_act.done("exp", nc.scalar.activation(g["t1"][:], g["t1"][:], ACT.Exp, scale=-1.0))
            gates_dve.wait(act, "u")
            gates_act.done("ln", nc.scalar.activation(g["t2"][:], g["u"][:], ACT.Ln))
            act.wait_ge(small_loaded, SMALL)
            gates_act.done("alog", nc.scalar.activation(a_neg[:], a_log[:], ACT.Exp))

        def act_decays(act):
            g = gate
            gates_dve.wait(act, "neg")
            cum = ps[:, 6, 0:32].rearrange("p (c h) -> p c h", h=8)
            tot = ps[:, 6, 32:64].rearrange("p (c h) -> p c h", h=8)
            gates_act.done("cum", nc.scalar.activation(g["beta_exp"][:], cum, ACT.Exp))
            gates_act.done("kdec", nc.scalar.activation(g["k_decay"][:], g["t3"][:], ACT.Exp))
            gates_act.done("last", nc.scalar.activation(g["last"][:], tot, ACT.Exp))

        def dve_gates(dve):
            g, v = gate, nc.vector
            gates_act.wait(dve, "beta")
            dve.wait_ge(small_loaded, SMALL)
            abp = ps[:, 7, 0:64].rearrange("p (c j) -> p c j", j=16)

            def wide(t):
                return t[:].rearrange("p (o h) -> p o h", o=1).to_broadcast([P, TC, A_HEADS])

            gates_dve.done("z", v.tensor_tensor(g["t0"][:], abp[:, :, 8:16], wide(a_dt), ALU.add))
            gates_dve.wait(dve, "z")
            gates_dve.done("pos", v.tensor_scalar(g["t3"][:], g["t0"][:], 0.0, None, ALU.max))
            gates_act.wait(dve, "exp")
            gates_dve.done("u", v.tensor_scalar(g["u"][:], g["t1"][:], 1.0, None, ALU.add))
            gates_dve.wait(dve, "u")
            gates_dve.done("um1", v.tensor_scalar(g["t0"][:], g["u"][:], -1.0, None, ALU.add))
            gates_dve.wait(dve, "um1")
            gates_dve.done("lost", v.tensor_tensor(g["t1"][:], g["t1"][:], g["t0"][:], ALU.subtract))
            gates_dve.done("rinv", v.reciprocal(g["k_decay"][:], g["u"][:]))
            gates_dve.wait(dve, "rinv")
            gates_dve.done("corr", v.tensor_tensor(g["t1"][:], g["t1"][:], g["k_decay"][:], ALU.mult))
            gates_dve.wait(dve, "corr")
            gates_act.wait(dve, "ln")
            gates_dve.done("l2", v.tensor_tensor(g["t1"][:], g["t1"][:], g["t2"][:], ALU.add))
            gates_dve.wait(dve, "l2")
            gates_dve.done("sp", v.tensor_tensor(g["t1"][:], g["t1"][:], g["t3"][:], ALU.add))
            gates_dve.wait(dve, "sp")
            gates_act.wait(dve, "alog")
            gates_dve.done("g", v.scalar_tensor_tensor(g["g"][:], g["t1"][:], -1.0, wide(a_neg), ALU.mult, ALU.mult))

        def dve_decays(dve):
            g, v = gate, nc.vector
            gates_pe.wait(dve, "total")
            cum = ps[:, 6, 0:32].rearrange("p (c h) -> p c h", h=8)
            tot = ps[:, 6, 32:64].rearrange("p (c h) -> p c h", h=8)
            gates_dve.done("ncum", v.tensor_scalar(g["neg_cum"][:], cum, -1.0, None, ALU.mult))
            gates_dve.wait(dve, "ncum")
            gates_dve.done("neg", v.tensor_tensor(g["t3"][:], tot, g["neg_cum"][:], ALU.add))
            gates_act.wait(dve, "cum")
            gates_dve.done("be", v.tensor_tensor(g["beta_exp"][:], g["beta_exp"][:], g["beta"][:], ALU.mult))

        def by_chunk(ap):
            return ap.rearrange("p (c q) -> p c q", q=P)

        def gate_col(name, i, a):
            return gate[name][:, :, bass.ds(i * 2 + a, 1)]

        def pe_filler(pe, tiles, i=None, period=0, h_from=None):
            def parts():
                for u in tiles:
                    pe.wait_ge(lo_done, at(lambda w: w + 1 + SPLIT_CREDIT, u, i, period))
                    wh, wl = w_hi[:, u % 2], w_lo[:, u % 2]
                    if h_from is not None and u == tiles[0]:
                        pe.wait_ge(in_free, in_before(u) + IN_CREDIT)
                        arriving(pe, h_from, wh, wl, (0, 1))
                        for _ in range(2 * KC):
                            yield
                        continue
                    for c in range(2):
                        pe.wait_ge(in_free, at(in_before, u, i, period) + (c - 1 + IN_CREDIT))
                        for k in range(KC):
                            w, dst = slice(k * 256 + c * P, k * 256 + c * P + P), ps[:, c]
                            nc.tensor.matmul(dst, wh[:, w], h_hi[:, k], start=k == 0, stop=False)
                            nc.tensor.matmul(dst, wh[:, w], h_lo[:, k], start=False, stop=False)
                            ins = nc.tensor.matmul(dst, wl[:, w], h_hi[:, k], start=False, stop=k == KC - 1)
                            if k == KC - 1:
                                ins.then_inc(chunk_done, 1)
                            yield

            left = parts()

            def emit(n=None):
                while n is None or n > 0:
                    if next(left, left) is left:
                        break
                    n = None if n is None else n - 1
            return emit

        def halves(ap, l, u):
            return ap.rearrange("p (n u h) -> p n u h", u=2, h=1 << l)[:, :, u]

        def pe_a_first(pe):
            n = pe_filler(pe, range(4), h_from=0)
            n(16)
            pe_gates(pe, n)
            n(28)
            pe_cumulate(pe)
            n()

        def pe_a(pe, i):
            mm, tr = nc.tensor.matmul, nc.tensor.transpose
            v = lambda t, a, c: t[:, a, c * P:c * P + P]
            pb = lambda b, c: ps[:, b, c * P:c * P + P]
            k0, r, period = a_tile_at(0, i)
            fill = pe_filler(pe, range(k0, k0 + (2 if last_pair(i) else 6)), r, period)
            fill(4)
            out_all_free(pe, *a_tile_at(0, i))
            for c in range(4):
                a_act.wait(pe, f"sq{c}", i)
                for q in range(TC):
                    ins = mm(ps[:, 6, 4 * c + q:4 * c + q + 1], square[:, c, q * P:q * P + P], ones[:, 0:1],
                             start=True, stop=True)
                a_pe.done(f"ss{c}", ins)
            for a in heads:
                a_dve.wait(pe, f"gw{a}", i)
                for c in range(TC):
                    ins = mm(pb(4 + a, c), v(g_wide, a, c), tri[:], start=True, stop=True)
                a_pe.done(f"gb{a}", ins)
            for a in heads:
                a_dve.wait(pe, f"bw{a}", i)
                for c in range(TC):
                    ins = mm(pb(2 + a, c), v(b_wide, a, c), ident[:], start=True, stop=True)
                a_pe.done(f"bb{a}", ins)
            fill(2)
            for c in range(4):
                a_dve.wait(pe, f"rw{c}", i)
                if c == 0:
                    a_act.wait(pe, "rk", i)
                elif c >= 2:
                    a_dve.wait(pe, f"msk{c - 2}", i)
                b = (6, 7, 4, 5)[c]
                for q in range(TC):
                    ins = mm(pb(b, q), square[:, c, q * P:q * P + P], ident[:], start=True, stop=True)
                a_pe.done(f"rb{c}", ins)
            fill(2)
            for a in heads:
                a_dve.wait(pe, f"nrm{2 + a}", i)
                for c in range(TC):
                    ins = mm(pb(4 + a, c), v(qkv, 2 + a, c), v(qkv, 2 + a, c), start=True, stop=True)
                a_pe.done(f"kk{a}", ins)
            for a in heads:
                a_dve.wait(pe, f"nrm{a}", i)
                for c in range(TC):
                    ins = mm(pb(6 + a, c), v(qkv, 2 + a, c), v(qn, a, c), start=True, stop=True)
                a_pe.done(f"qk{a}", ins)
            fill(2)
            for a in heads:
                a_dve.wait(pe, f"db{a}", i)
                for c in range(TC):
                    ins = tr(pb(2 + a, c), v(qkv, 2 + a, c), ident[:])
                a_pe.done(f"kt{a}", ins)
            fill(2)
            for l in range(LEVELS):
                if l:
                    for a in heads:
                        a_act.wait(pe, f"Tc{l - 1}{a}", i)
                        for c in range(TC):
                            ins = mm(halves(pb(4 + a, c), l, 0), v(lower_T, a, c), halves(v(inv, a, c), l, 0),
                                     start=True, stop=True)
                        a_pe.done(f"A{l}{a}", ins)
                    if l < 3:
                        for a in heads:
                            if l == 1:
                                a_dve.wait(pe, f"kd{a}", i)
                                n_act.before(pe, "silu7", i)
                            else:
                                a_dve.wait(pe, f"vb0{a}", i)
                            for c in range(TC):
                                ins = tr(pb(2 + a, c), v(qkv, 3 + l + 2 * a, c), ident[:])
                            a_pe.done(f"vt{a}{l - 1}", ins)
                    fill(3)
                    for a in heads:
                        a_dve.wait(pe, f"P{l}{a}", i)
                        for c in range(TC):
                            ins = mm(halves(pb(6 + a, c), l, 1), v(prod, a, c), halves(v(inv_T, a, c), l, 1),
                                     start=True, stop=True)
                        a_pe.done(f"X{l}{a}", ins)
                    fill(2)
                if l < LEVELS - 1:
                    for a in heads:
                        a_dve.wait(pe, f"U{l}{a}" if l else f"u1{a}", i)
                        for c in range(TC):
                            ins = tr(pb(4 + a, c), v(inv_T, a, c), ident[:])
                        a_pe.done(f"T{l}{a}", ins)
                    fill(2)
            for a in heads:
                a_dve.wait(pe, f"U{LEVELS - 1}{a}", i)
                for c in range(TC):
                    ins = mm(pb(2 + a, c), v(k_bg, a, c), v(inv_T, a, c), start=True, stop=True)
                a_pe.done(f"nw{a}", ins)
            for c in range(TC):
                for a in heads:
                    b = ps[:, 4 + a, 0:A_DV]
                    if c:
                        a_dve.wait(pe, f"S{c - 1}{a}", i)
                        a_act.wait(pe, f"nw{a}", i)
                    ins = mm(b, v(inv_T, a, c), v_beta[:, a, c], start=True, stop=c == 0)
                    if c:
                        ins = mm(b, v(neg_wT, a, c), state[:, a], start=False, stop=True)
                    a_pe.done(f"vn{c}{a}", ins)
                fill(2)
                for a in heads:
                    a_act.wait(pe, f"vn{c}{a}", i)
                    if c == 0:
                        a_act.wait(pe, "nw1", i)
                    for d in range(2):
                        b = pb((2, 3, 6, 7)[2 * a + d], c)
                        if c:
                            mm(b, state[:, a, d * P:d * P + P], v(qn, a, c), start=True, stop=False)
                        ins = mm(b, v_new[:, a, d * P:d * P + P], v(qk_T, a, c), start=c == 0, stop=True)
                    a_pe.done(f"o{c}{a}", ins)
                if c < TC - 1:
                    for a in heads:
                        ins = mm(ps[:, 4 + a, A_DV:2 * A_DV], v(k_dec, a, c), v_new[:, a], start=True, stop=True)
                        a_pe.done(f"sn{c}{a}", ins)
                fill(2)
            fill(4)
            for a in heads:
                for q in range(TC):
                    for d in range(2):
                        a_act.wait(pe, f"os{a}{d}", i)
                        ins = mm(ps[:, 4, 4 * a + q:4 * a + q + 1], square[:, 2 * a + d, q * P:q * P + P],
                                 ones[:, 0:1], start=d == 0, stop=d == 1)
                a_pe.done(f"os{a}", ins)
            fill(8)
            for a in heads:
                a_dve.wait(pe, f"orw{a}", i)
                a_act.wait(pe, "or1", i)
                for q in range(TC):
                    ins = mm(pb(4 + a, q), square[:, 2 * a, q * P:q * P + P], ident[:], start=True, stop=True)
                a_pe.done(f"or{a}", ins)
            fill()
            for k in (6, 7):
                pe_tile(pe, *a_tile_at(k, i))

        def act_take_q(act, c, i):
            if isinstance(i, int) and i < 0:
                wait_chunk(act, c // 2, c % 2)
            else:
                t, r, period = a_tile_at(2 + c // 2, i)
                wait_chunk(act, t, c % 2, r, period)
            if c >= 2:
                n_dve.wait(act, f"cv{c - 2}{TAPS - 1}", i)
            elif not isinstance(i, int):
                n_dve.before(act, f"cv{c + 6}{TAPS - 1}", i)
            nc.scalar.activation(conv_in[:, c % 2, TAPS - 1:], ps[:, c % 2], ACT.Copy).then_inc(in_free, 1)

        def act_silu(act, c, i):
            n_dve.wait(act, f"cv{c}{TAPS - 1}", i)
            n_act.done(f"silu{c}", nc.scalar.activation(qkv[:, c], qkv[:, c], ACT.Silu))

        def act_a_first(act):
            n_act.begin(act, n_act.n)
            round_tile(act, 1)
            for c in (0, 1):
                act_take_q(act, c, -1)
            round_tile(act, 2)
            act_gates(act)
            for c in (2, 3):
                act_take_q(act, c, -1)
            round_tile(act, 3)
            act_decays(act)
            for c in (0, 1):
                act_silu(act, c, -1)
            for c in (4, 5):
                act_take_q(act, c, -1)
            round_tile(act, 4)
            for c in (2, 3):
                act_silu(act, c, -1)
            for c in (6, 7):
                act_take_q(act, c, -1)
            for c in range(4, 8):
                act_silu(act, c, -1)

        def act_a(act, i):
            fn = nc.scalar.activation
            last = last_pair(i)

            def take_z(c):
                t, r, period = a_tile_at(c // 2, i)
                wait_chunk(act, t, c % 2, r, period)
                fn(z_gate[:, c], ps[:, c % 2], ACT.Copy).then_inc(in_free, 1)

            def take(c):
                if not last:
                    act_take_q(act, c, i)

            def rounded(k):
                if not last or k <= 1:
                    round_tile(act, *a_tile_at(k, i))
                elif k in (2, 3):
                    round_tile(act, T_KV - 4 + k)

            for c in range(4):
                n_act.before(act, f"silu{c}", i)
                a_act.done(f"sq{c}", fn(square[:, c], qkv[:, c], ACT.Square))
            rounded(1)
            a_pe.wait(act, "ss3", i)
            a_act.done("rq", fn(tok[:, 0:8], ps[:, 6, 0:8], ACT.Sqrt, bias=eps[:, 1:2], scale=float(A_DK)))
            a_act.done("rk", fn(tok[:, 8:16], ps[:, 6, 8:16], ACT.Sqrt, bias=eps[:, 0:1]))
            for a in heads:
                a_pe.wait(act, f"gb{a}", i)
                a_act.done(f"eg{a}", fn(expg[:, a], ps[:, 4 + a], ACT.Exp))
            for a in heads:
                a_dve.wait(act, f"msk{a}", i)
                for c in range(TC):
                    ins = fn(decay[:, a, c * P:c * P + P], masked[:, a, c * P:c * P + P], ACT.Exp,
                             bias=gate["neg_cum"][:, c, bass.ds(i * 2 + a, 1)])
                a_act.done(f"d{a}", ins)
            take_z(0)

            def turned(l):
                for a in heads:
                    a_pe.wait(act, f"T{l}{a}", i)
                    a_act.done(f"Tc{l}{a}", fn(inv[:, a], ps[:, 4 + a], ACT.Copy))

            turned(0)
            take_z(1)
            rounded(2)
            turned(1)
            take_z(2)
            turned(2)
            take_z(3)
            rounded(3)
            turned(3)
            take(0)
            turned(4)
            turned(5)
            take(1)
            rounded(4)
            for a in heads:
                a_pe.wait(act, f"nw{a}", i)
                a_act.done(f"nw{a}", fn(neg_wT[:, a], ps[:, 2 + a], ACT.Copy, scale=-1.0))
            for c in range(TC):
                for a in heads:
                    a_pe.wait(act, f"vn{c}{a}", i)
                    if c:
                        a_pe.wait(act, f"sn{c - 1}{a}", i)
                    a_act.done(f"vn{c}{a}", fn(v_new[:, a], ps[:, 4 + a, 0:A_DV], ACT.Copy))
                if c == 0:
                    take(2)
                elif c == 2:
                    take(3)
                    rounded(5)
            for a in heads:
                a_pe.wait(act, f"o{TC - 1}{a}", i)
                for d in range(2):
                    a_act.done(f"os{a}{d}", fn(square[:, 2 * a + d], ps[:, (2, 3, 6, 7)[2 * a + d]], ACT.Square))
            take(4)
            a_pe.wait(act, "os1", i)
            for a in heads:
                a_act.done(f"or{a}", fn(tok[:, 4 * a:4 * a + 4], ps[:, 4, 4 * a:4 * a + 4], ACT.Sqrt,
                                        bias=eps[:, 0:1], scale=1.0 / A_DV))
            take(5)
            rounded(6)
            for c in range(4):
                a_act.done(f"z{c}", fn(z_gate[:, c], z_gate[:, c], ACT.Silu))
            if not last:
                for c in range(4):
                    act_silu(act, c, i)
            for a in heads:
                for d in range(2):
                    a_dve.wait(act, f"gt{a}{d}", i)
                    fn(a_hi[:, a, d], z_gate[:, 2 * a + d], ACT.Copy).then_inc(a_hi_ready, 1)
            take(6)
            take(7)
            rounded(7)
            if last:
                round_tile(act, T_KV)
            else:
                act_silu(act, 4, i)
                act_silu(act, 5, i)
                round_tile(act, 4 + NA, i, NA)
                for c in (6, 7):
                    act_silu(act, c, i)

        def dve_pair(dve, t, src, i=None, period=0):
            buf = pairs_before(t) % 2
            for d in range(2):
                dve.wait_ge(a_hi_ready, at(lambda u: 2 * pairs_before(u), t, i, period) + (d + 1))
                ins = nc.vector.tensor_tensor(a_lo[:, buf, d], src[:, d], a_hi[:, buf, d].bitcast(F32), ALU.subtract)
            ins.then_inc(pair_ready, 1)

        def dve_tap(dve, c, j, i, n=None):
            v = nc.vector
            if j == 0:
                if n is None:
                    t, r, period = a_tile_at(2 + c // 2, i)
                else:
                    t, r, period = c // 2, None, 0
                dve.wait_ge(in_free, at(in_before, t, r, period) + (2 + IN_CREDIT))
            w = (0, 8)[c == 2] if c < 4 else 16 + c - 4
            step = 2 if c < 4 else 4
            for u in range(2):
                src = conv_in[:, u, j:j + T]
                row = PARAMS["a_conv"] + j * 32 + w + u
                tap = cols[:, row:row + 1] if n is not None else cols[:, bass.ds(i * step + (row + step), 1)]
                dst = qkv[:, c + u]
                if j == 0:
                    ins = v.tensor_scalar(dst, src, tap, None, ALU.mult)
                else:
                    n_dve.wait(dve, f"cv{c + u}{j - 1}", i)
                    ins = v.scalar_tensor_tensor(dst, src, tap, dst, ALU.mult, ALU.add)
                n_dve.done(f"cv{c + u}{j}", ins)

        def dve_a_first(dve):
            def convolved(c):
                for j in range(TAPS):
                    dve_tap(dve, c, j, -1, 0)

            n_dve.begin(dve, n_dve.n)
            split_tile(dve, 1)
            dve.wait_ge(conv_pad, 1)
            convolved(0)
            split_tile(dve, 2)
            dve_gates(dve)
            convolved(2)
            split_tile(dve, 3)
            dve_decays(dve)
            dve_relative(dve)
            convolved(4)
            split_tile(dve, 4)
            convolved(6)

        def dve_a(dve, i):
            v = nc.vector
            last = last_pair(i)

            def convolved(c):
                if not last:
                    for j in range(TAPS):
                        dve_tap(dve, c, j, i)

            def split(k):
                if not last or k <= 1:
                    split_tile(dve, *a_tile_at(k, i))
                elif k in (2, 3):
                    split_tile(dve, T_KV - 4 + k)

            a_pe.before(dve, "o31", i)
            for name, wide in (("g", g_wide), ("beta", b_wide)):
                for a in heads:
                    a_dve.done(f"{name[0]}w{a}", v.tensor_copy(
                        by_chunk(wide[:, a]), gate_col(name, i, a).to_broadcast([P, TC, P])))
            split(1)
            a_act.wait(dve, "rk", i)
            a_act.wait(dve, "rq", i)
            a_dve.done("rinv", v.reciprocal(tok[:, 0:16], tok[:, 0:16]))
            a_dve.wait(dve, "rinv", i)
            for c in range(4):
                a_dve.done(f"rw{c}", v.tensor_copy(by_chunk(square[:, c]),
                           tok[:, 4 * c:4 * c + 4].rearrange("p (c o) -> p c o", o=1).to_broadcast([P, TC, P])))
            mask4 = causal[:].rearrange("p (o q) -> p o q", o=1).to_broadcast([P, TC, P])
            lvl4 = lambda l: level_mask[:, l:l + 1, :].to_broadcast([P, TC, P])
            ident4 = ident[:].rearrange("p (o q) -> p o q", o=1).to_broadcast([P, TC, P])
            for a in heads:
                a_act.wait(dve, f"eg{a}", i)
                a_dve.done(f"msk{a}", v.tensor_tensor(by_chunk(masked[:, a]), by_chunk(ps[:, 4 + a]), mask4, ALU.add))
            for c in range(4):
                a_pe.wait(dve, f"rb{c}", i)
                dst = qn[:, c] if c < 2 else qkv[:, c]
                a_dve.done(f"nrm{c}", v.tensor_tensor(dst, qkv[:, c], ps[:, (6, 7, 4, 5)[c]], ALU.mult))
            for a in heads:
                a_act.wait(dve, f"d{a}", i)
                a_dve.done(f"db{a}", v.tensor_tensor(lower_T[:, a], decay[:, a], ps[:, 2 + a], ALU.mult))
                a_dve.wait(dve, f"db{a}", i)
                a_pe.wait(dve, f"kk{a}", i)
                a_dve.done(f"lt{a}", v.tensor_tensor(lower_T[:, a], lower_T[:, a], ps[:, 4 + a], ALU.mult))
                a_pe.wait(dve, f"qk{a}", i)
                a_dve.done(f"qk{a}", v.tensor_tensor(qk_T[:, a], decay[:, a], ps[:, 6 + a], ALU.mult))
                a_dve.done(f"qd{a}", v.tensor_tensor(qn[:, a], qn[:, a], expg[:, a], ALU.mult))
                a_dve.wait(dve, f"lt{a}", i)
                a_dve.done(f"u0{a}", v.tensor_tensor(by_chunk(inv_T[:, a]), by_chunk(lower_T[:, a]), lvl4(0), ALU.mult))
                a_dve.wait(dve, f"u0{a}", i)
                a_dve.done(f"u1{a}", v.tensor_tensor(by_chunk(inv_T[:, a]), ident4, by_chunk(inv_T[:, a]), ALU.subtract))
            for a in heads:
                wide = lambda name, n: gate_col(name, i, a).to_broadcast([P, TC, n])
                a_pe.wait(dve, f"kt{a}", i)
                a_dve.wait(dve, f"qd{a}", i)
                a_dve.done(f"kb{a}", v.tensor_tensor(by_chunk(k_bg[:, a]), by_chunk(ps[:, 2 + a]), wide("beta_exp", P), ALU.mult))
                a_dve.done(f"kd{a}", v.tensor_tensor(by_chunk(k_dec[:, a]), by_chunk(ps[:, 2 + a]), wide("k_decay", P), ALU.mult))
            for l in lv:
                for a in heads:
                    a_pe.wait(dve, f"A{l}{a}", i)
                    a_dve.done(f"P{l}{a}", v.tensor_tensor(by_chunk(prod[:, a]), by_chunk(ps[:, 4 + a]), lvl4(l), ALU.mult))
                if l < 3:
                    for a in heads:
                        a_pe.wait(dve, f"vt{a}{l - 1}", i)
                        a_dve.done(f"vb{l - 1}{a}", v.tensor_tensor(
                            v_beta[:, a, :, (l - 1) * P:l * P], by_chunk(ps[:, 2 + a]),
                            gate_col("beta", i, a).to_broadcast([P, TC, P]), ALU.mult))
                for a in heads:
                    a_pe.wait(dve, f"X{l}{a}", i)
                    half = halves(inv_T[:, a], l, 1)
                    a_dve.done(f"U{l}{a}", v.tensor_tensor(half, half, halves(ps[:, 6 + a], l, 1), ALU.subtract))
                if l == 1:
                    split(2)
                elif l == 3:
                    split(3)
                elif l == 6:
                    convolved(0)
                    split(4)
            for c in range(TC - 1):
                for a in heads:
                    a_pe.wait(dve, f"sn{c}{a}", i)
                    if c == 0:
                        ins = v.tensor_copy(state[:, a], ps[:, 4 + a, A_DV:])
                    else:
                        decayed = gate["last"][:, c, bass.ds(i * 2 + a, 1)]
                        ins = v.scalar_tensor_tensor(state[:, a], state[:, a], decayed, ps[:, 4 + a, A_DV:], ALU.mult, ALU.add)
                    a_dve.done(f"S{c}{a}", ins)
            convolved(2)
            split(5)
            for a in heads:
                a_act.wait(dve, f"or{a}", i)
                s = slice(4 * a, 4 * a + 4)
                a_dve.done(f"orinv{a}", v.reciprocal(tok[:, s], tok[:, s]))
                a_dve.wait(dve, f"orinv{a}", i)
                a_dve.done(f"orw{a}", v.tensor_copy(by_chunk(square[:, 2 * a]),
                           tok[:, s].rearrange("p (c o) -> p c o", o=1).to_broadcast([P, TC, P])))
            convolved(4)
            split(6)
            for a in heads:
                a_pe.wait(dve, f"or{a}", i)
                a_dve.done(f"oc{a}", v.tensor_copy(square[:, 2 * a + 1], ps[:, 4 + a]))
                a_dve.wait(dve, f"oc{a}", i)
                for d in range(2):
                    a_dve.done(f"og{a}{d}", v.scalar_tensor_tensor(
                        o_out[:, 2 * a + d], ps[:, (2, 3, 6, 7)[2 * a + d]], col("o_gain", d), square[:, 2 * a + 1],
                        ALU.mult, ALU.mult))
            for a in heads:
                for d in range(2):
                    c = 2 * a + d
                    a_act.wait(dve, f"z{c}", i)
                    a_dve.wait(dve, f"og{a}{d}", i)
                    a_dve.done(f"gt{a}{d}", v.tensor_tensor(z_gate[:, c], z_gate[:, c], o_out[:, c], ALU.mult))
                t, r, period = a_tile_at(6 + a, i)
                dve_pair(dve, t, z_gate[:, 2 * a:2 * a + 2], r, period)
            split(7)
            t, r, period = a_tile_at(6, i)
            add_chunks(dve, t, range(0, 4), r, period)
            for n in range(4):
                add_chunks(dve, t, (4 + n,), r, period)
                if not last:
                    dve_tap(dve, 6, n, i)
            if not last:
                split_tile(dve, 4 + NA, i, NA)
            add_chunks(dve, t + 1, range(0, 8), r, period, stat=1 if last else None)

        NB = 2 * len("IIO")
        kv_pe = Marks(sem("kv_pe"), ["ss", "rb0", "rb1", "kt", "vt", "kr0", "kr1", "kr2", "kr3", "vr"])
        kv_act = Marks(sem("kv_act"), ["sq0", "sq1", "root", "vt", "kr0", "kr1", "kr2", "kr3"])
        kv_dve = Marks(sem("kv_dve"), ["pad0", "pad1", "rinv", "rw0", "rw1", "n0", "n1", "kt0", "kt1", "vr"])
        blocks = range(TC)
        b_pe = Marks(sem("b_pe"), [f"{x}{pp}" for pp in range(2) for x in
                     ("S0", "S1", "pt0", "S2", "pv0", "pt1", "S3", "pv1", "pt2", "pv2", "pt3", "pv3")])
        b_act = Marks(sem("b_act"), [f"{x}{pp}" for pp in range(2) for x in
                      ((["kc", "vc"] if pp == 0 else [])
                       + ["ex0", "se0", "ex1", "se1", "pc0", "ex2", "se2", "pc1", "ex3", "se3", "pc2", "pc3"])])
        b_dve = Marks(sem("b_dve"), [f"{x}{pp}" for pp in range(2) for x in
                      [y for step in ("T0", "N0", "T1", "T2", "N1", "D1", "T3", "N2", "D2", "N3", "D3")
                         for y in {"T": [f"sk{step[1]}", f"add{step[1]}", f"top{step[1]}", f"neg{step[1]}", f"sd{step[1]}"],
                                   "N": [f"dn{step[1]}", f"ri{step[1]}", f"pn{step[1]}"],
                                   "D": [f"pd{step[1]}"]}[step[0]]]
                      + ["gt0", "gt1"]])
        q_pe = Marks(sem("q_pe"), [f"{x}{pp}" for pp in range(2) for x in ("ss", "rb0", "rb1")])
        q_act = Marks(sem("q_act"), [f"{x}{pp}" for pp in range(2) for x in ("sq0", "sq1", "root")])
        q_dve = Marks(sem("q_dve"), [f"{x}{pp}" for pp in range(2) for x in ("rinv", "rw0", "rw1", "nq0", "nq1")])

        def pe_kv(pe):
            mm, tr = nc.tensor.matmul, nc.tensor.transpose
            pe_tile(pe, T_KV, h_from=8)
            pe_tile(pe, T_KV + 1)
            out_all_free(pe, T_KV)
            for c in range(2):
                kv_act.wait(pe, f"sq{c}")
                for q in blocks:
                    o = 2 * (4 * c + q)
                    ins = mm(ps[:, 4, o:o + 2], kv_sq[:, c, q * P:q * P + P], half_ones[:], start=True, stop=True)
            kv_pe.done("ss", ins)
            q_pe.begin(pe, 3)
            b_pe.begin(pe)
            fill = pe_filler(pe, (T_B, T_B + 1), h_from=8 * 2)
            fill(16)
            for c in range(2):
                kv_dve.wait(pe, f"rw{c}")
                for q in blocks:
                    ins = mm(ps[:, 4 + c, q * P:q * P + P], kv_sq[:, c, q * P:q * P + P], ident[:], start=True, stop=True)
                kv_pe.done(f"rb{c}", ins)
            fill(4)
            for name, first, bank in (("kt", 0, 6), ("vt", 2, 2)):
                if first == 0:
                    kv_dve.wait(pe, "n1")
                for q in blocks:
                    for c in range(2):
                        o = ((q % 2) * 2 + c) * P
                        ins = tr(ps[:, bank + q // 2, o:o + P], kvf[:, first + c, q * P:q * P + P], ident[:])
                kv_pe.done(name, ins)
            fill(4)
            kv_dve.wait(pe, "kt1")
            kv_act.wait(pe, "vt")
            for j in range(B_KV):
                for q in blocks:
                    ins = mm(ps[:, 2 + j, (3 - q) * P:(4 - q) * P],
                             k_tok[:, q, j].rearrange("p u d -> p (u d)"), flip[:], start=True, stop=True)
                kv_pe.done(f"kr{j}", ins)
            for q in blocks:
                o = (q % 2) * 256
                ins = mm(ps[:, 6 + q // 2, o:o + 256], flip[:], v_tok[:, q], start=True, stop=True)
            kv_pe.done("vr", ins)
            fill(4)
            kv_act.wait(pe, "kr3")
            kv_dve.wait(pe, "vr")
            pe_q_squares(pe, -1, 1)
            fill()
            pe_q_spread(pe, -1, 1)

        def act_kv(act):
            fn = nc.scalar.activation
            round_tile(act, T_KV + 1)
            for c in range(4):
                wait_chunk(act, T_KV + c // 2, c % 2)
                fn(kvf[:, c], ps[:, c], ACT.Copy).then_inc(in_free, 1)
                if c < 2:
                    act.wait_ge(in_free, in_before(T_KV) + c + 1 + IN_CREDIT)
                    kv_act.done(f"sq{c}", fn(kv_sq[:, c], kvf[:, c], ACT.Square))
            round_tile(act, T_B)
            kv_pe.wait(act, "ss")
            kv_act.done("root", fn(tok[:, 0:16], ps[:, 4, 0:16], ACT.Sqrt, bias=eps[:, 0:1], scale=1.0 / B_HD))
            act_h(act, 2)
            round_tile(act, T_B + 1)
            q_act.begin(act, 3)
            b_act.begin(act)
            for c in range(2):
                act_q_take(act, c, T_B, None, -1, 1)
            kv_pe.wait(act, "vt")
            kv_act.done("vt", fn(v_tok[:].rearrange("p q c -> p (q c)"),
                                 ps[:, 2:4].rearrange("p k t -> p (k t)"), ACT.Copy))
            for j in range(B_KV):
                kv_pe.wait(act, f"kr{j}")
                kv_act.done(f"kr{j}", fn(k_rev[:, j], ps[:, 2 + j], ACT.Copy))
            act_q_root(act, -1, 1)
            round_tile(act, T_B + 2)
            for c in range(2):
                act_z_take(act, c, T_B + 1, None, 1)

        def dve_kv(dve):
            v = nc.vector
            kv_dve.done("pad0", v.memset(v_cur[:, :, 0:B_HD], 0.0))
            kv_dve.done("pad1", v.memset(v_cur[:, :, 2 * B_HD:], 0.0))
            split_tile(dve, T_KV + 1)
            kv_act.wait(dve, "root")
            kv_dve.done("rinv", v.reciprocal(tok[:, 0:16], tok[:, 0:16]))
            kv_dve.wait(dve, "rinv")
            for c in range(2):
                kv_dve.done(f"rw{c}", v.tensor_copy(
                    kv_sq[:, c].rearrange("p (n d) -> p n d", d=B_HD),
                    tok[:, 8 * c:8 * c + 8].rearrange("p (n o) -> p n o", o=1).to_broadcast([P, 8, B_HD])))
            split_tile(dve, T_B)
            dve_h(dve, 1, 2, gain_of("b_norm"), prev_tile=T_KV + 1)
            split_tile(dve, T_B + 1)
            for c in range(2):
                kv_pe.wait(dve, f"rb{c}")
                kv_dve.done(f"n{c}", v.scalar_tensor_tensor(kvf[:, c], kvf[:, c], col("k_gain", 0), ps[:, 4 + c],
                                                            ALU.mult, ALU.mult))
            kv_pe.wait(dve, "kt")
            for u in range(2):
                kv_dve.done(f"kt{u}", v.tensor_copy(
                    k_tok[:, :, :, u, :].rearrange("p q j d -> p (q j) d"),
                    ps[:, 6:8].rearrange("p k t -> p (k t)").rearrange("p (n d) -> p n d", d=B_HD)))
            kv_pe.wait(dve, "vr")
            kv_dve.done("vr", v.tensor_copy(v_rev[:].rearrange("p q j d -> p (q j d)"),
                                            ps[:, 6:8].rearrange("p k t -> p (k t)")))
            q_dve.begin(dve, 5)
            b_dve.begin(dve)
            dve_q_inverse(dve, -1, 1)
            dve_q_scale(dve, -1, 1)
            split_tile(dve, T_B + 2)

        def width(b):
            return P if b == 0 else 2 * P

        def b_out_tile(j, pp):
            return (T_B + 4 + 3 * pp, j) if pp == 0 or not last_step(j, pp) else (T_FF[0] - 1, None)

        def last_step(j, pp):
            return isinstance(j, int) and 2 * j + pp == B_STEPS - 1

        def pe_q_squares(pe, j, pp):
            b_dve.wait(pe, f"add3{pp}", j)
            for c in range(2):
                q_act.wait(pe, f"sq{c}{pp}", j)
                for q in blocks:
                    o = 2 * (4 * c + q)
                    ins = nc.tensor.matmul(ps[:, 3, o:o + 2], q_sq[:, c, q * P:q * P + P], half_ones[:], start=True, stop=True)
            q_pe.done(f"ss{pp}", ins)

        def pe_q_spread(pe, j, pp):
            for c in range(2):
                q_dve.wait(pe, f"rw{c}{pp}", j)
                for q in blocks:
                    ins = nc.tensor.matmul(ps[:, 2 + c, q * P:q * P + P], q_sq[:, c, q * P:q * P + P], ident[:],
                                           start=True, stop=True)
                q_pe.done(f"rb{c}{pp}", ins)

        def pe_b(pe, j, pp):
            mm, tr = nc.tensor.matmul, nc.tensor.transpose
            m = lambda name, ins: b_pe.done(f"{name}{pp}", ins)
            last = last_step(j, pp)
            fill = (lambda n: None) if last else pe_filler(pe, (T_B + 2 + 3 * pp, T_B + 3 + 3 * pp), j, NB)

            def scores(b):
                if b == 0:
                    if pp:
                        q_dve.wait(pe, "nq10", j)
                    else:
                        q_dve.before(pe, "nq11", j)
                    b_act.wait(pe, "vc0", j)
                else:
                    b_dve.wait(pe, f"add{b - 1}{pp}", j)
                for hh in range(4):
                    c, lo = hh // 2, B_HD * (hh % 2)
                    ins = mm(ps[:, 2 + hh % 2, c * 256:c * 256 + width(b)],
                             q_cur[lo:lo + B_HD, pp, c, b * P:b * P + P],
                             k_cur[lo:lo + B_HD, (3 - b) * P:(3 - b) * P + width(b)], start=True, stop=True)
                m(f"S{b}", ins)

            def turn(b):
                b_dve.wait(pe, f"pn{b}{pp}", j)
                if b:
                    b_act.wait(pe, f"pc{b - 1}{pp}", j)
                    if b > 1:
                        b_dve.wait(pe, f"pd{b - 1}{pp}", j)
                else:
                    if pp == 0:
                        out_all_free(pe, T_B + 2, j, NB)
                    else:
                        out_all_free(pe, T_B + 2 + 3, j, NB)
                for half in range(width(b) // P):
                    for hh in range(4):
                        ins = tr(ps[:, 4 + half, hh * P:hh * P + P], probs[:, b % 2, hh, half * P:half * P + P], ident[:])
                m(f"pt{b}", ins)

            def values(b):
                b_act.wait(pe, f"pc{b}{pp}", j)
                if b:
                    b_dve.wait(pe, f"pd{b}{pp}", j)
                n, k = 2 * (width(b) // P), 0
                for half in range(width(b) // P):
                    for odd in range(2):
                        lo = B_HD * (1 - odd)
                        ins = mm(ps[:, 6 + b // 2, (b % 2) * 256:(b % 2) * 256 + 256],
                                 v_cur[:, b - half, lo:lo + 2 * B_HD],
                                 probs_T[:, b % 2, half, odd::2, :], start=k == 0, stop=k == n - 1)
                        k += 1
                m(f"pv{b}", ins)

            scores(0)
            fill(4)
            scores(1)
            fill(4)
            turn(0)
            scores(2)
            fill(4)
            values(0)
            turn(1)
            scores(3)
            fill(4)
            values(1)
            turn(2)
            if not last:
                pe_q_squares(pe, j, pp)
            fill(3)
            values(2)
            if not last:
                pe_q_spread(pe, j, pp)
            fill(2)
            turn(3)
            fill(3)
            values(3)
            fill(8)
            fill(0)
            t, i = b_out_tile(j, pp)
            pe_tile(pe, t, i, NB)

        def act_q_take(act, c, t, i, j, pp):
            wait_chunk(act, t, c, i, NB)
            q_act.done(f"sq{c}{pp}", nc.scalar.activation(q_sq[:, c], ps[:, c], ACT.Square))
            nc.scalar.activation(q_cur[:, 1 - pp, c], ps[:, c], ACT.Copy).then_inc(in_free, 1)

        def act_z_take(act, c, t, i, pp):
            wait_chunk(act, t, c, i, NB)
            nc.scalar.activation(zb_gate[:, 1 - pp, c], ps[:, c], ACT.Silu).then_inc(in_free, 1)

        def act_q_root(act, j, pp):
            q_pe.wait(act, f"ss{pp}", j)
            q_act.done(f"root{pp}", nc.scalar.activation(tok[:, 0:16], ps[:, 3, 0:16], ACT.Sqrt, bias=eps[:, 2:3]))

        def act_b(act, j, pp):
            fn = nc.scalar.activation
            t = T_B + 2 + 3 * pp
            last = last_step(j, pp)
            m = lambda name, ins: b_act.done(f"{name}{pp}", ins)
            if pp == 0:
                m("kc", fn(k_cur[:], k_rev[:, bass.ds(j, 1), :].rearrange("p o t -> p (o t)"), ACT.Copy))
                m("vc", fn(v_cur[:, :, B_HD:2 * B_HD],
                           v_rev[:, :, bass.ds(j, 1), :].rearrange("p q o d -> p q (o d)"), ACT.Copy))

            def exps(b):
                b_dve.wait(act, f"neg{b}{pp}", j)
                for hh in range(4):
                    p = probs[:, b % 2, hh, 0:width(b)]
                    ins = fn(p, p, ACT.Exp, bias=small["neg"][:, b % 2, hh:hh + 1], accum_out=small["sum"][:, b % 2, hh:hh + 1])
                m(f"ex{b}", ins)
                b_dve.wait(act, f"sd{b}{pp}", j)
                m(f"se{b}", fn(small["sinke"][:, b % 2], small["sinkd"][:, b % 2], ACT.Exp))

            def copy(b):
                b_pe.wait(act, f"pt{b}{pp}", j)
                m(f"pc{b}", fn(probs_T[:, b % 2, 0].rearrange("p h q -> p (h q)"), ps[:, 4], ACT.Copy))

            exps(0)
            round_tile(act, t + 1, j, NB)
            exps(1)
            copy(0)
            exps(2)
            if not last:
                act_q_take(act, 0, t, j, j, pp)
            copy(1)
            exps(3)
            if not last:
                act_q_take(act, 1, t, j, j, pp)
            copy(2)
            if not last:
                act_q_root(act, j, pp)
                round_tile(act, t + 2, j, NB)
            copy(3)
            if not last:
                act_z_take(act, 0, t + 1, j, pp)
            for c in range(2):
                b_dve.wait(act, f"gt{c}{pp}", j)
                fn(a_hi[:, pp, c], zb_gate[:, pp, c], ACT.Copy).then_inc(a_hi_ready, 1)
            if not last:
                act_z_take(act, 1, t + 1, j, pp)
                round_tile(act, t + 3, j, NB)

        def dve_q_inverse(dve, j, pp):
            q_act.wait(dve, f"root{pp}", j)
            q_dve.done(f"rinv{pp}", nc.vector.reciprocal(tok[:, 0:16], tok[:, 0:16]))
            q_dve.wait(dve, f"rinv{pp}", j)
            for c in range(2):
                q_dve.done(f"rw{c}{pp}", nc.vector.tensor_copy(
                    q_sq[:, c].rearrange("p (n d) -> p n d", d=B_HD),
                    tok[:, 8 * c:8 * c + 8].rearrange("p (n o) -> p n o", o=1).to_broadcast([P, 8, B_HD])))

        def dve_q_scale(dve, j, pp):
            for c in range(2):
                q_pe.wait(dve, f"rb{c}{pp}", j)
                q = q_cur[:, 1 - pp, c]
                q_dve.done(f"nq{c}{pp}", nc.vector.scalar_tensor_tensor(q, q, col("q_gain", 0), ps[:, 2 + c],
                                                                        ALU.mult, ALU.mult))

        def dve_b(dve, j, pp):
            v = nc.vector
            t = T_B + 2 + 3 * pp
            last = last_step(j, pp)
            m = lambda name, ins: b_dve.done(f"{name}{pp}", ins)
            own = lambda name: b_dve.wait(dve, f"{name}{pp}", j)
            sink = sinks[:, bass.ds(j * 8 + 4 * pp, 4)]

            def tops(b):
                b_pe.wait(dve, f"S{b}{pp}", j)
                if b == 0:
                    dve.wait_ge(bias_loaded[pp], j * 16 + 16)
                w, r = width(b), {k: x[:, b % 2] for k, x in small.items()}
                m(f"sk{b}", v.tensor_scalar(r["sink"], sink, 1.0, None, ALU.mult))
                for hh in range(4):
                    o = (hh // 2) * 256
                    ins = v.tensor_tensor_reduce(
                        out=probs[:, b % 2, hh, 0:w], in0=ps[:, 2 + hh % 2, o:o + w],
                        in1=bias_cur[:, pp, hh, 0:w], scale=1.0, scalar=-3.0e38, op0=ALU.add, op1=ALU.max,
                        accum_out=r["max"][:, hh:hh + 1])
                m(f"add{b}", ins)
                own(f"add{b}")
                m(f"top{b}", v.tensor_tensor(r["top"], r["max"], r["sink"], ALU.max))
                own(f"top{b}")
                m(f"neg{b}", v.tensor_scalar(r["neg"], r["top"], -1.0, None, ALU.mult))
                m(f"sd{b}", v.tensor_tensor(r["sinkd"], r["sink"], r["top"], ALU.subtract))

            def norms(b):
                w, r = width(b), {k: x[:, b % 2] for k, x in small.items()}
                b_act.wait(dve, f"se{b}{pp}", j)
                m(f"dn{b}", v.tensor_tensor(r["den"], r["sum"], r["sinke"], ALU.add))
                own(f"dn{b}")
                m(f"ri{b}", v.reciprocal(r["inv"], r["den"]))
                own(f"ri{b}")
                p = probs[:, b % 2, :, 0:w]
                m(f"pn{b}", v.tensor_tensor(p, p, r["inv"].rearrange("p (h o) -> p h o", o=1).to_broadcast([P, 4, w]),
                                            ALU.mult))

            def copy(b):
                b_pe.wait(dve, f"pt{b}{pp}", j)
                m(f"pd{b}", v.tensor_copy(probs_T[:, b % 2, 1].rearrange("p h q -> p (h q)"), ps[:, 5]))

            tops(0)
            norms(0)
            tops(1)
            split_tile(dve, t + 1, j, NB)
            tops(2)
            norms(1)
            copy(1)
            tops(3)
            norms(2)
            copy(2)
            if not last:
                dve_q_inverse(dve, j, pp)
            norms(3)
            if not last:
                dve_q_scale(dve, j, pp)
            copy(3)
            if not last:
                split_tile(dve, t + 2, j, NB)
            b_pe.wait(dve, f"pv3{pp}", j)
            for c in range(2):
                o = ps[:, 6:8].rearrange("p k (b c q) -> p c k b q", b=2, c=2)[:, c]
                z = zb_gate[:, pp, c].rearrange("p (k b q) -> p k b q", k=2, b=2)
                m(f"gt{c}", v.tensor_tensor(z, z, o, ALU.mult))
            t_out, i = b_out_tile(j, pp)
            dve_pair(dve, t_out, zb_gate[:, pp], i, NB)
            add_chunks(dve, t_out, range(0, 2), i, NB)
            if not last:
                split_tile(dve, t + 3, j, NB)
            add_chunks(dve, t_out, range(2, 8), i, NB, stat=2 if last else None)

        f_silu = sem("f_silu")

        def pe_ff(pe, f, q):
            t = T_FF[f]
            pe_tile(pe, t, h_from=8 * q, all_free=True)
            pe_tile(pe, t + 1)
            with pe.Fori(0, FF_STEPS // 2) as i:
                for r in range(2):
                    for k in range(3):
                        pe_tile(pe, t + 2 + 3 * r + k, i, 6, all_free=k == 0)
            pe_tile(pe, t + 2 + 3 * (FF_STEPS - 1))

        def ff_silu(act, t, i=None):
            for c in range(2):
                wait_chunk(act, t, c, i, 6)
                act.wait_ge(in_free, at(in_before, t, i, 6) + (2 * c - 2 + IN_CREDIT))
                nc.scalar.activation(f_gate[:, c], ps[:, c], ACT.Silu).then_inc(f_silu, 1)

        def ff_round(act, f, t, i=None):
            for c in range(2):
                act.wait_ge(in_free, at(in_before, t, i, 6) + (2 * c + 2 + IN_CREDIT))
                buf = a_buf(f, t)
                nc.scalar.activation(a_hi[:, buf, c], f_hid[:, c], ACT.Copy).then_inc(a_hi_ready, 1)

        def a_tile(f, t):
            s = (t - T_FF[f] + 1) // 3
            return T_FF[f] + 4 + 3 * s if s < FF_STEPS - 1 else T_FF[f] + 2 + 3 * (FF_STEPS - 1)

        def a_buf(f, t):
            return pairs_before(a_tile(f, t)) % 2

        def act_ff(act, f):
            t = T_FF[f]
            round_tile(act, t + 1)
            round_tile(act, t + 2)
            ff_silu(act, t)
            ff_round(act, f, t)
            with act.Fori(0, FF_STEPS // 2) as i:
                for r in range(2):
                    u = t + 2 + 3 * r
                    round_tile(act, u + 1, i, 6)
                    round_tile(act, u + 2, i, 6)
                    ff_silu(act, u, i)
                    round_tile(act, u + 3, i, 6)
                    ff_round(act, f, u, i)
            end = t + 2 + 3 * (FF_STEPS - 1)
            if end + 1 < len(TILES):
                round_tile(act, end + 1)

        def ff_product(dve, f, t, s, i=None):
            n = pairs_before(a_tile(f, t))
            dve.wait_ge(pair_ready, n if i is None else i * 2 + n)
            for c in range(2):
                wait_chunk(dve, t + 1, c, i, 6)
                dve.wait_ge(f_silu, (2 * (FF_STEPS * f + s) + c + 1) if i is None
                            else i * 4 + (2 * (FF_STEPS * f + s) + c + 1))
                nc.vector.tensor_tensor(f_hid[:, c], f_gate[:, c], ps[:, 2 + c], ALU.mult).then_inc(in_free, 2)

        def ff_pair(dve, f, t, i=None):
            u = a_tile(f, t)
            base, buf = pairs_before(u), pairs_before(u) % 2
            for d in range(2):
                n = 2 * base + d + 1
                dve.wait_ge(a_hi_ready, n if i is None else i * 4 + n)
                ins = nc.vector.tensor_tensor(a_lo[:, buf, d], f_hid[:, d], a_hi[:, buf, d].bitcast(F32), ALU.subtract)
            ins.then_inc(pair_ready, 1)

        def dve_ff(dve, f):
            t = T_FF[f]
            split_tile(dve, t + 1)
            split_tile(dve, t + 2)
            ff_product(dve, f, t, 0)
            ff_pair(dve, f, t)
            with dve.Fori(0, FF_STEPS // 2) as i:
                for r in range(2):
                    u = t + 2 + 3 * r
                    split_tile(dve, u + 1, i, 6)
                    split_tile(dve, u + 2, i, 6)
                    ff_product(dve, f, u, 1 + r, i)
                    add_chunks(dve, u + 2, range(0, 2), i, 6, scale=0.5)
                    split_tile(dve, u + 3, i, 6)
                    add_chunks(dve, u + 2, range(2, 4), i, 6, scale=0.5)
                    ff_pair(dve, f, u, i)
                    add_chunks(dve, u + 2, range(4, 8), i, 6, scale=0.5)
            end = t + 2 + 3 * (FF_STEPS - 1)
            add_chunks(dve, end, range(0, 2), scale=0.5)
            add_chunks(dve, end, range(2, 8), scale=0.5, stat=(3, 5, 6, 9)[f])

        pool_step = sem("pool_step")
        pool_consts = sem("pool_consts")
        pool_g_made, pool_g_out = sem("pool_g_made"), sem("pool_g_out")

        def gp_pool_consts(pool):
            pool.wait_ge(sq_ready, 8 * 2 + 8)
            n = 0

            def step(ins):
                nonlocal n
                n += 1
                ins.then_inc(pool_consts, 1)
                return n

            for g in range(4):
                step(pool.memset(inv_cnt[:, g], 1.0 / (2 << g)))
            pool.wait_ge(pool_consts, n)
            for g in range(4):
                w = 2 << g
                for x in [*range(w // 2), *range(T - w // 2 + 1, T)]:
                    count = min(x + w // 2, T) - max(x - w // 2, 0)
                    step(pool.memset(inv_cnt[:, g, POOL_PAD + x:POOL_PAD + x + 1], 1.0 / count))
            pool.wait_ge(pool_consts, n)
            width_ = P + 2 * POOL_PAD
            for g in range(4):
                half = 1 << g
                for c in range(TC):
                    step(pool.affine_select(out=band[:, g, c], in_=inv_cnt[:, g, c * P:c * P + width_],
                                            compare_op=ALU.is_ge, fill=0.0, base=POOL_PAD + half,
                                            pattern=[[-1, width_]], channel_multiplier=1))
                pool.wait_ge(pool_consts, n)
                step(pool.affine_select(out=band[:, g], in_=band[:, g], compare_op=ALU.is_ge, fill=0.0,
                                        base=half - POOL_PAD - 1, pattern=[[0, TC], [1, width_]],
                                        channel_multiplier=-1))
                pool.wait_ge(pool_consts, n)
                own = band[:, g, :, POOL_PAD:POOL_PAD + P]
                step(nc.gpsimd.tensor_tensor(own, own, ident[:].rearrange("p (o q) -> p o q", o=1)
                                             .to_broadcast([P, TC, P]), ALU.subtract))
            return n

        POOL_CONSTS = 4 + sum((2 << g) - 1 for g in range(4)) + 4 * (TC + 2)

        def pe_pool(pe, q):
            mm = nc.tensor.matmul
            wh, wl = w_hi[:, T_POOL % 2], w_lo[:, T_POOL % 2]

            def by_matrix(g):
                pe.wait_ge(h_ready, 8 * q + 2 * g + 2)
                if g >= 2:
                    pe.wait_ge(pool_g_out, g - 1)
                for c in range(TC):
                    t = slice(c * P, c * P + P)
                    terms = []
                    for k in (2 * g, 2 * g + 1):
                        w = slice(k * 256, k * 256 + 256)
                        terms.append((h_hi[:, k, t], h_lo[:, k, t], wh[:, w], wl[:, w]))
                    ins = products(ps[:, 2 * (g % 2) + c // 2, (c % 2) * 256:(c % 2) * 256 + 256], terms)
                ins.then_inc(pool_g_made, 1)

            def pooled(g):
                pe.wait_ge(pool_g_out, g + 1)
                for n in (2 * g, 2 * g + 1):
                    pe.wait_ge(out_free, out_before(T_POOL) + (n - 4 + OUT_CREDIT + 1))
                    dst = ps[:, 4 + n % 4]
                    src = lambda c: pool_g[:, g, c, (n % 2) * P:(n % 2) * P + P]
                    for c in range(TC):
                        mm(dst[:, c * P:c * P + P], src(c), band[:, g, c, POOL_PAD:POOL_PAD + P],
                           start=c == 0, stop=False)
                    for c in range(TC):
                        if c:
                            ins = mm(dst[:, c * P - POOL_PAD:c * P], src(c), band[:, g, c, 0:POOL_PAD],
                               start=False, stop=c == TC - 1)
                        if c < TC - 1:
                            mm(dst[:, c * P + P:c * P + P + POOL_PAD], src(c), band[:, g, c, POOL_PAD + P:],
                               start=False, stop=False)
                    ins.then_inc(chunk_done, 1)

            pe.wait_ge(lo_done, T_POOL + 1 + SPLIT_CREDIT)
            in_all_free(pe, T_POOL)
            by_matrix(0)
            by_matrix(1)
            pe.wait_ge(pool_consts, POOL_CONSTS)
            pooled(0)
            by_matrix(2)
            pooled(1)
            by_matrix(3)
            pooled(2)
            pooled(3)

        def act_pool_out(act, g):
            act.wait_ge(pool_g_made, g + 1)
            nc.scalar.activation(pool_g[:, g].rearrange("p c n -> p (c n)"),
                                 ps[:, 2 * (g % 2):2 * (g % 2) + 2].rearrange("p k t -> p (k t)"),
                                 ACT.Copy).then_inc(pool_g_out, 1)

        def act_pool(act, q):
            act_h(act, q, {3: lambda: act_pool_out(act, 0), 5: lambda: act_pool_out(act, 1),
                           7: lambda: act_pool_out(act, 2)})
            act_pool_out(act, 3)

        def dve_pool(dve):
            v = nc.vector
            for n in range(8):
                wait_chunk(dve, T_POOL, n)
                v.tensor_scalar(pool_y[:, n % 2], ps[:, 4 + n % 4], col("pool_b", n), col("pool_scale", n),
                                ALU.add, ALU.mult).then_inc(pool_step, 1)
                dve.wait_ge(pool_step, n + 1)
                v.tensor_tensor(xT[:, n], xT[:, n], pool_y[:, n % 2], ALU.add).then_inc(out_free, 1)
                if n >= 2:
                    dve_sum(dve, 4, n - 1)

        NC = 2
        glu_act = sem("glu_act")
        glu_pad = sem("glu_pad")
        dw_step = sem("dw_step")
        taps_done, diag_ready = sem("taps_done"), sem("diag_ready")
        glu_hi_done, glu_lo_done, taps_split = sem("glu_hi_done"), sem("glu_lo_done"), sem("taps_split")
        taps_added = sem("taps_added")
        DW_STEPS = 2 * (DW - PE_TAPS)
        tap_rows = cols[:, PARAMS["dw"]:PARAMS["dw"] + PE_TAPS * KC]
        ln_pe = Marks(sem("ln_pe"), ["sum"])
        ln_dve = Marks(sem("ln_dve"), [f"c{n}" for n in range(KC)] + [f"n{n}" for n in range(KC)])
        ln_act = Marks(sem("ln_act"), [f"s{n}" for n in range(KC)])

        def pe_taps(pe, i=None):
            pe.wait_ge(glu_lo_done, KC // 2 if i is None else i + 1)
            pe.wait_ge(taps_added, KC if i is None else i * 2 + 2)
            for c in range(2):
                pe.wait_ge(diag_ready, 4 * (KC // 2) - 2 + 2 * c if i is None else i * 4 + (2 + 2 * c))
                products(ps[:, 4 + c], [(diag_hi[:, c, j], diag_lo[:, c, j], glu_hi[:, c, j:j + T],
                                         glu_lo[:, c, j:j + T]) for j in range(PE_TAPS)]).then_inc(taps_done, 1)

        def pe_conv(pe, m, q):
            for k in range(NC):
                pe_tile(pe, T_PW1 + k, h_from=8 * q if k == 0 else None)
            with pe.Fori(0, KC // 2 - 1) as i:
                for k in range(NC):
                    pe_tile(pe, T_PW1 + NC + k, i, NC, all_free=k == 0)
                pe_taps(pe, i)
            pe_taps(pe)
            in_all_free(pe, T_PW2)
            for n in range(KC):
                if n in (0, KC - 2):
                    pe.wait_ge(taps_added, KC if n == 0 else KC + 2)
                ins = nc.tensor.matmul(ps[:, 0], ones[:], dw_y[:, n], start=n == 0, stop=n == KC - 1)
            ln_pe.done("sum", ins)
            for n in range(KC):
                pe.wait_ge(sq_ready, 8 * m + n + 1)
                for c in range(TC):
                    ins = nc.tensor.matmul(ps[:, 6, c:c + 1], n_sq[:, n % 2, c * P:c * P + P], ones[:, 0:1],
                                           start=n == 0 and c == 0, stop=n == KC - 1 and c == TC - 1)
                ins.then_inc(sum_ready if n < KC - 1 else stat_ready, 1)
            pe_spread(pe, m)
            for s in range(4):
                pe_tile(pe, T_PW2 + s)

        def gp_taps(pool):
            pool.wait_ge(taps_split, 2)
            with pool.Fori(0, KC // 2) as i:
                for c in range(2):
                    pool.wait_ge(taps_done, i * 2 + (1 + c))
                    for dst, src in ((diag_hi, taps_hi), (diag_lo, taps_lo)):
                        tap = src[:, :, bass.ds(i * 2 + c, 1)].bitcast(F32).to_broadcast([P, PE_TAPS, P])
                        nc.gpsimd.tensor_tensor(dst[:, c], ident[:].rearrange("p (o q) -> p o q", o=1)
                                                .to_broadcast([P, PE_TAPS, P]), tap, ALU.mult).then_inc(diag_ready, 1)

        def act_glu(act, base, i=None):
            t = T_PW1 + base
            round_tile(act, t + 1, i, NC)
            round_tile(act, t + 2, i, NC)
            for c in range(2):
                wait_chunk(act, t + 1, c, i, NC)
                act.wait_ge(in_free, at(in_before, t, i, NC) + (2 * c - 2 + IN_CREDIT))
                bias = (col("pw1_b", KC + base + c) if i is None
                        else cols[:, bass.ds(i * 2 + (PARAMS["pw1_b"] + KC + base + c), 1)])
                nc.scalar.activation(glu_s[:, c], ps[:, 2 + c], ACT.Sigmoid, bias=bias).then_inc(glu_act, 1)

        def act_glu_hi(act, i=None):
            act.wait_ge(in_free, in_before(T_PW2) + IN_CREDIT if i is None
                        else at(in_before, T_PW1 + NC, i, NC) + IN_CREDIT)
            act.wait_ge(taps_done, KC if i is None else i * 2 + 2)
            g = glu[:, KC - 2:KC] if i is None else glu[:, bass.ds(i * 2, 2)]
            nc.scalar.activation(glu_hi[:], g, ACT.Copy).then_inc(glu_hi_done, 1)

        def act_conv(act, m):
            nc.scalar.activation(taps_hi[:].rearrange("p j n -> p (j n)"), tap_rows, ACT.Copy).then_inc(glu_hi_done, 1)
            act_glu(act, 0)
            with act.Fori(0, KC // 2 - 1) as i:
                act_glu_hi(act, i)
                act_glu(act, NC, i)
            act_glu_hi(act)
            act_squares(act, m, lambda e, n: ln_dve.wait(e, f"c{n}"), dw_y)
            act_root(act, m, 3)

            def silu(n):
                ln_dve.wait(act, f"n{n}")
                ln_act.done(f"s{n}", nc.scalar.activation(dw_y[:, n], dw_y[:, n], ACT.Silu, bias=col("ln_b", n),
                                                          scale=col("ln_g", n)))

            def rounded(n):
                ln_act.wait(act, f"s{n}")
                buf = pairs_before(T_PW2 + n // 2) % 2
                nc.scalar.activation(a_hi[:, buf, n % 2], dw_y[:, n], ACT.Copy).then_inc(a_hi_ready, 1)

            for n in (0, 1):
                silu(n)
                rounded(n)
            round_tile(act, T_PW2 + 1)
            for n in (2, 3):
                silu(n)
                rounded(n)
            for n in range(4, KC):
                silu(n)
            for s in (2, 3):
                wait_chunk(act, T_PW2 + s - 2, 7)
                rounded(2 * s)
                rounded(2 * s + 1)
                round_tile(act, T_PW2 + s)
            round_tile(act, T_PW2 + 4)

        def dve_glu(dve, base, i=None):
            v, t = nc.vector, T_PW1 + base
            for c in range(2):
                n = base + c
                wait_chunk(dve, t, c, i, NC)
                dve.wait_ge(glu_act, n + 1 if i is None else i * 2 + (n + 1))
                g = glu[:, n:n + 1] if i is None else glu[:, bass.ds(i * 2 + n, 1)]
                bias = col("pw1_b", n) if i is None else cols[:, bass.ds(i * 2 + (PARAMS["pw1_b"] + n), 1)]
                src = ps[:, c:c + 1, :]
                v.scalar_tensor_tensor(g[:, :, DW_PAD:DW_PAD + T], src, bias, glu_s[:, c:c + 1], ALU.add,
                                       ALU.mult).then_inc(in_free, 2)

        def dve_taps(dve, i=None, t=None):
            v = nc.vector
            dve.wait_ge(glu_hi_done, KC // 2 + 1 if i is None else i + 2)
            g = glu[:, KC - 2:KC] if i is None else glu[:, bass.ds(i * 2, 2)]
            v.tensor_tensor(glu_lo[:], g, glu_hi[:].bitcast(F32), ALU.subtract).then_inc(glu_lo_done, 1)
            if t is not None:
                split_tile(dve, t, i, NC)

            def pc(r):
                return cols[:, r + KC - 2:r + KC - 1] if i is None else cols[:, bass.ds(i * 2 + r, 1)]

            before = KC // 2 - 1
            for j in range(PE_TAPS, DW):
                if t is not None and j == (PE_TAPS + DW) // 2:
                    split_tile(dve, t + 1, i, NC)
                for c in range(2):
                    n = KC - 2 + c
                    y = dw_y[:, n:n + 1] if i is None else dw_y[:, bass.ds(i * 2 + c, 1)]
                    src = (glu[:, n:n + 1] if i is None else glu[:, bass.ds(i * 2 + c, 1)])[:, :, j:j + T]
                    tap = pc(PARAMS["dw"] + j * KC + c)
                    if j == PE_TAPS:
                        ins = v.tensor_scalar(y, src, tap, pc(PARAMS["dw_b"] + c), ALU.mult, ALU.add)
                    else:
                        done = 2 * (j - PE_TAPS) + c - 1
                        dve.wait_ge(dw_step, before * DW_STEPS + done if i is None else i * DW_STEPS + done)
                        ins = v.scalar_tensor_tensor(y, src, tap, y, ALU.mult, ALU.add)
                    ins.then_inc(dw_step, 1)

        def dve_taps_add(dve, i=None):
            for c in range(2):
                y = dw_y[:, KC - 2 + c:KC - 1 + c] if i is None else dw_y[:, bass.ds(i * 2 + c, 1)]
                done = DW_STEPS - 1 + c
                before = KC // 2 - 1
                dve.wait_ge(dw_step, before * DW_STEPS + done if i is None else i * DW_STEPS + done)
                dve.wait_ge(taps_done, KC + c + 1 if i is None else i * 2 + (c + 3))
                nc.vector.tensor_tensor(y, y, ps[:, 4 + c:5 + c, :], ALU.add).then_inc(taps_added, 1)

        def dve_conv(dve, m):
            v = nc.vector
            dve.wait_ge(glu_hi_done, 1)
            v.tensor_tensor(taps_lo[:].rearrange("p j n -> p (j n)"), tap_rows, taps_hi[:].rearrange("p j n -> p (j n)").bitcast(F32),
                            ALU.subtract).then_inc(taps_split, 2)
            v.memset(glu[:, :, 0:DW_PAD], 0.0).then_inc(glu_pad, 1)
            v.memset(glu[:, :, DW_PAD + T:], 0.0).then_inc(glu_pad, 1)
            dve.wait_ge(glu_pad, 2)
            split_tile(dve, T_PW1 + 1)
            split_tile(dve, T_PW1 + 2)
            dve_glu(dve, 0)
            with dve.Fori(0, KC // 2 - 1) as i:
                dve_taps(dve, i, T_PW1 + NC + 1)
                dve_glu(dve, NC, i)
                dve_taps_add(dve, i)
            dve_taps(dve)
            dve_taps_add(dve)
            ln_pe.wait(dve, "sum")
            for n in range(KC):
                ln_dve.done(f"c{n}", v.scalar_tensor_tensor(dw_y[:, n], ps[:, 0], -1.0 / D, dw_y[:, n], ALU.mult, ALU.add))
            dve_rstd(dve, m, copied=True)
            def scaled(n):
                ln_dve.done(f"n{n}", v.tensor_tensor(dw_y[:, n], dw_y[:, n], n_rstd[:], ALU.mult))

            for n in range(4):
                scaled(n)
            dve_pair(dve, T_PW2, dw_y[:, 0:2])
            split_tile(dve, T_PW2 + 1)
            scaled(4)
            scaled(5)
            dve_pair(dve, T_PW2 + 1, dw_y[:, 2:4])
            scaled(6)
            scaled(7)
            bias = lambda s: "pw2_b" if s == 3 else None
            for s in range(4):
                add_chunks(dve, T_PW2 + s, range(0 if s == 0 else 2, 8), bias=bias(s), stat=8 if s == 3 else None)
                if s < 3:
                    add_chunks(dve, T_PW2 + s + 1, range(0, 2), bias=bias(s + 1))
                if s < 2:
                    dve_pair(dve, T_PW2 + s + 2, dw_y[:, 2 * s + 4:2 * s + 6])
                if s < 2:
                    split_tile(dve, T_PW2 + s + 2)

        def sp_setup(sp):
            for q in range(TC):
                sp.dma_start(x_tok[:, q], x[0, q * P:q * P + P, :]).then_inc(x_loaded, 16)
            sp.wait_ge(rows_clear, 1)
            load_rows(sp, 1)

        def over_partitions(v, n):
            return bass.AP(tensor=v.tensor, offset=v.offset, ap=[[0, P], [1, n]])

        def act_loads(act):
            ld = lambda dst, src: act.dma_start(dst, src).then_inc(small_loaded, 16)
            ld(wab_raw[:], a_w_in[0][:, A_AB0:A_AB0 + 16].rearrange("(k p) n -> p k n", p=P))
            ld(a_log[:], over_partitions(a_A_log, A_HEADS))
            ld(a_dt[:], over_partitions(a_dt_bias, A_HEADS))
            ld(sinks[:], over_partitions(b_sinks, B_HEADS))
            ld(rel_in, rel_bias)
            act.wait_ge(rows_clear, 1)
            load_rows(act, 0)

        def load_rows(eng, half):
            n = 0
            for name, v, rows in (
                    ("a_conv", a_conv[0].rearrange("k (c p) -> (k c) p", p=P), TAPS * 32),
                    ("a_norm", a_norm[0].rearrange("(c p) -> c p", p=P), KC),
                    ("kv_norm", kv_norm.rearrange("(c p) -> c p", p=P), KC),
                    ("b_norm", b_norm[0].rearrange("(c p) -> c p", p=P), KC),
                    ("norm_g", norm_g.rearrange("l n (c p) -> (l n c) p", p=P), 6 * KC),
                    ("pool_b", pool_b[0].rearrange("(c p) -> c p", p=P), KC),
                    ("pool_scale", pool_scale[0].rearrange("(c p) -> c p", p=P), KC),
                    ("pw1_b", pw1_b[0].rearrange("(c p) -> c p", p=P), 2 * KC),
                    ("dw_b", dw_b[0].rearrange("(c p) -> c p", p=P), KC),
                    ("ln_g", ln_g[0].rearrange("(c p) -> c p", p=P), KC),
                    ("ln_b", ln_b[0].rearrange("(c p) -> c p", p=P), KC),
                    ("pw2_b", pw2_b[0].rearrange("(c p) -> c p", p=P), KC),
                    ("final_g", final_g.rearrange("(c p) -> c p", p=P), KC),
                    ("o_gain", a_o_gain[0].rearrange("(c p) -> c p", p=P), 2)):
                r, b = PARAMS[name] % P, PARAMS[name] // P
                if n % 2 == half:
                    eng.dma_start(param_rows[r:r + rows, b], v).then_inc(rows_loaded, 16)
                n += 1
            assert n + 6 == ROW_LOADS
            if half == 0:
                return
            dw = dw_w[0].rearrange("k (c p) -> (k c) p", p=P)
            eng.dma_start(param_rows[:, 1], dw[0:P]).then_inc(rows_loaded, 16)
            eng.dma_start(param_rows[0:DW_ROWS - P, 2], dw[P:DW_ROWS]).then_inc(rows_loaded, 16)
            for name, v in (("k_gain", k_gain.rearrange("(o d) -> o d", o=1)), ("q_gain", b_q_gain)):
                r = PARAMS[name] % P
                for u in range(2):
                    eng.dma_start(param_rows[r:r + 1, 4, u * B_HD:(u + 1) * B_HD], v).then_inc(rows_loaded, 16)
        ROW_LOADS = 20
        setup_const = sem("setup_const")

        def gp_setup(pool):
            n = 0

            def step(ins):
                nonlocal n
                n += 1
                ins.then_inc(setup_const, 1)
                pool.wait_ge(setup_const, n)

            pool.memset(param_rows[:], 0.0).then_inc(rows_clear, 1)
            step(pool.memset(ident[:], 0.0))
            step(pool.affine_select(out=ident[:], in_=ident[:], compare_op=ALU.not_equal, fill=1.0, base=0,
                                    pattern=[[-1, P]], channel_multiplier=1))
            step(pool.memset(ones[:], 1.0))
            step(pool.memset(half_ones[:], 0.0))
            step(pool.memset(half_ones[0:B_HD, 0:1], 1.0))
            step(pool.memset(half_ones[B_HD:P, 1:2], 1.0))
            for k, e in enumerate((EPS, A_DK * EPS, B_HD * EPS, LN_EPS)):
                step(pool.memset(eps[:, k:k + 1], e))
            assert n == FIRST_CONSTS
            step(pool.affine_select(out=tri[:], in_=ones[:], compare_op=ALU.is_ge, fill=0.0, base=0,
                                    pattern=[[1, P]], channel_multiplier=-1))
            step(pool.memset(flip[:], 0.0))
            step(pool.affine_select(out=flip[:], in_=flip[:], compare_op=ALU.not_equal, fill=1.0, base=-(P - 1),
                                    pattern=[[1, P]], channel_multiplier=1))
            step(pool.memset(causal[:], 0.0))
            step(pool.affine_select(out=causal[:], in_=causal[:], compare_op=ALU.is_ge, fill=MASKED, base=0,
                                    pattern=[[1, P]], channel_multiplier=-1))
            step(pool.memset(level_mask[:], 0.0))
            m = level_mask[:, 0].rearrange("p (n u) -> p n u", u=2)[:, :, 1:2]
            step(pool.affine_select(out=m, in_=m, compare_op=ALU.not_equal, fill=1.0, base=0,
                                    pattern=[[-2, P // 2], [0, 1]], channel_multiplier=1))
            for l in range(1, LEVELS):
                b = 1 << l
                m = level_mask[:, l].rearrange("p (n r) -> p n r", r=2 * b)[:, :, 0:b]
                step(pool.memset(m, 1.0))
                step(pool.affine_select(out=m, in_=m, compare_op=ALU.is_ge, fill=0.0, base=-b,
                                        pattern=[[-2 * b, P // (2 * b)], [0, b]], channel_multiplier=1))
                step(pool.affine_select(out=m, in_=m, compare_op=ALU.is_ge, fill=0.0, base=2 * b - 1,
                                        pattern=[[2 * b, P // (2 * b)], [0, b]], channel_multiplier=-1))
            return n

        FIRST_CONSTS = 3 + 3 + 4
        SETUP_CONSTS = 11 + 4 + 2 + 3 * (LEVELS - 1)

        def gp_relative(pool):
            pool.wait_ge(rel_ready, 1)
            pool.dma_start(rel_scratch, rel_line).then_inc(rel_stored, 16)
            pool.wait_ge(rel_stored, 16)

        def pe_setup(pe):
            pe.sem_inc(chunk_done, CHUNK_CREDIT)
            pe.wait_ge(setup_const, FIRST_CONSTS)
            pe.wait_ge(x_loaded, 16 * TC)
            for k in range(KC):
                if k >= 6:
                    pe.wait_ge(x_ready, k - 5)
                for q in range(TC):
                    ins = nc.tensor.transpose(ps[:, 2 + k % 6, q * P:q * P + P], x_tok[:, q, k * P:k * P + P], ident[:])
                ins.then_inc(setup_pe, 1)
            pe.wait_ge(rows_loaded, 16 * ROW_LOADS)
            for r in range(5):
                ins = nc.tensor.transpose(ps[:, r // 4, (r % 4) * P:(r % 4) * P + P], param_rows[:, r], ident[:])
            ins.then_inc(setup_pe, 1)

        def act_setup(act):
            act.sem_inc(in_free, IN_CREDIT)

        wab_round, wab_ready = sem("wab_round"), sem("wab_ready")

        def dve_setup(dve):
            v = nc.vector
            dve.sem_inc(lo_done, SPLIT_CREDIT)
            dve.sem_inc(out_free, OUT_CREDIT)
            for k in range(KC):
                dve.wait_ge(setup_pe, k + 1)
                v.tensor_copy(xT[:, k], ps[:, 2 + k % 6]).then_inc(x_ready, 1)
                if k >= 2:
                    dve_sum(dve, 0, k - 1)
            dve.wait_ge(setup_pe, KC + 1)
            v.tensor_copy(cols[:], ps[:, 0:2].rearrange("p k t -> p (k t)")[:, 0:5 * P]).then_inc(cols_ready, 1)

        def dve_first_tile(dve):
            dve.wait_ge(wab_round, 1)
            nc.vector.tensor_tensor(wab_lo[:], wab_raw[:], wab_hi[:].bitcast(F32), ALU.subtract).then_inc(wab_ready, 1)
            split_tile(dve, 0)

        def dve_relative(dve):
            v = nc.vector
            dve.wait_ge(small_loaded, SMALL)
            v.transpose(rel_T, rel_in).then_inc(rel_chain, 1)
            v.memset(rel_line, MASKED).then_inc(rel_chain, 1)
            dve.wait_ge(rel_chain, 2)
            for bucket, first, n in bucket_runs():
                o = P - 1 + first
                ins = v.tensor_copy(rel_line[:, o:o + n], rel_T[:, bucket:bucket + 1].to_broadcast([B_HEADS, n]))
                ins.then_inc(rel_chain, 1)
            dve.wait_ge(rel_chain, 2 + len(bucket_runs()))
            dve.sem_inc(rel_ready, 1)

        out_dve = sem("out_dve")

        def dve_output(dve, m):
            v = nc.vector
            for n in range(KC):
                v.scalar_tensor_tensor(dw_y[:, n], xT[:, n], col("final_g", n), n_rstd[:], ALU.mult,
                                       ALU.mult).then_inc(out_dve, 1)
            for q in range(1, TC, 2):
                dve.wait_ge(y_pe, q + 1)
                v.tensor_copy(y_tok[:, q], ps[:, 2 * q:2 * q + 2].rearrange("p k t -> p (k t)")).then_inc(y_ready, 1)

        y_act = sem("y_act")

        def act_output(act):
            for q in range(0, TC, 2):
                act.wait_ge(y_pe, q + 1)
                nc.scalar.activation(y_tok[:, q], ps[:, 2 * q:2 * q + 2].rearrange("p k t -> p (k t)"),
                                     ACT.Copy).then_inc(y_act, 1)

        def pe_output(pe):
            pe.wait_ge(out_dve, KC)
            for q in range(TC):
                for n in range(KC):
                    ins = nc.tensor.transpose(ps[:, 2 * q + n // 4, (n % 4) * P:(n % 4) * P + P],
                                              dw_y[:, n, q * P:q * P + P], ident[:])
                ins.then_inc(y_pe, 1)

        def sp_output(sp):
            for q in range(TC):
                sp.wait_ge((y_act, y_ready)[q % 2], q // 2 + 1)
                sp.dma_start(out[0, q * P:q * P + P, :], y_tok[:, q]).then_inc(out_stored, 16)
            sp.wait_ge(out_stored, 16 * TC)

        FF_W = [(0, 0), (0, 1), (1, 0), (1, 1)]
        T_A_END, T_B_END = T_KV, T_FF[0]

        def added(t):
            return lambda e, n: out_added(e, t, n)

        def end_of(f):
            return T_FF[f] + 2 + 3 * (FF_STEPS - 1)

        def gain_of(name, first=0):
            return lambda n: (name, first + n)

        block = ctx.enter_context(nc.Block())

        @block.sync
        def _(sp):
            sp_setup(sp)
            wi = a_w_in[0]
            for k, c in enumerate((0, A_QK_W, 2 * A_QK_W, 2 * A_QK_W + 256)):
                load(sp, k, cols256(wi, slice(c, c + 256)))

            def a_loads(i):
                for k in range(2):
                    load(sp, 4 + k, cols256(wi, bass.ds(i * 512 + (A_Z0 + 256 * k), 256)), i, NA)
                if not last_pair(i):
                    for k, c in enumerate((256, A_QK_W + 256)):
                        load(sp, 6 + k, cols256(wi, bass.ds(i * 256 + c, 256)), i, NA)
                    for k in range(2):
                        load(sp, 8 + k, cols256(wi, bass.ds(i * 512 + (2 * A_QK_W + 512 + 256 * k), 256)), i, NA)
                for k in range(2):
                    t, r, period = a_tile_at(6 + k, i)
                    load(sp, t, rows256(a_w_out[0], bass.ds(i * 512 + 256 * k, 256)), r, period)

            with sp.Fori(0, A_PAIRS - 1) as i:
                a_loads(i)
            a_loads(A_PAIRS - 1)
            for k in range(2):
                load(sp, T_KV + k, cols256(w_kv, slice(256 * k, 256 * k + 256)))
            for k, c in enumerate((0, B_W)):
                load(sp, T_B + k, cols256(b_w_in[0], slice(c, c + 256)))

            def b_step(j, pp):
                t = T_B + 2 + 3 * pp
                for k, c in enumerate((0, B_W)):
                    load(sp, t + k, cols256(b_w_in[0], bass.ds(j * 512 + (256 * (pp + 1) + c), 256)), j, NB)
                load(sp, t + 2, rows256(b_w_out[0], bass.ds(j * 512 + 256 * pp, 256)), j, NB)

            with sp.Fori(0, B_KV - 1) as j:
                for pp in range(2):
                    b_step(j, pp)
            b_step(B_KV - 1, 0)
            load(sp, T_FF[0] - 1, rows256(b_w_out[0], slice(B_W - 256, B_W)))

            def ff(f):
                t, (l, k) = T_FF[f], FF_W[f]
                w_in, w_out = ffn_w_in[l, k], ffn_w_out[l, k]
                load(sp, t, cols256(w_in, slice(0, 256)))
                load(sp, t + 1, cols256(w_in, slice(FF, FF + 256)))
                with sp.Fori(0, FF_STEPS // 2) as i:
                    for r in range(2):
                        u = t + 2 + 3 * r
                        load(sp, u, cols256(w_in, bass.ds(i * 512 + 256 * (r + 1), 256)), i, 6)
                        load(sp, u + 1, cols256(w_in, bass.ds(i * 512 + (FF + 256 * (r + 1)), 256)), i, 6)
                        load(sp, u + 2, rows256(w_out, bass.ds(i * 512 + 256 * r, 256)), i, 6)
                load(sp, end_of(f), rows256(w_out, slice(FF - 256, FF)))

            ff(0)
            load(sp, T_POOL, pool_w[0].rearrange("g (k p) n -> p (g k) n", p=P))
            ff(1)
            ff(2)
            for c in range(2):
                load(sp, T_PW1 + c, cols256(pw1_w[0], slice(D * c, D * c + 256)))
            with sp.Fori(0, KC // 2 - 1) as i:
                for c in range(2):
                    load(sp, T_PW1 + NC + c, cols256(pw1_w[0], bass.ds(i * 256 + (256 + D * c), 256)), i, NC)
            for s in range(4):
                load(sp, T_PW2 + s, rows256(pw2_w[0], slice(256 * s, 256 * s + 256)))
            ff(3)
            sp_output(sp)

        @block.gpsimd
        def _(pool):
            assert gp_setup(pool) == SETUP_CONSTS
            gp_relative(pool)
            with pool.Fori(0, B_KV) as j:
                for pp in range(2):
                    b_dve.before(pool, f"add3{pp}", j)
                    pool.dma_start(bias_cur[:, pp], rel_band[bass.ds(j * 8 + 4 * pp, 4)].rearrange("h q s -> q h s")
                                   ).then_inc(bias_loaded[pp], 16)
            assert gp_pool_consts(pool) == POOL_CONSTS
            gp_taps(pool)

        @block.scalar
        def _(act):
            act_loads(act)
            act_setup(act)
            act_squares(act, 0, lambda e, n: e.wait_ge(x_ready, n + 1))
            act.wait_ge(small_loaded, SMALL)
            nc.scalar.activation(wab_hi[:], wab_raw[:], ACT.Copy).then_inc(wab_round, 1)
            round_tile(act, 0)
            act_root(act, 0)
            act_h(act, 0)
            gates_act.begin(act)
            a_act.begin(act)
            act_a_first(act)
            act.wait_ge(rel_stored, 16)
            with act.Fori(0, A_PAIRS - 1) as i:
                act_a(act, i)
            act_a(act, A_PAIRS - 1)
            act_squares(act, 1, added(T_A_END - 1))
            act_root(act, 1)
            act_h(act, 1)
            kv_act.begin(act)
            act_kv(act)
            with act.Fori(0, B_KV - 1) as j:
                for pp in range(2):
                    act_b(act, j, pp)
            for pp in range(2):
                act_b(act, B_KV - 1, pp)

            def norm(m, q, t):
                act_squares(act, m, added(t))
                act_root(act, m)
                if q is not None:
                    act_h(act, q)

            norm(2, 3, T_B_END - 1)
            act_ff(act, 0)
            norm(3, None, end_of(0))
            act_pool(act, 4)
            round_tile(act, T_POOL + 1)
            norm(4, 5, T_POOL)
            act_ff(act, 1)
            norm(5, 6, end_of(1))
            act_ff(act, 2)
            norm(6, 7, end_of(2))
            ln_act.begin(act)
            act_conv(act, 7)
            norm(8, 8, T_PW2 + 3)
            act_ff(act, 3)
            norm(9, None, end_of(3))
            act_output(act)

        @block.vector
        def _(dve):
            dve_setup(dve)
            dve_rstd(dve, 0, meanwhile=dve_first_tile)
            dve.wait_ge(cols_ready, 1)
            dve_h(dve, 0, 0, gain_of("a_norm"))
            dve.wait_ge(setup_const, SETUP_CONSTS)
            gates_dve.begin(dve)
            a_dve.begin(dve)
            dve.wait_ge(h_ready, KC)
            nc.vector.memset(conv_in[:, :, 0:TAPS - 1], 0.0).then_inc(conv_pad, 1)
            dve_a_first(dve)
            gates_dve.wait(dve, "be")
            gates_act.wait(dve, "last")
            with dve.Fori(0, A_PAIRS - 1) as i:
                dve_a(dve, i)
            dve_a(dve, A_PAIRS - 1)
            dve_rstd(dve, 1, copied=True)
            dve_h(dve, 1, 1, gain_of("kv_norm"))
            kv_dve.begin(dve)
            dve_kv(dve)
            with dve.Fori(0, B_KV - 1) as j:
                for pp in range(2):
                    dve_b(dve, j, pp)
            for pp in range(2):
                dve_b(dve, B_KV - 1, pp)
            dve_rstd(dve, 2)
            dve_h(dve, 2, 3, gain_of("norm_g", 0))
            dve_ff(dve, 0)
            dve_rstd(dve, 3, copied=True)
            dve_h(dve, 3, 4, gain_of("norm_g", KC))
            dve_pool(dve)
            dve_rstd(dve, 4)
            dve_h(dve, 4, 5, gain_of("norm_g", 2 * KC))
            dve_ff(dve, 1)
            dve_rstd(dve, 5)
            dve_h(dve, 5, 6, gain_of("norm_g", 3 * KC))
            dve_ff(dve, 2)
            dve_rstd(dve, 6)
            dve_h(dve, 6, 7, gain_of("norm_g", 4 * KC))
            ln_dve.begin(dve)
            dve.sem_inc(taps_added, 2)
            dve_conv(dve, 7)
            dve_rstd(dve, 8)
            dve_h(dve, 8, 8, gain_of("norm_g", 5 * KC))
            dve_ff(dve, 3)
            dve_rstd(dve, 9, copied=True)
            dve_output(dve, 9)

        @block.tensor
        def _(pe):
            pe_setup(pe)
            pe.wait_ge(cols_ready, 1)
            pe_stat(pe, 0, 0)
            pe.wait_ge(wab_ready, 1)
            gates_pe.begin(pe)
            a_pe.begin(pe)
            pe.wait_ge(setup_const, SETUP_CONSTS)
            pe_a_first(pe)
            with pe.Fori(0, A_PAIRS - 1) as i:
                pe_a(pe, i)
            pe_a(pe, A_PAIRS - 1)
            pe_stat(pe, 1, T_KV)
            kv_pe.begin(pe)
            pe_kv(pe)
            with pe.Fori(0, B_KV - 1) as j:
                for pp in range(2):
                    pe_b(pe, j, pp)
            for pp in range(2):
                pe_b(pe, B_KV - 1, pp)
            pe_stat(pe, 2, T_FF[0])
            pe_ff(pe, 0, 3)
            pe_stat(pe, 3, T_POOL)
            pe_pool(pe, 4)
            pe_stat(pe, 4, T_POOL + 1)
            pe_ff(pe, 1, 5)
            pe_stat(pe, 5, T_FF[2])
            pe_ff(pe, 2, 6)
            pe_stat(pe, 6, T_PW1)
            ln_pe.begin(pe)
            pe.sem_inc(taps_done, 2)
            pe_conv(pe, 7, 7)
            pe_stat(pe, 8, T_FF[3])
            pe_ff(pe, 3, 8)
            pe_stat(pe, 9, len(TILES))
            pe_output(pe)


_INS = ["x", "a_norm", "a_w_in", "a_conv", "a_A_log", "a_dt_bias", "a_o_gain", "a_w_out", "kv_norm", "w_kv",
        "k_gain", "rel_bias", "b_norm", "b_w_in", "b_q_gain", "b_sinks", "b_w_out", "norm_g_2", "ffn_w_in_2",
        "ffn_w_out_2", "pool_w_2", "pool_b_2", "pool_scale_2", "conv_w_pw1_2", "conv_b_pw1_2", "conv_w_dw_2",
        "conv_b_dw_2", "conv_ln_g_2", "conv_ln_b_2", "conv_w_pw2_2", "conv_b_pw2_2", "final_g_2"]


def kernel(**inputs):
    import numpy as _np
    import concourse.bacc as _bacc
    from concourse import mybir as _mybir
    from concourse.bass_utils import run_bass_kernel_spmd as _run

    nc = _bacc.Bacc("TRN2", target_bir_lowering=False, num_devices=1)
    arrays, args = {}, []
    for name in _INS:
        a = _np.ascontiguousarray(inputs[name])
        arrays[f"in_{name}_dram"] = a
        args.append(nc.dram_tensor(f"in_{name}_dram", a.shape, _mybir.dt.from_np(a.dtype), kind="ExternalInput").ap())
    out = nc.dram_tensor("out_dram", (1, T, D), F32, kind="ExternalOutput").ap()
    build(nc, *args, out)
    r = _run(nc, [arrays], core_ids=[0])
    return r.results[0]["out_dram"]
```
